# Optimizing a Trainium2 kernel written in Bass

```python
import math
import jax, jax.numpy as jnp
from jax import lax
import numpy as np

D_MODEL = 2048
BATCH = 1
SEQ = 256
DEPTH = 1

GRID_W = 64
CTX_LEN = 256
D_FF = 5632
N_MOD = 9
EPS = 1e-6
HG_WIDTH = D_MODEL // 2
HG_HEADS = 8
HG_DK = HG_WIDTH // HG_HEADS
HG_DV = HG_WIDTH // HG_HEADS
CHUNK = 64
HY_WIDTH = D_MODEL - HG_WIDTH
FILT_EMB = 33
FILT_ORDER = 64
DECAY_TARGET = 1e-2
DECAY_FAST_PCT = 0.3
DECAY_SLOW_PCT = 1.5
COL_Q = 3 * HG_WIDTH
COL_G = 4 * HG_WIDTH
COL_HY = 5 * HG_WIDTH
IN_COLS = 5 * HG_WIDTH + 3 * HY_WIDTH

kernel_name = 'hybrid_hgrn2_hyena_macaron_dit'

F32 = jnp.float32

def _rmsnorm(x, g):
    xf = x.astype(F32)
    y = xf * lax.rsqrt(jnp.mean(xf * xf, axis=-1, keepdims=True) + EPS)
    return (y * g.astype(F32)).astype(x.dtype)

def _modulate(h, shift, scale):
    return h * (1 + scale) + shift

def _swiglu(h, w1, w3, w2):
    return (jax.nn.silu(h @ w1) * (h @ w3)) @ w2

def _flip(a):
    return jnp.flip(a, axis=1)

def _heads(a):
    return a.reshape(a.shape[:-1] + (HG_HEADS, a.shape[-1] // HG_HEADS))

def _hgrn_gates(a, lb):
    a = a.astype(F32)
    logf = jnp.log(lb + (1 - lb) * jax.nn.sigmoid(a))
    k = (1 - lb) * jax.nn.sigmoid(-a)
    return _heads(k), _heads(logf)

def _hgrn_inputs(p, lb):
    k_f, g_f = _hgrn_gates(p[..., :HG_WIDTH], lb[0])
    k_b, g_b = _hgrn_gates(p[..., HG_WIDTH:2 * HG_WIDTH], lb[1])
    v = _heads(p[..., 2 * HG_WIDTH:COL_Q].astype(F32))
    return k_f, g_f, k_b, g_b, v

def _query(p):
    return _heads(p[..., COL_Q:COL_G].astype(F32)) * (HG_DK ** -0.5)

def _hgrn_scan(q, k, v, logf, s0):
    bsz, n, h, _ = q.shape
    dv = v.shape[-1]
    nc = n // CHUNK

    def to_chunks(a):
        return a.reshape(bsz, nc, CHUNK, h, a.shape[-1]).transpose(1, 0, 3, 2, 4)

    lower_tri = jnp.tril(jnp.ones((CHUNK, CHUNK), dtype=bool))[:, :, None]

    def step(s, inp):
        qc, kc, vc, gc = inp
        b = jnp.cumsum(gc, axis=2)
        o = jnp.einsum('bhtk,bhkv->bhtv', qc * jnp.exp(b), s)
        rel = jnp.exp(jnp.where(lower_tri, b[:, :, :, None, :] - b[:, :, None, :, :], -jnp.inf))
        scores = jnp.einsum('bhtk,bhtsk,bhsk->bhts', qc, rel, kc)
        o = o + jnp.einsum('bhts,bhsv->bhtv', scores, vc)
        b_end = b[:, :, -1:, :]
        s = jnp.exp(b_end[:, :, 0, :, None]) * s + jnp.einsum('bhsk,bhsv->bhkv', kc * jnp.exp(b_end - b), vc)
        return s, o

    s_fin, o = lax.scan(step, s0, (to_chunks(q), to_chunks(k), to_chunks(v), to_chunks(logf)))
    o = o.transpose(1, 0, 3, 2, 4).reshape(bsz, n, h, dv)
    return o, s_fin

def _final_state(k, v, logf):
    cum = jnp.cumsum(logf, axis=1)
    return jnp.einsum('blhk,blhv->bhkv', k * jnp.exp(cum[:, -1:] - cum), v)

def _bidir_hgrn(q, k_f, g_f, k_b, g_b, v, s_f, s_b):
    o_f, s_f = _hgrn_scan(q, k_f, v, g_f, s_f)
    o_b, s_b = _hgrn_scan(_flip(q), _flip(k_b), _flip(v), _flip(g_b), s_b)
    return o_f + _flip(o_b), s_f, s_b

def _hgrn_readout(o, g, gain):
    o = o * lax.rsqrt(jnp.mean(o * o, axis=-1, keepdims=True) + EPS) * gain.astype(F32).reshape(HG_HEADS, HG_DV)
    o = o.reshape(o.shape[:2] + (HG_WIDTH,))
    return (o * jax.nn.silu(g.astype(F32))).astype(g.dtype)

def _short_conv(u, w, b, on_grid):
    shape = u.shape
    if on_grid:
        rows = shape[1] // GRID_W
        u = u.reshape(shape[0], rows, GRID_W, shape[2])
    pad = [(0, 0)] * (u.ndim - 2) + [(1, 1), (0, 0)]
    up = jnp.pad(u, pad)
    y = up[..., :-2, :] * w[0] + up[..., 1:-1, :] * w[1] + up[..., 2:, :] * w[2] + b
    return y.reshape(shape)

def _hyena_spectrum(n, w1, b1, w2, b2, w3, b3, freq, w_out):
    w1, b1, w2, b2, w3, b3, freq, w_out = [a.astype(F32) for a in (w1, b1, w2, b2, w3, b3, freq, w_out)]
    pos = jnp.arange(n, dtype=F32)
    t = pos / max(n - 1, 1)
    bands = (FILT_EMB - 1) // 2
    fb = jnp.linspace(1e-4, bands - 1, bands, dtype=F32)
    ang = (2 * math.pi / n) * pos[:, None] * fb[None, :]
    z = jnp.concatenate([t[:, None], jnp.cos(ang), -jnp.sin(ang)], axis=-1)
    hid = jnp.sin(freq * (z @ w1 + b1))
    hid = jnp.sin(freq * (hid @ w2 + b2))
    hid = jnp.sin(freq * (hid @ w3 + b3))
    h = (hid @ w_out).reshape(n, 2, 2, HY_WIDTH)
    deltas = jnp.abs(jnp.linspace(math.log(DECAY_TARGET) / DECAY_SLOW_PCT,
                                  math.log(DECAY_TARGET) / DECAY_FAST_PCT, HY_WIDTH, dtype=F32))
    h = h * jnp.exp(-t[:, None] * deltas)[:, None, None, :]
    h_fwd = h[:, :, 0]
    h_bwd = h[1:, :, 1]
    l1 = jnp.sum(jnp.abs(h_fwd), axis=0) + jnp.sum(jnp.abs(h_bwd), axis=0)
    filt = jnp.concatenate([h_fwd, jnp.zeros((1, 2, HY_WIDTH), F32), h_bwd[::-1]], axis=0) / l1
    return jnp.fft.rfft(filt, axis=0)

def _long_conv(u, spec, d):
    n = u.shape[1]
    uf = u.astype(F32)
    y = jnp.fft.irfft(jnp.fft.rfft(uf, n=2 * n, axis=1) * spec, n=2 * n, axis=1)[:, :n]
    return (y + d.astype(F32) * uf).astype(u.dtype)

def _hyena(p, spec, d, conv_w, conv_b, on_grid):
    u = _short_conv(p, conv_w, conv_b, on_grid)
    v, x1, x2 = jnp.split(u, 3, axis=-1)
    z = x1 * _long_conv(v, spec[:, 0], d[0])
    return x2 * _long_conv(z, spec[:, 1], d[1])

def setup_inputs(seed: int = 0) -> dict:
    key = jax.random.key(seed)
    ks = iter(jax.random.split(key, 40))

    def nrm(shape, scale):
        return jax.random.normal(next(ks), shape, F32) * scale

    def gain(shape):
        return 1.0 + nrm(shape, 0.02)

    return {
        'x': nrm((BATCH, SEQ, D_MODEL), 1.0),
        'c': nrm((BATCH, D_MODEL), 1.0),
        'ctx': nrm((BATCH, CTX_LEN, D_MODEL), 1.0),
        'c_ctx': nrm((D_MODEL,), 1.0),
        'ada_w': nrm((DEPTH, D_MODEL, N_MOD * D_MODEL), D_MODEL ** -0.5),
        'ada_b': nrm((DEPTH, N_MOD * D_MODEL), 0.02),
        'norm_ffn1': gain((DEPTH, D_MODEL)),
        'ffn1_w1': nrm((DEPTH, D_MODEL, D_FF), D_MODEL ** -0.5),
        'ffn1_w3': nrm((DEPTH, D_MODEL, D_FF), D_MODEL ** -0.5),
        'ffn1_w2': nrm((DEPTH, D_FF, D_MODEL), D_FF ** -0.5),
        'norm_mix': gain((DEPTH, D_MODEL)),
        'w_in': nrm((DEPTH, D_MODEL, IN_COLS), D_MODEL ** -0.5),
        'hg_lb_logits': nrm((2, DEPTH + 1, HG_WIDTH), 0.5),
        'hg_norm': gain((DEPTH, HG_WIDTH)),
        'hy_conv_w': nrm((DEPTH, 3, 3 * HY_WIDTH), 3 ** -0.5),
        'hy_conv_b': nrm((DEPTH, 3 * HY_WIDTH), 0.02),
        'filt_w1': nrm((DEPTH, FILT_EMB, FILT_ORDER), FILT_EMB ** -0.5),
        'filt_b1': nrm((DEPTH, FILT_ORDER), 0.1),
        'filt_w2': nrm((DEPTH, FILT_ORDER, FILT_ORDER), FILT_ORDER ** -0.5),
        'filt_b2': nrm((DEPTH, FILT_ORDER), 0.1),
        'filt_w3': nrm((DEPTH, FILT_ORDER, FILT_ORDER), FILT_ORDER ** -0.5),
        'filt_b3': nrm((DEPTH, FILT_ORDER), 0.1),
        'filt_freq': 1.0 + nrm((DEPTH, FILT_ORDER), 0.1),
        'filt_w_out': nrm((DEPTH, FILT_ORDER, 4 * HY_WIDTH), FILT_ORDER ** -0.5),
        'hy_d': nrm((DEPTH, 2, HY_WIDTH), 0.1),
        'w_out': nrm((DEPTH, D_MODEL, D_MODEL), D_MODEL ** -0.5),
        'norm_ffn2': gain((DEPTH, D_MODEL)),
        'ffn2_w1': nrm((DEPTH, D_MODEL, D_FF), D_MODEL ** -0.5),
        'ffn2_w3': nrm((DEPTH, D_MODEL, D_FF), D_MODEL ** -0.5),
        'ffn2_w2': nrm((DEPTH, D_FF, D_MODEL), D_FF ** -0.5),
        'final_norm': gain((D_MODEL,)),
    }

def reference(x, c, ctx, c_ctx, ada_w, ada_b, norm_ffn1, ffn1_w1, ffn1_w3, ffn1_w2, norm_mix, w_in,
              hg_lb_logits, hg_norm, hy_conv_w, hy_conv_b, filt_w1, filt_b1, filt_w2, filt_b2, filt_w3,
              filt_b3, filt_freq, filt_w_out, hy_d, w_out, norm_ffn2, ffn2_w1, ffn2_w3, ffn2_w2, final_norm):
    bsz, lat_len, _ = x.shape
    ctx_len = ctx.shape[1]
    lower = jnp.cumsum(jax.nn.softmax(hg_lb_logits.astype(F32), axis=1), axis=1)
    zero_state = jnp.zeros((bsz, HG_HEADS, HG_DK, HG_DV), F32)
    y = ctx
    for l in range(DEPTH):
        last = l == DEPTH - 1
        mx = [m[:, None, :] for m in jnp.split(jax.nn.silu(c) @ ada_w[l] + ada_b[l], N_MOD, axis=-1)]
        mc = jnp.split(jax.nn.silu(c_ctx) @ ada_w[l] + ada_b[l], N_MOD, axis=-1)
        filt = (filt_w1[l], filt_b1[l], filt_w2[l], filt_b2[l], filt_w3[l], filt_b3[l], filt_freq[l], filt_w_out[l])
        lb = lower[:, l]

        x = x + 0.5 * mx[2] * _swiglu(_modulate(_rmsnorm(x, norm_ffn1[l]), mx[0], mx[1]),
                                      ffn1_w1[l], ffn1_w3[l], ffn1_w2[l])
        y = y + 0.5 * mc[2] * _swiglu(_modulate(_rmsnorm(y, norm_ffn1[l]), mc[0], mc[1]),
                                      ffn1_w1[l], ffn1_w3[l], ffn1_w2[l])

        hc = _modulate(_rmsnorm(y, norm_mix[l]), mc[3], mc[4])
        if last:
            pc = hc @ w_in[l][:, :COL_Q]
            kcf, gcf, kcb, gcb, vc = _hgrn_inputs(pc, lb)
            s_f = _final_state(kcf, vc, gcf)
            s_b = _final_state(_flip(kcb), _flip(vc), _flip(gcb))
        else:
            pc = hc @ w_in[l]
            kcf, gcf, kcb, gcb, vc = _hgrn_inputs(pc, lb)
            o_c, s_f, s_b = _bidir_hgrn(_query(pc), kcf, gcf, kcb, gcb, vc, zero_state, zero_state)
            mix_c = jnp.concatenate([
                _hgrn_readout(o_c, pc[..., COL_G:COL_HY], hg_norm[l]),
                _hyena(pc[..., COL_HY:], _hyena_spectrum(ctx_len, *filt), hy_d[l], hy_conv_w[l], hy_conv_b[l], False),
            ], axis=-1)
            y = y + mc[5] * (mix_c @ w_out[l])
            y = y + 0.5 * mc[8] * _swiglu(_modulate(_rmsnorm(y, norm_ffn2[l]), mc[6], mc[7]),
                                          ffn2_w1[l], ffn2_w3[l], ffn2_w2[l])

        hx = _modulate(_rmsnorm(x, norm_mix[l]), mx[3], mx[4])
        px = hx @ w_in[l]
        kxf, gxf, kxb, gxb, vx = _hgrn_inputs(px, lb)
        o_x, _, _ = _bidir_hgrn(_query(px), kxf, gxf, kxb, gxb, vx, s_f, s_b)
        mix_x = jnp.concatenate([
            _hgrn_readout(o_x, px[..., COL_G:COL_HY], hg_norm[l]),
            _hyena(px[..., COL_HY:], _hyena_spectrum(lat_len, *filt), hy_d[l], hy_conv_w[l], hy_conv_b[l], True),
        ], axis=-1)
        x = x + mx[5] * (mix_x @ w_out[l])

        x = x + 0.5 * mx[8] * _swiglu(_modulate(_rmsnorm(x, norm_ffn2[l]), mx[6], mx[7]),
                                      ffn2_w1[l], ffn2_w3[l], ffn2_w2[l])
    return _rmsnorm(x, final_norm)


_drawn_inputs = setup_inputs


def setup_inputs(seed=0):
    import zlib

    import numpy as np

    out = dict(_drawn_inputs(seed))
    spreads = {}
    factors = {'ctx': 3.244,
     'norm_ffn1': 5.679,
     'norm_mix': 4.281,
     'hg_norm': 22.471,
     'hy_conv_b': 64.0,
     'filt_b1': 4.866,
     'filt_b2': 3.637,
     'filt_b3': 4.102,
     'filt_freq': 8.0,
     'norm_ffn2': 22.208,
     'final_norm': 7.88}
    for name, (base, spread) in spreads.items():
        noise = np.random.default_rng([zlib.crc32(name.encode()), seed]).standard_normal(out[name].shape)
        drawn = base * np.exp(spread * noise) if base else spread * noise
        out[name] = __import__('jax').numpy.asarray(drawn.astype(out[name].dtype))
    for name, factor in factors.items():
        out[name] = (out[name] * factor).astype(out[name].dtype)
    return out
```

```python
from contextlib import ExitStack

import numpy as np

import concourse.bass as bass
from concourse import mybir

F32 = mybir.dt.float32
F32R = mybir.dt.float32r
I32 = mybir.dt.int32
ACT = mybir.ActivationFunctionType
ALU = mybir.AluOpType

P = 128
D = 2048
KB = D // P
SEQ = 256
CTX = 256
TB = SEQ // P
FF = 5632
CHUNK = 256
N_CHUNK = FF // CHUNK
N_MOD = 9
EPS = 1e-6
HEADS = 8
PAIRS = HEADS // 2
DK = 128
HG = HEADS * DK
HY = D - HG
GRID_W = 64
FILT_EMB = 33
FILT_ORDER = 64
LEVELS = 8
UNIT = 1024
RING = 4
KG = KB // 4
TWO_PI = 2.0 * np.pi

U_FFN1 = 0
U_CTX = U_FFN1 + 12 * N_CHUNK
U_HG = U_CTX + 12 * PAIRS
U_HY = U_HG + 20 * PAIRS
U_OUT = U_HY + 12 * PAIRS
U_FFN2 = U_OUT + 4 * (KB // 2)
U_END = U_FFN2 + 12 * N_CHUNK

ADA_FIRST = 3
ADA_LOOPS = 16
ADA_PER = (N_MOD - ADA_FIRST) * (KB // 2) // ADA_LOOPS
FILT_STEPS = 4
ADA_STEP = ADA_FIRST * (KB // 2) // FILT_STEPS

T_COS, T_SIN, T_COSN, T_SINN, T_ITR, T_ITI = 0, 512, 1024, 1280, 1792, 2304
T_COLS = 2816


def shape_tables():
    n2 = 2 * SEQ
    t = np.arange(SEQ, dtype=np.float64)
    ang = 2 * np.pi * ((t[:, None] * t[None, :]) % n2) / n2
    alt = 1.0 - 2.0 * (t % 2)

    def blocks(m):
        return m.reshape(TB, P, m.shape[1]).transpose(1, 0, 2).reshape(P, -1)

    cosn = np.cos(ang)[:, :P].copy()
    cosn[:, 0] = alt
    sinn = -np.sin(ang)
    sinn[:, 0] = alt
    weight = np.where(t == 0, 1.0, 2.0)[:, None] / n2
    itr = weight * np.cos(ang)
    iti = -weight * np.sin(ang)
    iti[0] = alt / n2
    dft = np.concatenate([blocks(m) for m in (np.cos(ang), np.sin(ang), cosn, sinn, itr, iti)], 1).astype(np.float32)

    pos = np.arange(SEQ, dtype=np.float32)
    tt = pos / np.float32(SEQ - 1)
    bands = (FILT_EMB - 1) // 2
    fb = np.linspace(1e-4, bands - 1, bands, dtype=np.float32)
    a = np.float32(2 * np.pi / SEQ) * pos[:, None] * fb[None, :]
    z = np.concatenate([tt[:, None], np.cos(a), -np.sin(a)], 1).T.astype(np.float32)
    deltas = np.abs(np.linspace(np.log(1e-2) / 1.5, np.log(1e-2) / 0.3, HY, dtype=np.float32))
    window = blocks(np.exp(-tt[:, None] * deltas)).astype(np.float32)

    i = np.arange(P)
    masks = [((i[:, None] // (2 * m) == i[None, :] // (2 * m)) & (i[:, None] // m != i[None, :] // m))
             for m in (1, 2, 4, 8, 16, 32, 64)]
    masks = np.concatenate(masks, 1).astype(np.int32)
    return {
        "t_dft": np.ascontiguousarray(dft),
        "t_emb": np.ascontiguousarray(z),
        "t_window": np.ascontiguousarray(window),
        "t_mask": np.ascontiguousarray(masks),
        "t_ident": np.eye(P, dtype=np.float32),
    }


class Units:

    def __init__(self, base, it=0, per=0):
        self.base, self.it, self.per = base, it, per

    def slot(self, j):
        return j % RING

    def number(self, j):
        return self.it * self.per + (self.base + j) if self.per else self.base + j

    def loads(self, j):
        n = (self.base + j) // RING + 1
        return self.it * (self.per // RING) + n if self.per else n


def build(nc, i, out):
    with ExitStack() as life:
        def sem(name):
            return life.enter_context(nc.semaphore(name))

        def sb(name, shape, dt=F32, scope=life):
            return scope.enter_context(nc.sbuf_tensor(name, shape, dt))

        x_res = sb("x_res", [P, KB, SEQ])
        raw = [sb(f"raw{s}", [P, UNIT]) for s in range(RING)]
        w_hi = [sb(f"w_hi{s}", [P, UNIT], F32R) for s in range(RING)]
        w_lo = [sb(f"w_lo{s}", [P, UNIT], F32R) for s in range(RING)]
        ident = sb("ident", [P, P])
        ones_d = sb("ones_d", [P, P])
        ones_h = sb("ones_h", [P, P])
        ones_1 = sb("ones_1", [P, P])
        rows = [sb(f"rows{n}", [P, P]) for n in range(3)]
        cols = [sb(f"cols{n}", [P, P]) for n in range(3)]
        mods = sb("mods", [P, N_MOD, KB, 2])
        silu_c = sb("silu_c", [P, KB, 2])
        scale_a = sb("scale_a", [P, 3, KB, 2])
        gate = sb("gate", [P, 3, KB, 2])
        gate_x = sb("gate_x", [P, KB])
        spec_mark = sb("spec_mark", [P, 1])
        lb = sb("lb", [P, 2, HEADS])
        lbe = sb("lbe", [P, 2, 2, HEADS])
        lbt = sb("lbt", [P, 2, HEADS])
        hg_cols = sb("hg_cols", [P, PAIRS, 10])
        hy_cols = sb("hy_cols", [P, PAIRS, 24])
        states = sb("states", [P, PAIRS, 4, DK])
        sq = [sb(f"sq{s}", [P, 512]) for s in range(2)]
        sq_sum = sb("sq_sum", [P, 512])
        root = sb("root", [P, 512])
        rstd = sb("rstd", [P, 512])
        xn = [sb(f"xn{s}", [P, 512]) for s in range(2)]

        ffn1 = ExitStack()
        y_res = sb("y_res", [P, KB, CTX], scope=ffn1)
        ada_raw = [sb(f"ada_raw{s}", [P, UNIT], scope=ffn1) for s in range(RING)]
        first = ExitStack()
        dft = sb("dft", [P, T_COLS], scope=first)
        emb = sb("emb", [FILT_EMB, SEQ], scope=first)
        window = sb("window", [P, TB, HY], scope=first)
        fw1 = sb("fw1", [FILT_EMB, FILT_ORDER], scope=first)
        fw23 = sb("fw23", [FILT_ORDER, 2, FILT_ORDER], scope=first)
        fbias = sb("fbias", [FILT_ORDER, 4], scope=first)
        fout = sb("fout", [FILT_ORDER, 2, 512], scope=first)
        hyd_row = sb("hyd_row", [1, 512], scope=first)
        hid = [sb(f"hid{n}", [FILT_ORDER, SEQ], scope=first) for n in range(3)]
        ang = [sb(f"ang{n}", [FILT_ORDER, SEQ], scope=first) for n in range(4)]
        tok_in = ExitStack()
        xin = sb("xin", [P, TB, D], scope=tok_in)
        yin = sb("yin", [P, TB, D], scope=tok_in)
        tok_in.close()
        taps = sb("taps", [P, TB, 2, 512], scope=first)
        tabs = sb("tabs", [P, TB, 2, 512], scope=first)
        l1inv = sb("l1inv", [P, 512], scope=first)
        tsum = sb("tsum", [P, TB, 512], scope=first)
        tdif = sb("tdif", [P, TB, 512], scope=first)
        spec_out = sb("spec_out", [P, 5, 512], scope=first)
        first.close()
        ffn = ExitStack()
        h1_hi = sb("h1_hi", [P, 2, KB, SEQ], F32R, scope=ffn)
        h1_lo = sb("h1_lo", [P, 2, KB, SEQ], F32R, scope=ffn)
        s1 = [sb(f"s1_{b}", [P, 512], scope=ffn) for b in range(2)]
        g1 = [sb(f"g1_{b}", [P, 512], scope=ffn) for b in range(2)]
        g1_hi = [sb(f"g1_hi{b}", [P, 512], F32R, scope=ffn) for b in range(2)]
        g1_lo = [sb(f"g1_lo{b}", [P, 512], F32R, scope=ffn) for b in range(2)]
        ffn.close()
        con = ExitStack()
        hc_hi = sb("hc_hi", [P, KB, CTX], F32R, scope=con)
        hc_lo = sb("hc_lo", [P, KB, CTX], F32R, scope=con)
        c_cur = sb("c_cur", [P, 10], scope=con)
        ck = sb("ck", [P, 2, 2, CTX], scope=con)
        cg = sb("cg", [P, 2, 2, CTX], scope=con)
        cv = sb("cv", [P, 2, CTX], scope=con)
        ctot = [sb(f"ctot{n}", [P, 2, 2, CTX // 2], scope=con) for n in range(2)]
        csum = sb("csum", [P, 2, 2, CTX], scope=con)
        cexp = sb("cexp", [P, 2, 2, CTX], scope=con)
        ckd = sb("ckd", [P, 2, 2, CTX], scope=con)
        ctok = sb("ctok", [P, 3, 4, P], scope=con)
        con.close()
        ffn1.close()

        mixo = ExitStack()
        mix = sb("mix", [P, KB, SEQ], scope=mixo)
        mixs = ExitStack()
        hx_hi = sb("hx_hi", [P, KB, SEQ], F32R, scope=mixs)
        hx_lo = sb("hx_lo", [P, KB, SEQ], F32R, scope=mixs)
        hgs = ExitStack()
        mask = sb("mask", [P, 7, P], I32, scope=hgs)
        x_cur = sb("x_cur", [P, 10], scope=hgs)
        s_cur = sb("s_cur", [P, 4, DK], scope=hgs)
        xk = sb("xk", [P, 2, 2, SEQ], scope=hgs)
        xa = sb("xa", [P, 2, 2, SEQ], scope=hgs)
        xe = sb("xe", [P, 2, 2, SEQ], scope=hgs)
        xv = sb("xv", [P, 2, SEQ], scope=hgs)
        xq = sb("xq", [P, 2, SEQ], scope=hgs)
        xg = sb("xg", [P, 2, SEQ], scope=hgs)
        eq = [sb(f"eq{n}", [P, 2, SEQ], scope=hgs) for n in range(2)]
        ek = [sb(f"ek{n}", [P, 2, SEQ], scope=hgs) for n in range(2)]
        lq = [sb(f"lq{n}", [P, 2, SEQ], scope=hgs) for n in range(2)]
        lk = [sb(f"lk{n}", [P, 2, SEQ], scope=hgs) for n in range(2)]
        prob = sb("prob", [P, 4, P], scope=hgs)
        cross = sb("cross", [P, 4, P], scope=hgs)
        vtok = sb("vtok", [P, 4, P], scope=hgs)
        osq = sb("osq", [P, 512], scope=hgs)
        onorm = sb("onorm", [P, 2, SEQ], scope=hgs)
        hgs.close()
        hys = ExitStack()
        dfty = sb("dfty", [P, T_COLS], scope=hys)
        y_cur = sb("y_cur", [P, 24], scope=hys)
        spec = sb("spec", [P, 2, 3, 2, 256], scope=hys)
        conv = sb("conv", [P, 3, 2, SEQ], scope=hys)
        ut = sb("ut", [P, TB, 256], scope=hys)
        prod = [sb(f"prod{n}", [P, 2, 256], scope=hys) for n in range(4)]
        yf = sb("yf", [P, 2, 2, 256], scope=hys)
        zg = sb("zg", [P, 2, SEQ], scope=hys)
        hys.close()
        mixs.close()
        outs = ExitStack()
        m_hi = sb("m_hi", [P, KB, SEQ], F32R, scope=outs)
        m_lo = sb("m_lo", [P, KB, SEQ], F32R, scope=outs)
        outs.close()
        mixo.close()
        f2 = ExitStack()
        h2_hi = sb("h2_hi", [P, KB, SEQ], F32R, scope=f2)
        h2_lo = sb("h2_lo", [P, KB, SEQ], F32R, scope=f2)
        s2 = [sb(f"s2_{b}", [P, SEQ], scope=f2) for b in range(2)]
        g2 = [sb(f"g2_{b}", [P, SEQ], scope=f2) for b in range(2)]
        g2_hi = [sb(f"g2_hi{b}", [P, SEQ], F32R, scope=f2) for b in range(2)]
        g2_lo = [sb(f"g2_lo{b}", [P, SEQ], F32R, scope=f2) for b in range(2)]
        xo = sb("xo", [P, KB, SEQ], scope=f2)
        xt = sb("xt", [P, TB, D], scope=f2)
        f2.close()

        bank = [life.enter_context(nc.psum_tensor(f"bank{n}", [P, 512], F32)) for n in range(8)]
        spec_dram = nc.dram_tensor("spec_spill", [2, P, 6, HY], F32, kind="Internal").ap()

        raw_in = [sem(f"raw_in{s}") for s in range(RING)]
        hi_done = sem("hi_done")
        lo_done = sem("lo_done")
        w_used = sem("w_used")
        ada_in = [sem(f"ada_in{s}") for s in range(RING)]
        ada_used = sem("ada_used")
        ada_out = sem("ada_out")

        small_in = sem("small_in")
        x_in = sem("x_in")
        y_in = sem("y_in")
        tab_in = sem("tab_in")
        memsets = sem("memsets")
        rows_t = sem("rows_t")
        cols_done = sem("cols_done")
        silu_done = sem("silu_done")
        tr_done = sem("tr_done")
        tr_out = sem("tr_out")
        lb_act = sem("lb_act")
        lb_dve = sem("lb_dve")

        fm_pe = sem("fm_pe")
        fm_arg = sem("fm_arg")
        fm_sin = sem("fm_sin")
        fm_dve = sem("fm_dve")
        fs_in = sem("fs_in")
        fs_taps_pe = sem("fs_taps_pe")
        fs_taps = sem("fs_taps")
        fs_abs = sem("fs_abs")
        fs_l1 = sem("fs_l1")
        fs_inv = sem("fs_inv")
        fs_norm = sem("fs_norm")
        fs_spec = sem("fs_spec")
        fs_out = sem("fs_out")
        fs_dma = sem("fs_dma")
        fs_tz = sem("fs_tz")
        fs_hyd = sem("fs_hyd")
        stats_done = sem("stats_done")

        def norm_sems(tag):
            return {n: sem(f"{tag}_{n}") for n in ("sq", "sum", "mean", "root", "rstd", "xn", "hi", "lo")}

        n1, nctx, nx, n2, nf = [norm_sems(t) for t in ("n1", "nc", "nx", "n2", "nf")]
        mod_done = sem("mod_done")

        def ffn_sems(tag):
            return {n: sem(f"{tag}_{n}") for n in ("silu", "gmul", "ghi", "glo", "bdone", "bfree")}

        fa, fb_ = ffn_sems("ffn1"), ffn_sems("ffn2")

        def chain_sems(tag, names):
            return {n: sem(f"{tag}_{n}") for n in names}

        cs = chain_sems("ctx", ("cur", "gate", "log", "v", "k", "init", "sum", "exp", "kd", "tpe", "tok", "st", "stout"))
        xs = chain_sems("hg", ("cur", "gate", "log", "v", "k", "init", "sum", "exp", "kq", "score", "pred",
                               "tpe", "tok", "ope", "osq", "mean", "root", "rstd", "on", "mix"))
        ys = chain_sems("hy", ("cur", "spec", "tab", "cb", "conv", "tpe", "ut", "specfree", "fft", "prod", "yf", "inv", "z"))
        msk_in = sem("msk_in")
        ms = chain_sems("wout", ("hi", "lo", "res"))
        fin = chain_sems("fin", ("o", "tr", "ev", "dma"))

        def load_unit(sy, un, j, src):
            n = un.number(j)
            if not (isinstance(n, int) and n < RING):
                sy.wait_ge(lo_done, n - RING + 1)
            a = src.shape[1]
            sy.dma_start(raw[un.slot(j)][:].rearrange("p (a c) -> p a c", a=a), src).then_inc(raw_in[un.slot(j)], 16)

        def col_src(w, kg, c0):
            return w[kg * 4 * P:(kg + 1) * 4 * P, bass.ds(c0, 256)].rearrange("(k p) c -> p k c", p=P)

        def row_src(w, chunk, q):
            return w[bass.ds(chunk * CHUNK, CHUNK), q * 512:(q + 1) * 512].rearrange("(f p) c -> p f c", p=P)

        def round_unit(ac, un, j):
            ac.wait_ge(raw_in[un.slot(j)], un.loads(j) * 16)
            ac.wait_ge(w_used, un.number(j) + 1)
            nc.scalar.activation(w_hi[un.slot(j)][:], raw[un.slot(j)][:], ACT.Copy).then_inc(hi_done, 1)

        def rest_unit(ve, un, j):
            ve.wait_ge(hi_done, un.number(j) + 1)
            nc.vector.tensor_tensor(w_lo[un.slot(j)][:], raw[un.slot(j)][:], w_hi[un.slot(j)][:].bitcast(F32),
                                    ALU.subtract).then_inc(lo_done, 1)

        def used(un, j):
            return un.number(j) + 1 + RING

        AHEAD = 2

        def three_pass(o, slot, c0, hi, lo, start, stop):
            nc.tensor.matmul(o, w_hi[slot][:, c0:c0 + P], hi, start=start, stop=False, skip_group_check=True)
            nc.tensor.matmul(o, w_hi[slot][:, c0:c0 + P], lo, start=False, stop=False, skip_group_check=True)
            return nc.tensor.matmul(o, w_lo[slot][:, c0:c0 + P], hi, start=False, stop=stop, skip_group_check=True)

        def col_unit(pe, un, j, kg, outs2, hi, lo, shared):
            pe.wait_ge(lo_done, un.number(j) + 1)
            for k in range(4):
                kb = 4 * kg + k
                for b in range(2):
                    last = three_pass(outs2[b], un.slot(j), k * 256 + b * P, hi(kb), lo(kb),
                                      kb == 0 and (b == 0 or not shared), kb == KB - 1)
            last.then_inc(w_used, 1)

        def norm_act(ac, s, src, ntok):
            for kb in range(KB):
                if kb >= 2:
                    ac.wait_ge(s["sum"], kb - 1)
                for t, part in enumerate(src):
                    ins = nc.scalar.activation(sq[kb % 2][:, t * 256:(t + 1) * 256], part[:, kb, :], ACT.Square)
                ins.then_inc(s["sq"], 1)
            ac.wait_ge(s["mean"], 1)
            nc.scalar.activation(root[:, 0:ntok], bank[7][:, 0:ntok], ACT.Sqrt, bias=EPS).then_inc(s["root"], 1)

        def norm_dve(ve, s, ntok):
            for kb in range(KB):
                ve.wait_ge(s["sq"], kb + 1)
                if kb == 0:
                    nc.vector.tensor_copy(sq_sum[:, 0:ntok], sq[0][:, 0:ntok]).then_inc(s["sum"], 1)
                else:
                    ve.wait_ge(s["sum"], kb)
                    nc.vector.tensor_tensor(sq_sum[:, 0:ntok], sq_sum[:, 0:ntok], sq[kb % 2][:, 0:ntok],
                                            ALU.add).then_inc(s["sum"], 1)
            ve.wait_ge(s["root"], 1)
            nc.vector.reciprocal(rstd[:, 0:ntok], root[:, 0:ntok]).then_inc(s["rstd"], 1)

        def norm_pe(pe, s, ntok):
            pe.wait_ge(s["sum"], KB)
            nc.tensor.matmul(bank[7][:, 0:ntok], ones_d[:], sq_sum[:, 0:ntok], start=True, stop=True).then_inc(s["mean"], 1)

        def modulate_dve(ve, s, which, src, lo, tcs):
            shift = (0, 3, 6)[which]
            ve.wait_ge(s["rstd"], 1)

            def scaled(kb):
                if kb >= 2:
                    ve.wait_ge(s["lo"], kb - 1)
                for t, part in enumerate(src):
                    ins = nc.vector.scalar_tensor_tensor(
                        out=xn[kb % 2][:, t * 256:(t + 1) * 256], in0=part[:, kb, :],
                        scalar=scale_a[:, which, kb, tcs[t]:tcs[t] + 1], in1=rstd[:, t * 256:(t + 1) * 256],
                        op0=ALU.mult, op1=ALU.mult)
                ins.then_inc(s["xn"], 1)

            scaled(0)
            for kb in range(KB):
                if kb + 1 < KB:
                    scaled(kb + 1)
                ve.wait_ge(s["hi"], kb + 1)
                for t in range(len(src)):
                    ins = nc.vector.scalar_tensor_tensor(
                        out=lo(t, kb), in0=xn[kb % 2][:, t * 256:(t + 1) * 256],
                        scalar=mods[:, shift, kb, tcs[t]:tcs[t] + 1], in1=s["hi_ap"](t, kb).bitcast(F32),
                        op0=ALU.add, op1=ALU.subtract)
                ins.then_inc(s["lo"], 1)

        def modulate_act(ac, s, which, hi, tcs):
            shift = (0, 3, 6)[which]
            for kb in range(KB):
                ac.wait_ge(s["xn"], kb + 1)
                for t in range(len(tcs)):
                    ins = nc.scalar.activation(hi(t, kb), xn[kb % 2][:, t * 256:(t + 1) * 256], ACT.Identity,
                                               bias=mods[:, shift, kb, tcs[t]:tcs[t] + 1])
                ins.then_inc(s["hi"], 1)

        n1["hi_ap"] = lambda t, kb: h1_hi[:, t, kb, :]
        nctx["hi_ap"] = lambda t, kb: hc_hi[:, kb, :]
        nx["hi_ap"] = lambda t, kb: hx_hi[:, kb, :]
        n2["hi_ap"] = lambda t, kb: h2_hi[:, kb, :]

        def ffn_loops(eng, base, body, loops):
            start = 0
            for count, ada in loops:
                with eng.Fori(0, count) as it:
                    body(Units(base + 8 + 12 * start, it, 12), it + start if start else it, ada, it)
                start += count

        F1_LOOPS = ((ADA_LOOPS, True), (N_CHUNK - 1 - ADA_LOOPS, False))
        F2_LOOPS = ((N_CHUNK - 1, False),)

        def ffn_sync(sy, base, w1, w3, w2, loops):
            un = Units(base)
            for j in range(8):
                load_unit(sy, un, j, col_src(w1 if j < 4 else w3, j % 4, 0))

            def body(un, c, ada, it):
                for j in range(12):
                    if j < 8:
                        load_unit(sy, un, j, col_src(w1 if j < 4 else w3, j % 4, (c + 1) * CHUNK))
                    else:
                        load_unit(sy, un, j, row_src(w2, c, j - 8))
                    if ada:
                        load_ada(sy, ADA0 + j, it, 12, lambda pair: (it * ADA_PER + (pair + ADA_FIRST * KB // 2)) * 256, j)

            ffn_loops(sy, base, body, loops)
            un = Units(base + 8 + 12 * (N_CHUNK - 1))
            for j in range(4):
                load_unit(sy, un, j, row_src(w2, N_CHUNK - 1, j))

        ADA0 = ADA_FIRST * KB // 2 * 4
        ada_w = i["ada_w"][0]

        def load_ada(sy, n0, it, per, col, j):
            sy.wait_ge(ada_used, it * per + (n0 + 1))
            sy.dma_start(ada_raw[j % RING][:].rearrange("p (a c) -> p a c", a=4),
                         col_src(ada_w, j % 4, col(j // 4))).then_inc(ada_in[j % RING], 16)

        def ada_unit(pe, n0, it, per, j, to):
            pe.wait_ge(ada_in[j % RING], (it * (per // RING) + (n0 // RING + 1)) * 16)
            for k in range(4):
                kb = 4 * (j % 4) + k
                for b in range(2):
                    last = nc.tensor.matmul(bank[to][:, 2 * b:2 * b + 2],
                                            ada_raw[j % RING][:, k * 256 + b * P:k * 256 + (b + 1) * P],
                                            silu_c[:, kb, :], start=(kb == 0 and b == 0), stop=(kb == KB - 1),
                                            skip_group_check=True)
            last.then_inc(ada_used, 1)

        mods_flat = mods[:].rearrange("p m k t -> p (m k t)")

        def ada_take(ve, used_value, pair, to):
            ve.wait_ge(ada_used, used_value)
            nc.vector.tensor_copy(mods_flat[:, bass.ds(pair * 4, 4)], bank[to][:, 0:4]).then_inc(ada_out, 1)

        def ffn_pe(pe, s, base, hi, lo, g_hi, g_lo, ntok, loops):
            def out(b):
                return bank[b][:, 0:ntok]

            def up(un, j, c):
                if c is not None and j in (0, 4):
                    pe.wait_ge(s["silu"] if j == 0 else s["gmul"], c * 2 + 2)
                b0 = 0 if j < 4 else 2
                col_unit(pe, un, j, j % 4, [out(b0), out(b0 + 1)], hi, lo, False)

            def down(un, j, jj, c):
                if jj == 0:
                    pe.wait_ge(s["glo"], c * 2 + 2)
                pe.wait_ge(lo_done, un.number(j) + 1)
                for q in range(4):
                    d = 4 * jj + q
                    pe.wait_ge(s["bfree"], c * KB + (d + 1))
                    for f in range(2):
                        last = three_pass(bank[4 + d % 2][:, 0:ntok], un.slot(j), f * 512 + q * P,
                                          g_hi[f][:], g_lo[f][:], f == 0, f == 1)
                    if q < 3:
                        last.then_inc(s["bdone"], 1)
                    else:
                        last.then_inc(w_used, 1)

            un = Units(base)
            for j in range(8):
                up(un, j, None)

            def body(un, c, ada, it):
                for j in range(12):
                    if j < 8:
                        up(un, j, c)
                    else:
                        down(un, j, j - 8, c)
                    if ada:
                        if j % 4 == 0:
                            pe.wait_ge(ada_out, it * ADA_PER + (ADA_FIRST * KB // 2 + j // 4 + 1 - (j > 0)))
                        ada_unit(pe, ADA0 + j, it, 12, j, 6 + j // 4 % 2)

            ffn_loops(pe, base, body, loops)
            un = Units(base + 8 + 12 * (N_CHUNK - 1))
            for j in range(4):
                down(un, j, j, N_CHUNK - 1)

        def ffn_act(ac, s, base, sil, g, g_hi, ntok, loops):
            def silu(un, j, c):
                ac.wait_ge(w_used, used(un, j))
                for b in range(2):
                    if not (isinstance(c, int) and c == 0):
                        ac.wait_ge(s["gmul"], c * 2 + (b + 1 - 2))
                    nc.scalar.activation(sil[b][:], bank[b][:, 0:ntok], ACT.Silu).then_inc(s["silu"], 1)

            def ghi(c):
                for b in range(2):
                    ac.wait_ge(s["gmul"], c * 2 + (b + 1))
                    nc.scalar.activation(g_hi[b][:], g[b][:], ACT.Copy).then_inc(s["ghi"], 1)

            un = Units(base)
            for j in range(8):
                round_unit(ac, un, j + AHEAD)
                if j == 3:
                    silu(un, j, 0)
            ghi(0)

            def body(un, c, ada, it):
                for j in range(12):
                    round_unit(ac, un, j + AHEAD)
                    if j == 3:
                        silu(un, j, c + 1)
                    if j == 11:
                        ac.wait_ge(w_used, used(un, j))
                        ghi(c + 1)

            ffn_loops(ac, base, body, loops)
            un = Units(base + 8 + 12 * (N_CHUNK - 1))
            for j in range(4):
                if un.number(j + AHEAD) < U_END:
                    round_unit(ac, un, j + AHEAD)

        def ffn_dve(ve, s, base, sil, g, g_hi, g_lo, ntok, res, gt, loops):
            ve.sem_inc(s["bfree"], 2)

            def gmul(un, j, c):
                ve.wait_ge(w_used, used(un, j))
                for b in range(2):
                    ve.wait_ge(s["silu"], c * 2 + (b + 1))
                    nc.vector.tensor_tensor(g[b][:], sil[b][:], bank[2 + b][:, 0:ntok], ALU.mult).then_inc(s["gmul"], 1)

            def glo(c):
                for b in range(2):
                    ve.wait_ge(s["ghi"], c * 2 + (b + 1))
                    nc.vector.tensor_tensor(g_lo[b][:], g[b][:], g_hi[b][:].bitcast(F32), ALU.subtract).then_inc(s["glo"], 1)

            def add(un, j, jj, c):
                if jj == 0:
                    ve.wait_ge(s["bfree"], c * KB + 2)
                for q in range(4):
                    d = 4 * jj + q
                    if q < 3:
                        ve.wait_ge(s["bdone"], c * 12 + (3 * jj + q + 1))
                    else:
                        ve.wait_ge(w_used, used(un, j))
                    for t, part in enumerate(res):
                        ins = nc.vector.scalar_tensor_tensor(
                            out=part[:, d, :], in0=bank[4 + d % 2][:, t * 256:(t + 1) * 256],
                            scalar=gate[:, gt, d, t:t + 1], in1=part[:, d, :], op0=ALU.mult, op1=ALU.add)
                    ins.then_inc(s["bfree"], 1)

            un = Units(base)
            for j in range(8):
                rest_unit(ve, un, j + AHEAD)
            gmul(un, 7, 0)
            glo(0)

            def body(un, c, ada, it):
                for j in range(12):
                    rest_unit(ve, un, j + AHEAD)
                    if j == 7:
                        gmul(un, j, c + 1)
                    if j >= 8:
                        add(un, j, j - 8, c)
                    if ada and j % 4 == 3:
                        ada_take(ve, it * 12 + (ADA0 + j + 1 + RING),
                                 it * ADA_PER + (ADA_FIRST * KB // 2 + j // 4), 6 + j // 4 % 2)
                glo(c + 1)

            ffn_loops(ve, base, body, loops)
            un = Units(base + 8 + 12 * (N_CHUNK - 1))
            for j in range(4):
                if un.number(j + AHEAD) < U_END:
                    rest_unit(ve, un, j + AHEAD)
                add(un, j, j, N_CHUNK - 1)

        def as_rows(ap, n):
            return ap.rearrange("(n p) -> n p", p=P) if len(ap.shape) == 1 else ap

        ROWS = [
            (0, 0, 128, i["ada_b"][0, 0:128 * P]),
            (1, 0, 16, i["ada_b"][0, 128 * P:144 * P]),
            (1, 16, 16, i["norm_ffn1"][0]), (1, 32, 16, i["norm_mix"][0]), (1, 48, 16, i["norm_ffn2"][0]),
            (1, 64, 16, i["final_norm"]), (1, 80, 8, i["hg_norm"][0]),
            (1, 88, 8, i["hg_lb_logits"][0, 0]), (1, 96, 8, i["hg_lb_logits"][0, 1]),
            (1, 104, 8, i["hg_lb_logits"][1, 0]), (1, 112, 8, i["hg_lb_logits"][1, 1]),
            (2, 0, 24, i["hy_conv_w"][0, 0]), (2, 24, 24, i["hy_conv_w"][0, 1]), (2, 48, 24, i["hy_conv_w"][0, 2]),
            (2, 72, 24, i["hy_conv_b"][0]), (2, 96, 16, i["c"][0]), (2, 112, 16, i["c_ctx"]),
        ]
        N_COLS = (128, 120, 128)
        C_GAIN = {0: 16, 1: 32, 2: 48}
        w_in = i["w_in"][0]
        HG_COLS = (0, HG, 2 * HG, 3 * HG, 4 * HG)
        HY_COLS = (5 * HG, 5 * HG + HY, 5 * HG + 2 * HY)

        block = life.enter_context(nc.Block())

        @block.sync
        def _(sy):
            for tile, r, n, src in ROWS:
                sy.dma_start(rows[tile][r:r + n, :], as_rows(src, n)).then_inc(small_in, 16)
            sy.dma_start(ident[:], i["t_ident"]).then_inc(small_in, 16)
            sy.dma_start(emb[:], i["t_emb"]).then_inc(small_in, 16)
            sy.dma_start(fw1[:], i["filt_w1"][0]).then_inc(small_in, 16)
            sy.dma_start(fw23[:, 0, :], i["filt_w2"][0]).then_inc(small_in, 16)
            sy.dma_start(fw23[:, 1, :], i["filt_w3"][0]).then_inc(small_in, 16)
            for n, name in enumerate(("filt_b1", "filt_b2", "filt_b3", "filt_freq")):
                sy.dma_start(fbias[:, n:n + 1], i[name][0].rearrange("(p a) -> p a", a=1)).then_inc(small_in, 16)
            sy.dma_start(dft[:], i["t_dft"]).then_inc(tab_in, 16)
            sy.dma_start(window[:].rearrange("p a c -> p (a c)"), i["t_window"]).then_inc(tab_in, 16)
            sy.dma_start(xin[:], i["x"][0].rearrange("(a p) d -> p a d", p=P)).then_inc(x_in, 16)
            sy.dma_start(yin[:], i["ctx"][0].rearrange("(a p) d -> p a d", p=P)).then_inc(y_in, 16)
            with sy.Fori(0, 2) as filt:
                for half in range(2):
                    sy.wait_ge(fs_taps_pe, filt * 8 + (half * 4 + 4))
                    for r in range(2):
                        sy.dma_start(fout[:, r, :],
                                     i["filt_w_out"][0][:, bass.ds(filt * (2 * HY) + (r * HY + half * 512), 512)]
                                     ).then_inc(fs_in, 16)
                    sy.wait_ge(fs_norm, filt * 2 + (half + 1))
                    sy.dma_start(hyd_row[:], i["hy_d"][0][bass.ds(filt, 1), half * 512:(half + 1) * 512]
                                 ).then_inc(fs_hyd, 16)
                    for j in range(4 * ADA_STEP):
                        load_ada(sy, half * 4 * ADA_STEP + j, filt, 8 * ADA_STEP,
                                 lambda pair: (filt * (2 * ADA_STEP) + (half * ADA_STEP + pair)) * 256, j)

            ffn_sync(sy, U_FFN1, i["ffn1_w1"][0], i["ffn1_w3"][0], i["ffn1_w2"][0], F1_LOOPS)
            with sy.Fori(0, PAIRS) as it:
                un = Units(U_CTX, it, 12)
                for j in range(12):
                    load_unit(sy, un, j, col_src(w_in, j % 4, it * 256 + HG_COLS[j // 4]))
            with sy.Fori(0, PAIRS) as it:
                un = Units(U_HG, it, 20)
                for j in range(20):
                    load_unit(sy, un, j, col_src(w_in, j % 4, it * 256 + HG_COLS[j // 4]))
            with sy.Fori(0, PAIRS) as it:
                un = Units(U_HY, it, 12)
                for j in range(12):
                    load_unit(sy, un, j, col_src(w_in, j % 4, it * 256 + HY_COLS[j // 4]))
            with sy.Fori(0, KB // 4) as it:
                un = Units(U_OUT, it, 8)
                for j in range(8):
                    load_unit(sy, un, j, col_src(i["w_out"][0], j % 4, it * 512 + j // 4 * 256))
            ffn_sync(sy, U_FFN2, i["ffn2_w1"][0], i["ffn2_w3"][0], i["ffn2_w2"][0], F2_LOOPS)
            for a in range(TB):
                sy.wait_ge(fin["ev"], 4 * (a + 1))
                sy.dma_start(out[0, a * P:(a + 1) * P, :], xt[:, a, :]).then_inc(fin["dma"], 16)
            sy.wait_ge(fin["dma"], 16 * TB)

        def halves(ap, m):
            return ap.rearrange("p h (n s m) -> p (h n) s m", s=2, m=m)

        @block.gpsimd
        def _(po):
            nc.gpsimd.memset(ones_d[:], 1.0 / D).then_inc(memsets, 1)
            nc.gpsimd.memset(ones_h[:], 1.0 / DK).then_inc(memsets, 1)
            nc.gpsimd.memset(ones_1[:], 1.0).then_inc(memsets, 1)

            with po.Fori(0, PAIRS) as it:
                po.wait_ge(cs["log"], it * 2 + 2)
                po.wait_ge(cs["init"], it + 1)
                total = cg[:].rearrange("p d h t -> p d (h t)")
                for lv in range(LEVELS):
                    m = 1 << lv
                    if lv:
                        po.wait_ge(cs["sum"], it * 24 + 3 * lv)
                    pair = total.rearrange("p d (n s) -> p d n s", s=2)
                    behind, before = halves(csum[:, 0], m)[:, :, 0, :], halves(csum[:, 1], m)[:, :, 1, :]
                    shape = list(behind.shape)
                    nc.gpsimd.tensor_tensor(behind, behind, pair[:, 0, :, 1:2].to_broadcast(shape), ALU.add
                                            ).then_inc(cs["sum"], 1)
                    nc.gpsimd.tensor_tensor(before, before, pair[:, 1, :, 0:1].to_broadcast(shape), ALU.add
                                            ).then_inc(cs["sum"], 1)
                    nxt = ctot[lv % 2][:].rearrange("p d h t -> p d (h t)")[:, :, 0:SEQ // m]
                    nc.gpsimd.tensor_tensor(nxt, pair[:, :, :, 0], pair[:, :, :, 1], ALU.add).then_inc(cs["sum"], 1)
                    total = nxt
                po.wait_ge(cs["exp"], it + 1)
                po.wait_ge(cs["k"], it * 2 + 2)
                nc.gpsimd.tensor_tensor(ckd[:], ck[:], cexp[:], ALU.mult).then_inc(cs["kd"], 1)

            po.wait_ge(nx["lo"], KB)
            po.dma_start(mask[:].rearrange("p a c -> p (a c)"), i["t_mask"]).then_inc(msk_in, 16)
            with po.Fori(0, PAIRS) as it:
                po.wait_ge(xs["init"], it + 1)
                po.wait_ge(xs["log"], it * 2 + 2)
                for lv in range(LEVELS):
                    m = 1 << lv
                    po.wait_ge(xs["exp"], it * 9 + (lv + 1))
                    if lv:
                        po.wait_ge(xs["sum"], it * 32 + 4 * lv)
                    upto, fromon = halves(xa[:, 0], m), halves(xa[:, 1], m)
                    behind, before = halves(xe[:, 0], m), halves(xe[:, 1], m)
                    shape = [P, SEQ // m, m]
                    for dst, side, tot in ((behind, 0, upto[:, :, 1, m - 1:m]), (upto, 1, upto[:, :, 0, m - 1:m]),
                                           (before, 1, fromon[:, :, 0, 0:1]), (fromon, 0, fromon[:, :, 1, 0:1])):
                        if dst is upto:
                            po.wait_ge(xs["sum"], it * 32 + (4 * lv + 1))
                        if dst is fromon:
                            po.wait_ge(xs["sum"], it * 32 + (4 * lv + 3))
                        nc.gpsimd.tensor_tensor(dst[:, :, side, :], dst[:, :, side, :], tot.to_broadcast(shape),
                                                ALU.add).then_inc(xs["sum"], 1)

            po.wait_ge(xs["mix"], 1 + PAIRS)
            po.dma_start(dfty[:], i["t_dft"]).then_inc(ys["tab"], 16)
            with po.Fori(0, PAIRS) as it:
                po.wait_ge(ys["specfree"], it + 1)
                for f in range(2):
                    po.dma_start(spec[:, f, :, :, :].rearrange("p a b c -> p (a b) c"),
                                 spec_dram[f][:, :, bass.ds(it * 256, 256)]).then_inc(ys["spec"], 16)

        SMALL = 16 * (len(ROWS) + 9)

        @block.tensor
        def _(pe):
            pe.sem_inc(w_used, RING)
            pe.sem_inc(ada_used, RING)
            pe.sem_inc(fs_taps_pe, 4)
            pe.sem_inc(fs_spec, 5)
            pe.wait_ge(small_in, SMALL)
            for n in range(3):
                nc.tensor.transpose(bank[n][:, 0:N_COLS[n]], rows[n][0:N_COLS[n], :],
                                    ident[0:N_COLS[n], 0:N_COLS[n]]).then_inc(rows_t, 1)
            pe.wait_ge(cols_done, 3)
            for n in range(3):
                if n:
                    pe.wait_ge(fm_sin, n)
                nc.tensor.matmul(bank[0][0:FILT_ORDER, 0:SEQ], fw1[:] if n == 0 else fw23[:, n - 1, :],
                                 emb[:] if n == 0 else hid[n - 1][:], start=True, stop=True).then_inc(fm_pe, 1)
            pe.wait_ge(fm_dve, 18)
            for g in range(16):
                src = xin if g < 8 else yin
                pe.wait_ge(x_in if g < 8 else y_in, 16)
                if g >= 4:
                    pe.wait_ge(tr_out, g - 3)
                for k in range(2):
                    for a in range(TB):
                        kb = 2 * (g % 8) + k
                        ins = nc.tensor.transpose(bank[g % 4][:, k * 256 + a * P:k * 256 + (a + 1) * P],
                                                  src[:, a, kb * P:(kb + 1) * P], ident[:])
                ins.then_inc(tr_done, 1)
            pe.wait_ge(memsets, 3)
            norm_pe(pe, n1, 512)
            pe.wait_ge(silu_done, 1)
            pe.wait_ge(fm_sin, 3)
            pe.wait_ge(tab_in, 32)
            pe.wait_ge(n1["root"], 1)
            with pe.Fori(0, 2) as filt:
                for half in range(2):
                    def ada_pairs(first, count):
                        for pair in range(first, first + count):
                            pe.wait_ge(ada_out, filt * (2 * ADA_STEP) + (half * ADA_STEP + pair + 1))
                            for j in range(4 * pair, 4 * pair + 4):
                                ada_unit(pe, half * 4 * ADA_STEP + j, filt, 8 * ADA_STEP, j, 6)

                    ada_pairs(0, 1)
                    pe.wait_ge(fs_in, filt * 64 + (half * 32 + 32))
                    pe.wait_ge(fs_taps, filt * 8 + (half * 4 + 4))
                    for a in range(TB):
                        for r in range(2):
                            nc.tensor.matmul(bank[2 * a + r][:], hid[2][:, a * P:(a + 1) * P], fout[:, r, :],
                                             start=True, stop=True).then_inc(fs_taps_pe, 1)
                    ada_pairs(1, 2)
                    pe.wait_ge(fs_abs, filt * 2 + (half + 1))
                    for n in range(4):
                        ins = nc.tensor.matmul(bank[4][:], ones_1[:], tabs[:, n // 2, n % 2, :], start=(n == 0), stop=(n == 3))
                    ins.then_inc(fs_l1, 1)
                    ada_pairs(3, 1)
                    pe.wait_ge(fs_norm, filt * 2 + (half + 2))
                    for o, (tab, part) in enumerate(((T_COS, tsum), (T_COS + P, tsum), (T_SIN, tdif), (T_SIN + P, tdif),
                                                     (T_COSN, tsum))):
                        pe.wait_ge(fs_out, filt * 10 + (half * 5 + o + 1))
                        for a in range(TB):
                            step = 256 if tab != T_COSN else P
                            ins = nc.tensor.matmul(bank[5 if (half * 5 + o) % 2 else 7][:],
                                                   dft[:, tab + a * step:tab + a * step + P], part[:, a, :],
                                                   start=(a == 0), stop=(a == 1))
                        ins.then_inc(fs_spec, 1)
                        if o == 2:
                            ada_pairs(4, 1)
                    ada_pairs(5, 1)

            pe.wait_ge(fs_taps, 20)
            pe.wait_ge(fs_out, 22)
            pe.wait_ge(n1["lo"], KB)
            ffn_pe(pe, fa, U_FFN1, lambda k: h1_hi[:, :, k, :], lambda k: h1_lo[:, :, k, :], g1_hi, g1_lo, 512, F1_LOOPS)

            norm_pe(pe, nctx, 256)
            pe.wait_ge(nctx["lo"], KB)
            with pe.Fori(0, PAIRS) as it:
                un = Units(U_CTX, it, 12)
                pe.wait_ge(cs["stout"], it + 1)
                for j in range(12):
                    col_unit(pe, un, j, j % 4, [bank[j // 4][:, 0:256], bank[j // 4][:, 256:512]],
                             lambda k: hc_hi[:, k, :], lambda k: hc_lo[:, k, :], True)
                for n in range(3):
                    pe.wait_ge(cs["kd"], it + 1)
                    pe.wait_ge(cs["v"], it + 1)
                    for h in range(2):
                        for a in range(TB):
                            src = cv[:, h, a * P:(a + 1) * P] if n == 2 else ckd[:, n, h, a * P:(a + 1) * P]
                            ins = nc.tensor.transpose(bank[3 + n][:, (2 * h + a) * P:(2 * h + a + 1) * P], src, ident[:])
                    ins.then_inc(cs["tpe"], 1)
                pe.wait_ge(cs["tok"], it * 3 + 3)
                for d in range(2):
                    for h in range(2):
                        for a in range(TB):
                            ins = nc.tensor.matmul(bank[6][:, (2 * d + h) * P:(2 * d + h + 1) * P],
                                                   ctok[:, d, 2 * h + a, :], ctok[:, 2, 2 * h + a, :],
                                                   start=(a == 0), stop=(a == 1))
                ins.then_inc(cs["st"], 1)

            norm_pe(pe, nx, 256)
            pe.wait_ge(nx["lo"], KB)
            with pe.Fori(0, PAIRS) as it:
                un = Units(U_HG, it, 20)
                pe.wait_ge(xs["mix"], it + 1)
                for j in range(20):
                    col_unit(pe, un, j, j % 4, [bank[j // 4][:, 0:256], bank[j // 4][:, 256:512]],
                             lambda k: hx_hi[:, k, :], lambda k: hx_lo[:, k, :], True)
                pe.wait_ge(xs["v"], it * 3 + 1)
                for h in range(2):
                    for a in range(TB):
                        ins = nc.tensor.transpose(bank[7][:, (2 * h + a) * P:(2 * h + a + 1) * P],
                                                  xv[:, h, a * P:(a + 1) * P], ident[:])
                ins.then_inc(xs["tpe"], 1)
                for s in range(LEVELS + 1):
                    pe.wait_ge(xs["kq"], it * 10 + (s + 1))
                    pe.wait_ge(xs["pred"], it * 9 + (s - 1) + 2)
                    for h in range(2):
                        for a in range(TB):
                            b = a if s < LEVELS else 1 - a
                            ins = nc.tensor.matmul(bank[5 + s % 2][:, (2 * h + a) * P:(2 * h + a + 1) * P],
                                                   lk[s % 2][:, h, a * P:(a + 1) * P], lq[s % 2][:, h, b * P:(b + 1) * P],
                                                   start=True, stop=True)
                    ins.then_inc(xs["score"], 1)
                pe.wait_ge(xs["pred"], it * 9 + 11)
                pe.wait_ge(xs["tok"], it + 1)
                pe.wait_ge(xs["kq"], it * 10 + 10)
                pe.wait_ge(xs["cur"], it + 1)
                pe.wait_ge(xs["v"], it * 3 + 2)
                for h in range(2):
                    for a in range(TB):
                        o = bank[3][:, h * 256 + a * P:h * 256 + (a + 1) * P]
                        b = 2 * h + a
                        other = 2 * h + 1 - a
                        nc.tensor.matmul(o, vtok[:, b, :], prob[:, b, :], start=True, stop=False)
                        nc.tensor.matmul(o, vtok[:, other, :], cross[:, other, :], start=False, stop=False)
                        nc.tensor.matmul(o, s_cur[:, h, :], lq[1][:, h, a * P:(a + 1) * P], start=False, stop=False)
                        ins = nc.tensor.matmul(o, s_cur[:, 2 + h, :], lk[1][:, h, a * P:(a + 1) * P], start=False, stop=True)
                ins.then_inc(xs["ope"], 1)
                pe.wait_ge(xs["osq"], it + 1)
                pe.wait_ge(xs["v"], it * 3 + 3)
                nc.tensor.matmul(bank[4][:], ones_h[:], osq[:], start=True, stop=True).then_inc(xs["mean"], 1)

            pe.wait_ge(ys["tab"], 16)
            with pe.Fori(0, PAIRS) as it:
                un = Units(U_HY, it, 12)
                pe.wait_ge(ys["z"], it * 2 + 2)
                for j in range(12):
                    col_unit(pe, un, j, j % 4, [bank[j // 4][:, 0:256], bank[j // 4][:, 256:512]],
                             lambda k: hx_hi[:, k, :], lambda k: hx_lo[:, k, :], True)
                for f in range(2):
                    if f == 0:
                        pe.wait_ge(ys["conv"], it * 12 + 4)
                    else:
                        pe.wait_ge(ys["z"], it * 2 + 3)
                    for a in range(TB):
                        for b in range(2):
                            src = conv[:, 0, b, a * P:(a + 1) * P] if f == 0 else zg[:, b, a * P:(a + 1) * P]
                            ins = nc.tensor.transpose(bank[3][:, a * 256 + b * P:a * 256 + (b + 1) * P], src, ident[:])
                    ins.then_inc(ys["tpe"], 1)
                    pe.wait_ge(ys["ut"], it * 2 + (f + 1))
                    for ri, tab in enumerate((T_COS, T_SINN)):
                        for b in range(2):
                            for a in range(TB):
                                ins = nc.tensor.matmul(bank[4 + ri][:, b * 256:(b + 1) * 256],
                                                       dfty[:, tab + a * 256 + b * P:tab + a * 256 + (b + 1) * P],
                                                       ut[:, a, :], start=(a == 0), stop=(a == 1))
                    ins.then_inc(ys["fft"], 1)
                    pe.wait_ge(ys["yf"], it * 4 + (2 * f + 2))
                    for b in range(2):
                        for n, (ri, fb) in enumerate(((0, 0), (0, 1), (1, 0), (1, 1))):
                            tab = (T_ITR, T_ITI)[ri] + fb * 256
                            ins = nc.tensor.matmul(bank[6][:, b * 256:(b + 1) * 256], yf[:, ri, fb, b * P:(b + 1) * P],
                                                   dfty[:, tab:tab + 256], start=(n == 0), stop=(n == 3))
                    ins.then_inc(ys["inv"], 1)

            pe.wait_ge(ms["lo"], 4)
            with pe.Fori(0, KB // 4) as it:
                un = Units(U_OUT, it, 8)
                for j in range(8):
                    if j % 4 == 0:
                        pe.wait_ge(ms["res"], it * 2 + (j // 4 + 1))
                    col_unit(pe, un, j, j % 4, [bank[j // 4][:, 0:256], bank[j // 4][:, 256:512]],
                             lambda k: m_hi[:, k, :], lambda k: m_lo[:, k, :], True)

            norm_pe(pe, n2, 256)
            pe.wait_ge(n2["lo"], KB)
            ffn_pe(pe, fb_, U_FFN2, lambda k: h2_hi[:, k, :], lambda k: h2_lo[:, k, :], g2_hi, g2_lo, 256, F2_LOOPS)
            norm_pe(pe, nf, 256)
            for g in range(8):
                a, q = g // 4, g % 4
                pe.wait_ge(fin["o"], KB)
                if g >= 4:
                    pe.wait_ge(fin["ev"], g - 3)
                for k in range(4):
                    ins = nc.tensor.transpose(bank[g % 4][:, k * P:(k + 1) * P], xo[:, 4 * q + k, a * P:(a + 1) * P], ident[:])
                ins.then_inc(fin["tr"], 1)

        @block.scalar
        def _(ac):
            ac.sem_inc(cs["stout"], 1)
            ac.sem_inc(fs_out, 2)
            ac.wait_ge(cols_done, 3)
            nc.scalar.activation(silu_c[:, :, 0], cols[2][:, 96:112], ACT.Silu)
            nc.scalar.activation(silu_c[:, :, 1], cols[2][:, 112:128], ACT.Silu).then_inc(silu_done, 1)
            ac.wait_ge(lb_dve, 3)
            nc.scalar.activation(lbe[:], lbe[:], ACT.Exp).then_inc(lb_act, 1)
            for n in range(3):
                ac.wait_ge(fm_dve, 6 * (n + 1))
                nc.scalar.activation(hid[n][:], ang[n % 2][:], ACT.Sin).then_inc(fm_sin, 1)
            for g in range(16):
                ac.wait_ge(tr_done, g + 1)
                dst = x_res if g < 8 else y_res
                nc.scalar.activation(dst[:, 2 * (g % 8):2 * (g % 8) + 2, :].rearrange("p a c -> p (a c)"),
                                     bank[g % 4][:], ACT.Copy).then_inc(tr_out, 1)
            ac.wait_ge(tr_out, 16)
            norm_act(ac, n1, [x_res, y_res], 512)
            with ac.Fori(0, 2) as filt:
                for half in range(2):
                    ac.wait_ge(fs_tz, filt * 2 + (half + 1))
                    nc.scalar.activation(tabs[:], taps[:], ACT.Abs).then_inc(fs_abs, 1)
                    for o in range(5):
                        ac.wait_ge(fs_spec, filt * 10 + (half * 5 + o + 6))
                        nc.scalar.activation(spec_out[:, o, :], bank[5 if (half * 5 + o) % 2 else 7][:], ACT.Copy
                                             ).then_inc(fs_out, 1)
                    ac.wait_ge(fs_out, filt * 10 + (half * 5 + 7))
                    dst = spec_dram[bass.ds(filt, 1)].rearrange("a p s c -> (a p) s c")[:, :, half * 512:(half + 1) * 512]
                    ac.dma_start(dst[:, 0:5, :], spec_out[:]).then_inc(fs_dma, 16)
                    ac.dma_start(dst[:, 5:6, :], spec_out[:, 1:2, :]).then_inc(fs_dma, 16)
                    ac.wait_ge(fs_dma, filt * 64 + (half * 32 + 32))
            for j in range(AHEAD):
                round_unit(ac, Units(0), j)
            modulate_act(ac, n1, 0, n1["hi_ap"], (0, 1))
            ffn_act(ac, fa, U_FFN1, s1, g1, g1_hi, 512, F1_LOOPS)

            ac.wait_ge(fa["bfree"], 2 + KB * N_CHUNK)
            norm_act(ac, nctx, [y_res], 256)
            modulate_act(ac, nctx, 1, nctx["hi_ap"], (1,))

            def gates(s, it, d, b, k_ap, g_ap, cur, value):
                ac.wait_ge(w_used, value)
                nc.scalar.activation(k_ap, bank[b][:], ACT.Sigmoid, scale=-1.0)
                nc.scalar.activation(g_ap, bank[b][:], ACT.Sigmoid).then_inc(s["gate"], 1)
                ac.wait_ge(s["gate"], it * 2 + (d + 1))
                ac.wait_ge(s["cur"], it + 1)
                for h in range(2):
                    ins = nc.scalar.activation(g_ap[:, h * 256:(h + 1) * 256], g_ap[:, h * 256:(h + 1) * 256], ACT.Ln,
                                               scale=cur[:, 4 + 2 * d + h:5 + 2 * d + h], bias=cur[:, 2 * d + h:2 * d + h + 1])
                ins.then_inc(s["log"], 1)
                for h in range(2):
                    ins = nc.scalar.activation(k_ap[:, h * 256:(h + 1) * 256], k_ap[:, h * 256:(h + 1) * 256], ACT.Copy,
                                               scale=cur[:, 4 + 2 * d + h:5 + 2 * d + h])
                ins.then_inc(s["k"], 1)

            def flat(ap):
                return ap.rearrange("p h t -> p (h t)")

            with ac.Fori(0, PAIRS) as it:
                un = Units(U_CTX, it, 12)
                for j in range(12):
                    round_unit(ac, un, j + AHEAD)
                    if j in (3, 7):
                        d = j // 4
                        gates(cs, it, d, d, flat(ck[:, d]), flat(cg[:, d]), c_cur, used(un, j))
                ac.wait_ge(w_used, used(un, 11))
                nc.scalar.activation(flat(cv[:]), bank[2][:], ACT.Copy).then_inc(cs["v"], 1)
                ac.wait_ge(cs["sum"], it * 24 + 24)
                nc.scalar.activation(cexp[:], csum[:], ACT.Exp).then_inc(cs["exp"], 1)
                for n in range(3):
                    ac.wait_ge(cs["tpe"], it * 3 + (n + 1))
                    nc.scalar.activation(flat(ctok[:, n]), bank[3 + n][:], ACT.Copy).then_inc(cs["tok"], 1)
                ac.wait_ge(cs["st"], it + 1)
                nc.scalar.activation(states[:, bass.ds(it, 1)].rearrange("p a n c -> p (a n c)"), bank[6][:], ACT.Copy
                                     ).then_inc(cs["stout"], 1)

            norm_act(ac, nx, [x_res], 256)
            modulate_act(ac, nx, 1, nx["hi_ap"], (0,))
            with ac.Fori(0, PAIRS) as it:
                un = Units(U_HG, it, 20)
                for j in range(20):
                    round_unit(ac, un, j + AHEAD)
                    if j in (3, 7):
                        d = j // 4
                        gates(xs, it, d, d, flat(xk[:, d]), flat(xa[:, d]), x_cur, used(un, j))
                    if j == 11:
                        ac.wait_ge(w_used, used(un, j))
                        nc.scalar.activation(flat(xv[:]), bank[2][:], ACT.Copy).then_inc(xs["v"], 1)
                    if j == 15:
                        ac.wait_ge(w_used, used(un, j))
                        nc.scalar.activation(flat(xq[:]), bank[3][:], ACT.Copy, scale=DK ** -0.5).then_inc(xs["v"], 1)
                    if j == 19:
                        ac.wait_ge(w_used, used(un, j))
                        nc.scalar.activation(flat(xg[:]), bank[4][:], ACT.Silu).then_inc(xs["v"], 1)
                ac.wait_ge(xs["tpe"], it + 1)
                nc.scalar.activation(flat(vtok[:]), bank[7][:], ACT.Copy).then_inc(xs["tok"], 1)
                ac.wait_ge(xs["log"], it * 2 + 2)
                ac.wait_ge(xs["init"], it + 1)
                for lv in range(LEVELS + 1):
                    s = lv + 1
                    if lv:
                        ac.wait_ge(xs["sum"], it * 32 + 4 * lv)
                    if lv >= 2:
                        ac.wait_ge(xs["kq"], it * 10 + (s - 1))
                    if lv < LEVELS:
                        m = 1 << lv
                        nc.scalar.activation(halves(eq[s % 2][:], m)[:, :, 1, :], halves(xa[:, 0], m)[:, :, 1, :], ACT.Exp)
                        nc.scalar.activation(halves(eq[s % 2][:], m)[:, :, 0, :], halves(xa[:, 1], m)[:, :, 0, :], ACT.Exp)
                        nc.scalar.activation(halves(ek[s % 2][:], m)[:, :, 0, :], halves(xe[:, 0], m)[:, :, 0, :], ACT.Exp)
                        nc.scalar.activation(halves(ek[s % 2][:], m)[:, :, 1, :], halves(xe[:, 1], m)[:, :, 1, :], ACT.Exp
                                             ).then_inc(xs["exp"], 1)
                    else:
                        nc.scalar.activation(eq[1][:], xa[:, 0], ACT.Exp)
                        nc.scalar.activation(ek[1][:], xa[:, 1], ACT.Exp).then_inc(xs["exp"], 1)
                ac.wait_ge(xs["ope"], it + 1)
                nc.scalar.activation(osq[:], bank[3][:], ACT.Square).then_inc(xs["osq"], 1)
                ac.wait_ge(xs["mean"], it + 1)
                nc.scalar.activation(root[:], bank[4][:], ACT.Sqrt, bias=EPS).then_inc(xs["root"], 1)

            with ac.Fori(0, PAIRS) as it:
                un = Units(U_HY, it, 12)
                for j in range(12):
                    round_unit(ac, un, j + AHEAD)
                    if j % 4 == 3:
                        ac.wait_ge(w_used, used(un, j))
                        ac.wait_ge(ys["cur"], it + 1)
                        p = j // 4
                        for b in range(2):
                            c0 = p * 8 + b * 4
                            ins = nc.scalar.activation(conv[:, p, b, :], bank[p][:, b * 256:(b + 1) * 256], ACT.Identity,
                                                       scale=y_cur[:, c0 + 1:c0 + 2], bias=y_cur[:, c0 + 3:c0 + 4])
                        ins.then_inc(ys["cb"], 1)
                for f in range(2):
                    ac.wait_ge(ys["tpe"], it * 2 + (f + 1))
                    nc.scalar.activation(flat(ut[:]), bank[3][:], ACT.Copy).then_inc(ys["ut"], 1)

            ac.wait_ge(ys["z"], 2 + 2 * PAIRS)
            for n in range(4):
                nc.scalar.activation(m_hi[:, 4 * n:4 * n + 4, :], mix[:, 4 * n:4 * n + 4, :], ACT.Copy).then_inc(ms["hi"], 1)
            with ac.Fori(0, KB // 4) as it:
                un = Units(U_OUT, it, 8)
                for j in range(8):
                    round_unit(ac, un, j + AHEAD)
            ac.wait_ge(ms["res"], 2 + KB // 2)
            norm_act(ac, n2, [x_res], 256)
            modulate_act(ac, n2, 2, n2["hi_ap"], (0,))
            ffn_act(ac, fb_, U_FFN2, s2, g2, g2_hi, 256, F2_LOOPS)
            ac.wait_ge(fb_["bfree"], 2 + KB * N_CHUNK)
            norm_act(ac, nf, [x_res], 256)
            for g in range(8):
                a, q = g // 4, g % 4
                ac.wait_ge(fin["tr"], g + 1)
                nc.scalar.activation(xt[:, a, q * 512:(q + 1) * 512], bank[g % 4][:], ACT.Copy).then_inc(fin["ev"], 1)

        @block.vector
        def _(ve):
            ve.sem_inc(ada_out, 1)
            ve.sem_inc(fs_taps, 4)
            ve.sem_inc(fs_norm, 1)
            ve.sem_inc(xs["mix"], 1)
            ve.sem_inc(xs["pred"], 2)
            ve.sem_inc(ys["z"], 2)
            ve.sem_inc(ys["specfree"], 1)
            ve.sem_inc(ms["res"], 2)
            for n in range(3):
                ve.wait_ge(rows_t, n + 1)
                nc.vector.tensor_copy(cols[n][:, 0:N_COLS[n]], bank[n][:, 0:N_COLS[n]]).then_inc(cols_done, 1)
            ve.wait_ge(cols_done, 3)
            logits = cols[1][:, 88:120].rearrange("p (d n h) -> p d n h", d=2, n=2)
            nc.vector.tensor_tensor(lbt[:], logits[:, :, 0], logits[:, :, 1], ALU.max).then_inc(lb_dve, 1)
            ve.wait_ge(lb_dve, 1)
            for n in range(2):
                nc.vector.tensor_tensor(lbe[:, n], logits[:, :, n], lbt[:], ALU.subtract).then_inc(lb_dve, 1)
            ve.wait_ge(lb_act, 1)
            nc.vector.tensor_tensor(lbt[:], lbe[:, 0], lbe[:, 1], ALU.add).then_inc(lb_dve, 1)
            ve.wait_ge(lb_dve, 4)
            nc.vector.reciprocal(lbt[:], lbt[:]).then_inc(lb_dve, 1)
            ve.wait_ge(lb_dve, 5)
            nc.vector.tensor_tensor(lb[:], lbe[:, 0], lbt[:], ALU.mult).then_inc(lb_dve, 1)
            ve.wait_ge(lb_dve, 6)
            for d in range(2):
                by_pair = lb[:, d, :].rearrange("p (a h) -> p a h", h=2)
                nc.vector.tensor_copy(hg_cols[:, :, 2 * d:2 * d + 2], by_pair)
                nc.vector.tensor_scalar(hg_cols[:, :, 4 + 2 * d:6 + 2 * d], by_pair, -1.0, 1.0, ALU.mult, ALU.add)
            nc.vector.tensor_copy(hg_cols[:, :, 8:10], cols[1][:, 80:88].rearrange("p (a h) -> p a h", h=2))
            for part in range(3):
                for w in range(4):
                    c0 = w * 24 + part * 8
                    dst = hy_cols[:, :, part * 8:(part + 1) * 8].rearrange("p a (b w) -> p a b w", w=4)[:, :, :, w]
                    ins = nc.vector.tensor_copy(dst, cols[2][:, c0:c0 + 8].rearrange("p (a b) -> p a b", b=2))
            ins.then_inc(lb_dve, 1)
            MAGIC = 1.5 * 2.0 ** 23
            C1 = 6.28125
            C2 = float(np.float32(TWO_PI - C1))
            C3 = float(np.float32(TWO_PI - C1 - C2))
            PI = float(np.nextafter(np.float32(np.pi), np.float32(0)))
            ve.wait_ge(small_in, SMALL)
            for n in range(3):
                ve.wait_ge(fm_pe, n + 1)
                r, a, k = ang[n % 2], ang[2], ang[3]
                nc.vector.tensor_scalar(a[:], bank[0][0:FILT_ORDER, 0:SEQ], fbias[:, n:n + 1], fbias[:, 3:4],
                                        ALU.add, ALU.mult).then_inc(fm_dve, 1)
                ve.wait_ge(fm_dve, 6 * n + 1)
                nc.vector.tensor_scalar(k[:], a[:], 1.0 / TWO_PI, MAGIC, ALU.mult, ALU.add).then_inc(fm_dve, 1)
                ve.wait_ge(fm_dve, 6 * n + 2)
                nc.vector.tensor_scalar(k[:], k[:], MAGIC, None, ALU.subtract).then_inc(fm_dve, 1)
                ve.wait_ge(fm_dve, 6 * n + 3)
                for m, (c, src) in enumerate(((C1, a), (C2, r))):
                    nc.vector.scalar_tensor_tensor(out=r[:], in0=k[:], scalar=-c, in1=src[:], op0=ALU.mult, op1=ALU.add
                                                   ).then_inc(fm_dve, 1)
                    ve.wait_ge(fm_dve, 6 * n + 4 + m)
                nc.vector.scalar_tensor_tensor(out=a[:], in0=k[:], scalar=-C3, in1=r[:], op0=ALU.mult, op1=ALU.add
                                               ).then_inc(fm_arg, 1)
                ve.wait_ge(fm_arg, n + 1)
                nc.vector.tensor_scalar(r[:], a[:], PI, -PI, ALU.min, ALU.max).then_inc(fm_dve, 1)
            norm_dve(ve, n1, 512)
            ve.wait_ge(tab_in, 32)
            with ve.Fori(0, 2) as filt:
                for half in range(2):
                    def take(pair):
                        value = filt * (8 * ADA_STEP) + (half * 4 * ADA_STEP + 4 * pair + 4 + RING)
                        ada_take(ve, value, filt * (2 * ADA_STEP) + (half * ADA_STEP + pair), 6)

                    take(0)
                    for n in range(4):
                        ve.wait_ge(fs_taps_pe, filt * 8 + (half * 4 + n + 5))
                        nc.vector.tensor_tensor(taps[:, n // 2, n % 2, :], bank[n][:],
                                                window[:, n // 2, half * 512:(half + 1) * 512], ALU.mult).then_inc(fs_taps, 1)
                    ve.wait_ge(fs_taps, filt * 8 + (half * 4 + 8))
                    nc.vector.memset(taps[0:1, 0, 1, :], 0.0).then_inc(fs_tz, 1)
                    take(1)
                    take(2)
                    ve.wait_ge(fs_l1, filt * 2 + (half + 1))
                    nc.vector.reciprocal(l1inv[:], bank[4][:]).then_inc(fs_inv, 1)
                    ve.wait_ge(fs_tz, filt * 2 + (half + 1))
                    ve.wait_ge(fs_spec, filt * 10 + (half * 5 + 5))
                    nc.vector.tensor_tensor(tsum[:], taps[:, :, 0, :], taps[:, :, 1, :], ALU.add)
                    nc.vector.tensor_tensor(tdif[:], taps[:, :, 1, :], taps[:, :, 0, :], ALU.subtract).then_inc(fs_inv, 1)
                    ve.wait_ge(fs_inv, filt * 8 + (half * 4 + 2))
                    for a in range(TB):
                        nc.vector.tensor_tensor(tsum[:, a, :], tsum[:, a, :], l1inv[:], ALU.mult)
                        ins = nc.vector.tensor_tensor(tdif[:, a, :], tdif[:, a, :], l1inv[:], ALU.mult)
                        ins.then_inc(fs_inv, 1)
                    ve.wait_ge(fs_inv, filt * 8 + (half * 4 + 4))
                    ve.wait_ge(fs_hyd, filt * 32 + (half * 16 + 16))
                    nc.vector.tensor_tensor(tsum[0:1, 0, :], tsum[0:1, 0, :], hyd_row[:], ALU.add).then_inc(fs_norm, 1)
                    take(3)
                    take(4)
                    take(5)

            def finish_mods(m0, m1):
                for t in range(2):
                    for m in range(m0, m1):
                        bias = cols[0][:, m * KB:(m + 1) * KB] if m < 8 else cols[1][:, 0:KB]
                        ins = nc.vector.tensor_tensor(mods[:, m, :, t], mods[:, m, :, t], bias, ALU.add)
                ins.then_inc(mod_done, 1)

            def norm_scale(which, m):
                g = C_GAIN[which]
                for t in range(2):
                    ins = nc.vector.scalar_tensor_tensor(out=scale_a[:, which, :, t], in0=mods[:, m, :, t], scalar=1.0,
                                                         in1=cols[1][:, g:g + KB], op0=ALU.add, op1=ALU.mult)
                return ins

            ve.wait_ge(ada_out, 1 + ADA_FIRST * KB // 2)
            finish_mods(0, ADA_FIRST)
            ve.wait_ge(mod_done, 1)
            norm_scale(0, 1)
            nc.vector.tensor_scalar(gate[:, 0], mods[:, 2], 0.5, None, ALU.mult).then_inc(mod_done, 1)
            for j in range(AHEAD):
                rest_unit(ve, Units(0), j)
            ve.wait_ge(mod_done, 2)
            modulate_dve(ve, n1, 0, [x_res, y_res], lambda t, kb: h1_lo[:, t, kb, :], (0, 1))
            ffn_dve(ve, fa, U_FFN1, s1, g1, g1_hi, g1_lo, 512, [x_res, y_res], 0, F1_LOOPS)

            ve.wait_ge(ada_out, 1 + N_MOD * KB // 2)
            finish_mods(ADA_FIRST, N_MOD)
            ve.wait_ge(mod_done, 3)
            norm_scale(1, 4)
            norm_scale(2, 7)
            nc.vector.tensor_copy(gate_x[:], mods[:, 5, :, 0])
            nc.vector.tensor_scalar(gate[:, 2], mods[:, 8], 0.5, None, ALU.mult).then_inc(mod_done, 1)
            norm_dve(ve, nctx, 256)
            ve.wait_ge(mod_done, 4)
            modulate_dve(ve, nctx, 1, [y_res], lambda t, kb: hc_lo[:, kb, :], (1,))
            with ve.Fori(0, PAIRS) as it:
                un = Units(U_CTX, it, 12)
                ve.wait_ge(cs["stout"], it + 1)
                nc.vector.tensor_copy(c_cur[:], hg_cols[:, bass.ds(it, 1), :].rearrange("p a c -> p (a c)")).then_inc(cs["cur"], 1)
                nc.vector.memset(csum[:], 0.0).then_inc(cs["init"], 1)
                for j in range(12):
                    rest_unit(ve, un, j + AHEAD)

            norm_dve(ve, nx, 256)
            ve.wait_ge(cs["stout"], 1 + PAIRS)
            modulate_dve(ve, nx, 1, [x_res], lambda t, kb: hx_lo[:, kb, :], (0,))
            ve.wait_ge(msk_in, 16)
            with ve.Fori(0, PAIRS) as it:
                un = Units(U_HG, it, 20)
                nc.vector.tensor_copy(s_cur[:].rearrange("p n c -> p (n c)"),
                                      states[:, bass.ds(it, 1)].rearrange("p a n c -> p (a n c)"))
                nc.vector.tensor_copy(x_cur[:], hg_cols[:, bass.ds(it, 1), :].rearrange("p a c -> p (a c)")).then_inc(xs["cur"], 1)
                nc.vector.memset(xe[:], 0.0).then_inc(xs["init"], 1)
                for j in range(20):
                    rest_unit(ve, un, j + AHEAD)

                def keys(s):
                    b = s % 2
                    if s >= 2:
                        ve.wait_ge(xs["score"], it * 9 + (s - 1))
                    if s == 0:
                        ve.wait_ge(xs["k"], it * 2 + 2)
                        ve.wait_ge(xs["v"], it * 3 + 2)
                        nc.vector.tensor_tensor(lk[b][:], xk[:, 0], xk[:, 1], ALU.add)
                        nc.vector.tensor_copy(lq[b][:], xq[:]).then_inc(xs["kq"], 1)
                        return
                    ve.wait_ge(xs["exp"], it * 9 + s)
                    nc.vector.tensor_tensor(lq[b][:], xq[:], eq[b][:], ALU.mult)
                    if s <= LEVELS:
                        m = 1 << (s - 1)
                        for side in range(2):
                            ins = nc.vector.tensor_tensor(halves(lk[b][:], m)[:, :, side, :], halves(xk[:, side], m)[:, :, side, :],
                                                          halves(ek[b][:], m)[:, :, side, :], ALU.mult)
                    else:
                        ins = nc.vector.tensor_tensor(lk[b][:], xq[:], ek[b][:], ALU.mult)
                    ins.then_inc(xs["kq"], 1)

                keys(0)
                for s in range(LEVELS + 1):
                    keys(s + 1)
                    ve.wait_ge(xs["score"], it * 9 + (s + 1))
                    scores = bank[5 + s % 2][:].rearrange("p (n c) -> p n c", n=4)
                    if s == 0:
                        nc.vector.tensor_tensor(prob[:], scores, ident[:].rearrange("p (a c) -> p a c", a=1).to_broadcast([P, 4, P]),
                                                ALU.mult).then_inc(xs["pred"], 1)
                    elif s < LEVELS:
                        ve.wait_ge(xs["pred"], it * 9 + (s + 2))
                        nc.vector.tensor_copy(spec_mark[:], ident[:, 0:1])
                        nc.vector.copy_predicated(prob[:], mask[:, s - 1:s, :].to_broadcast([P, 4, P]), scores
                                                  ).then_inc(xs["pred"], 1)
                    else:
                        nc.vector.tensor_copy(cross[:], scores).then_inc(xs["pred"], 1)
                ve.wait_ge(xs["root"], it + 1)
                nc.vector.reciprocal(rstd[:], root[:]).then_inc(xs["rstd"], 1)
                ve.wait_ge(xs["rstd"], it + 1)
                for h in range(2):
                    ins = nc.vector.scalar_tensor_tensor(out=onorm[:, h, :], in0=bank[3][:, h * 256:(h + 1) * 256],
                                                         scalar=x_cur[:, 8 + h:9 + h], in1=rstd[:, h * 256:(h + 1) * 256],
                                                         op0=ALU.mult, op1=ALU.mult)
                ins.then_inc(xs["on"], 1)
                ve.wait_ge(xs["on"], it + 1)
                ve.wait_ge(xs["v"], it * 3 + 3)
                nc.vector.tensor_tensor(mix[:, bass.ds(it * 2, 2), :], onorm[:], xg[:], ALU.mult).then_inc(xs["mix"], 1)

            with ve.Fori(0, PAIRS) as it:
                un = Units(U_HY, it, 12)
                nc.vector.tensor_copy(y_cur[:], hy_cols[:, bass.ds(it, 1), :].rearrange("p a c -> p (a c)")).then_inc(ys["cur"], 1)
                for j in range(12):
                    rest_unit(ve, un, j + AHEAD)
                    if j % 4 == 3:
                        p = j // 4
                        ve.wait_ge(ys["cb"], it * 3 + (p + 1))
                        for b in range(2):
                            c0 = p * 8 + b * 4
                            o = conv[:, p, b, :].rearrange("p (r c) -> p r c", c=GRID_W)
                            u = bank[p][:, b * 256:(b + 1) * 256].rearrange("p (r c) -> p r c", c=GRID_W)
                            nc.vector.scalar_tensor_tensor(out=o[:, :, 1:], in0=u[:, :, :-1], scalar=y_cur[:, c0:c0 + 1],
                                                           in1=o[:, :, 1:], op0=ALU.mult, op1=ALU.add).then_inc(ys["conv"], 1)
                            ve.wait_ge(ys["conv"], it * 12 + (4 * p + 2 * b + 1))
                            nc.vector.scalar_tensor_tensor(out=o[:, :, :-1], in0=u[:, :, 1:], scalar=y_cur[:, c0 + 2:c0 + 3],
                                                           in1=o[:, :, :-1], op0=ALU.mult, op1=ALU.add).then_inc(ys["conv"], 1)
                ve.wait_ge(ys["spec"], it * 32 + 32)
                for f in range(2):
                    ve.wait_ge(ys["fft"], it * 2 + (f + 1))
                    re, im = (bank[4 + n][:].rearrange("p (b c) -> p b c", b=2) for n in range(2))
                    for n, (part, s) in enumerate(((re, 0), (im, 1), (re, 1), (im, 2))):
                        ins = nc.vector.tensor_tensor(prod[n][:], part, spec[:, f, s], ALU.mult)
                        if n % 2:
                            ins.then_inc(ys["prod"], 1)
                    for n in range(2):
                        ve.wait_ge(ys["prod"], it * 4 + (2 * f + n + 1))
                        nc.vector.tensor_tensor(yf[:, n], prod[2 * n][:], prod[2 * n + 1][:],
                                                ALU.add if n else ALU.subtract).then_inc(ys["yf"], 1)
                    if f == 1:
                        ve.wait_ge(ys["prod"], it * 4 + 4)
                        nc.vector.tensor_copy(spec_mark[:], ident[:, 0:1]).then_inc(ys["specfree"], 1)
                    ve.wait_ge(ys["inv"], it * 2 + (f + 1))
                    ve.wait_ge(ys["conv"], it * 12 + 12)
                    y = bank[6][:].rearrange("p (b c) -> p b c", b=2)
                    if f == 0:
                        nc.vector.tensor_tensor(zg[:], y, conv[:, 1], ALU.mult).then_inc(ys["z"], 1)
                    else:
                        nc.vector.tensor_tensor(mix[:, bass.ds(it * 2 + HEADS, 2), :], y, conv[:, 2], ALU.mult).then_inc(ys["z"], 1)

            for n in range(4):
                ve.wait_ge(ms["hi"], n + 1)
                nc.vector.tensor_tensor(m_lo[:, 4 * n:4 * n + 4, :], mix[:, 4 * n:4 * n + 4, :],
                                        m_hi[:, 4 * n:4 * n + 4, :].bitcast(F32), ALU.subtract).then_inc(ms["lo"], 1)
            with ve.Fori(0, KB // 4) as it:
                un = Units(U_OUT, it, 8)
                for j in range(8):
                    rest_unit(ve, un, j + AHEAD)
                    if j % 4 == 3:
                        ve.wait_ge(w_used, used(un, j))
                        for b in range(2):
                            d = it * 4 + (j // 4 * 2 + b)
                            res = x_res[:, bass.ds(d, 1), :].rearrange("p a c -> p (a c)")
                            ins = nc.vector.scalar_tensor_tensor(
                                out=res, in0=bank[j // 4][:, b * 256:(b + 1) * 256],
                                scalar=gate_x[:, bass.ds(d, 1)], in1=res, op0=ALU.mult, op1=ALU.add)
                        ins.then_inc(ms["res"], 1)

            norm_dve(ve, n2, 256)
            modulate_dve(ve, n2, 2, [x_res], lambda t, kb: h2_lo[:, kb, :], (0,))
            ffn_dve(ve, fb_, U_FFN2, s2, g2, g2_hi, g2_lo, 256, [x_res], 2, F2_LOOPS)
            norm_dve(ve, nf, 256)
            ve.wait_ge(nf["rstd"], 1)
            for kb in range(KB):
                nc.vector.scalar_tensor_tensor(out=xo[:, kb, :], in0=x_res[:, kb, :], scalar=cols[1][:, 64 + kb:65 + kb],
                                               in1=rstd[:, 0:256], op0=ALU.mult, op1=ALU.mult).then_inc(fin["o"], 1)


_INS = ['x', 'c', 'ctx', 'c_ctx', 'ada_w', 'ada_b', 'norm_ffn1', 'ffn1_w1', 'ffn1_w3', 'ffn1_w2', 'norm_mix', 'w_in',
        'hg_lb_logits', 'hg_norm', 'hy_conv_w', 'hy_conv_b', 'filt_w1', 'filt_b1', 'filt_w2', 'filt_b2', 'filt_w3',
        'filt_b3', 'filt_freq', 'filt_w_out', 'hy_d', 'w_out', 'norm_ffn2', 'ffn2_w1', 'ffn2_w3', 'ffn2_w2',
        'final_norm']


def kernel(**inputs):
    import concourse.bacc as _bacc
    from concourse.bass_utils import run_bass_kernel_spmd as _run

    nc = _bacc.Bacc("TRN2", target_bir_lowering=False, num_devices=1)
    arrays, args = {}, {}
    for name, a in [(n, inputs[n]) for n in _INS] + list(shape_tables().items()):
        a = np.ascontiguousarray(a)
        arrays[f"in_{name}_dram"] = a
        args[name] = nc.dram_tensor(f"in_{name}_dram", a.shape, mybir.dt.from_np(a.dtype), kind="ExternalInput").ap()
    out = nc.dram_tensor("out_0_dram", (1, SEQ, D), F32, kind="ExternalOutput").ap()
    build(nc, args, out)
    r = _run(nc, [arrays], core_ids=[0])
    return r.results[0]["out_0_dram"]
```

```python
from contextlib import ExitStack

import numpy as np

import concourse.bass as bass
from concourse import mybir

F32 = mybir.dt.float32
F32R = mybir.dt.float32r
I32 = mybir.dt.int32
ACT = mybir.ActivationFunctionType
ALU = mybir.AluOpType

P = 128
D = 2048
KB = D // P
SEQ = 256
CTX = 256
TB = SEQ // P
FF = 5632
CHUNK = 256
N_CHUNK = FF // CHUNK
N_MOD = 9
EPS = 1e-6
HEADS = 8
PAIRS = HEADS // 2
DK = 128
HG = HEADS * DK
HY = D - HG
GRID_W = 64
FILT_EMB = 33
FILT_ORDER = 64
LEVELS = 8
UNIT = 1024
RING = 4
KG = KB // 4
TWO_PI = 2.0 * np.pi

U_FFN1 = 0
U_CTX = U_FFN1 + 12 * N_CHUNK
U_HG = U_CTX + 12 * PAIRS
U_HY = U_HG + 20 * PAIRS
U_OUT = U_HY + 12 * PAIRS
U_FFN2 = U_OUT + 4 * (KB // 2)
U_END = U_FFN2 + 12 * N_CHUNK

ADA_FIRST = 3
HALF = 1024
ADA_FIRST_H = 2 * ADA_FIRST
ADA_BOTH = 4
ADA_LATENT = 8
FILT_STEPS = 4
ADA_BODY = 3 * KB
ADA_PE = (3, 6, 9, 12, 15)
ADA_EW = KB - len(ADA_PE)

T_COS, T_SIN, T_COSN, T_SINN, T_ITR, T_ITI = 0, 512, 1024, 1280, 1792, 2304
T_COLS = 2816


def shape_tables():
    n2 = 2 * SEQ
    t = np.arange(SEQ, dtype=np.float64)
    ang = 2 * np.pi * ((t[:, None] * t[None, :]) % n2) / n2
    alt = 1.0 - 2.0 * (t % 2)

    def blocks(m):
        return m.reshape(TB, P, m.shape[1]).transpose(1, 0, 2).reshape(P, -1)

    cosn = np.cos(ang)[:, :P].copy()
    cosn[:, 0] = alt
    sinn = -np.sin(ang)
    sinn[:, 0] = alt
    weight = np.where(t == 0, 1.0, 2.0)[:, None] / n2
    itr = weight * np.cos(ang)
    iti = -weight * np.sin(ang)
    iti[0] = alt / n2
    dft = np.concatenate([blocks(m) for m in (np.cos(ang), np.sin(ang), cosn, sinn, itr, iti)], 1).astype(np.float32)

    pos = np.arange(SEQ, dtype=np.float32)
    tt = pos / np.float32(SEQ - 1)
    bands = (FILT_EMB - 1) // 2
    fb = np.linspace(1e-4, bands - 1, bands, dtype=np.float32)
    a = np.float32(2 * np.pi / SEQ) * pos[:, None] * fb[None, :]
    z = np.concatenate([tt[:, None], np.cos(a), -np.sin(a)], 1).T.astype(np.float32)
    deltas = np.abs(np.linspace(np.log(1e-2) / 1.5, np.log(1e-2) / 0.3, HY, dtype=np.float32))
    window = blocks(np.exp(-tt[:, None] * deltas)).astype(np.float32)

    i = np.arange(P)
    masks = [((i[:, None] // (2 * m) == i[None, :] // (2 * m)) & (i[:, None] // m != i[None, :] // m))
             for m in (1, 2, 4, 8, 16, 32, 64)]
    masks = np.concatenate(masks, 1).astype(np.int32)
    return {
        "t_dft": np.ascontiguousarray(dft),
        "t_emb": np.ascontiguousarray(z),
        "t_window": np.ascontiguousarray(window),
        "t_mask": np.ascontiguousarray(masks),
        "t_ident": np.eye(P, dtype=np.float32),
    }


class Units:

    def __init__(self, base, it=0, per=0):
        self.base, self.it, self.per = base, it, per

    def slot(self, j):
        return j % RING

    def number(self, j):
        return self.it * self.per + (self.base + j) if self.per else self.base + j

    def loads(self, j):
        n = (self.base + j) // RING + 1
        return self.it * (self.per // RING) + n if self.per else n


def build(nc, i, out):
    with ExitStack() as life:
        def sem(name):
            return life.enter_context(nc.semaphore(name))

        def sb(name, shape, dt=F32, scope=life):
            return scope.enter_context(nc.sbuf_tensor(name, shape, dt))

        x_res = sb("x_res", [P, KB, SEQ])
        raw = [sb(f"raw{s}", [P, UNIT]) for s in range(RING)]
        w_hi = [sb(f"w_hi{s}", [P, UNIT], F32R) for s in range(RING)]
        w_lo = [sb(f"w_lo{s}", [P, UNIT], F32R) for s in range(RING)]
        ident = sb("ident", [P, P])
        ones_d = sb("ones_d", [P, P])
        ones_h = sb("ones_h", [P, P])
        ones_1 = sb("ones_1", [P, P])
        rows = [sb(f"rows{n}", [P, P]) for n in range(3)]
        cols = [sb(f"cols{n}", [P, P]) for n in range(3)]
        mods = sb("mods", [P, N_MOD, KB, 2])
        silu_c = sb("silu_c", [P, KB, 2])
        scale_a = sb("scale_a", [P, 3, KB, 2])
        gate = sb("gate", [P, 3, KB, 2])
        gate_x = sb("gate_x", [P, KB])
        spec_mark = sb("spec_mark", [P, 1])
        lb = sb("lb", [P, 2, HEADS])
        lbe = sb("lbe", [P, 2, 2, HEADS])
        lbt = sb("lbt", [P, 2, HEADS])
        hg_cols = sb("hg_cols", [P, PAIRS, 10])
        hy_cols = sb("hy_cols", [P, PAIRS, 24])
        states = sb("states", [P, PAIRS, 4, DK])
        ada_sum = [states[:, 2 * t:2 * t + 2].rearrange("p a n c -> p (a n c)") for t in range(2)]
        sq2 = sb("sq2", [P, 2 * 512])
        sq = [sq2[:, n * 512:(n + 1) * 512] for n in range(2)]
        sq_sum = sb("sq_sum", [P, 512])
        root = sb("root", [P, 512])
        rstd = sb("rstd", [P, 512])
        xn2 = sb("xn2", [P, 2 * 512])
        xn = [xn2[:, n * 512:(n + 1) * 512] for n in range(2)]
        ada_prod = [sq2, xn2]

        ffn1 = ExitStack()
        y_res = sb("y_res", [P, KB, CTX], scope=ffn1)
        ada_raw = [sb(f"ada_raw{s}", [P, UNIT], scope=ffn1) for s in range(RING)]
        first = ExitStack()
        dft = sb("dft", [P, T_COLS], scope=first)
        emb = sb("emb", [FILT_EMB, SEQ], scope=first)
        window = sb("window", [P, TB, HY], scope=first)
        fw1 = sb("fw1", [FILT_EMB, FILT_ORDER], scope=first)
        fw23 = sb("fw23", [FILT_ORDER, 2, FILT_ORDER], scope=first)
        fbias = sb("fbias", [FILT_ORDER, 4], scope=first)
        fout = sb("fout", [FILT_ORDER, 2, 512], scope=first)
        hyd_row = sb("hyd_row", [1, 512], scope=first)
        hid = [sb(f"hid{n}", [FILT_ORDER, SEQ], scope=first) for n in range(3)]
        ang = [sb(f"ang{n}", [FILT_ORDER, SEQ], scope=first) for n in range(4)]
        tok_in = ExitStack()
        xin = sb("xin", [P, TB, D], scope=tok_in)
        yin = sb("yin", [P, TB, D], scope=tok_in)
        tok_in.close()
        taps = sb("taps", [P, TB, 2, 512], scope=first)
        tabs = sb("tabs", [P, TB, 2, 512], scope=first)
        l1inv = sb("l1inv", [P, 512], scope=first)
        tsum = sb("tsum", [P, TB, 512], scope=first)
        tdif = sb("tdif", [P, TB, 512], scope=first)
        spec_out = sb("spec_out", [P, 5, 512], scope=first)
        first.close()
        ffn = ExitStack()
        h1_hi = sb("h1_hi", [P, 2, KB, SEQ], F32R, scope=ffn)
        h1_lo = sb("h1_lo", [P, 2, KB, SEQ], F32R, scope=ffn)
        s1 = [sb(f"s1_{b}", [P, 512], scope=ffn) for b in range(2)]
        g1 = [sb(f"g1_{b}", [P, 512], scope=ffn) for b in range(2)]
        g1_hi = [sb(f"g1_hi{b}", [P, 512], F32R, scope=ffn) for b in range(2)]
        g1_lo = [sb(f"g1_lo{b}", [P, 512], F32R, scope=ffn) for b in range(2)]
        ffn.close()
        con = ExitStack()
        hc_hi = sb("hc_hi", [P, KB, CTX], F32R, scope=con)
        hc_lo = sb("hc_lo", [P, KB, CTX], F32R, scope=con)
        c_cur = sb("c_cur", [P, 10], scope=con)
        ck = sb("ck", [P, 2, 2, CTX], scope=con)
        cg = sb("cg", [P, 2, 2, CTX], scope=con)
        cv = sb("cv", [P, 2, CTX], scope=con)
        ctot = [sb(f"ctot{n}", [P, 2, 2, CTX // 2], scope=con) for n in range(2)]
        csum = sb("csum", [P, 2, 2, CTX], scope=con)
        cexp = sb("cexp", [P, 2, 2, CTX], scope=con)
        ckd = sb("ckd", [P, 2, 2, CTX], scope=con)
        ctok = sb("ctok", [P, 3, 4, P], scope=con)
        con.close()
        ffn1.close()

        mixo = ExitStack()
        mix = sb("mix", [P, KB, SEQ], scope=mixo)
        mixs = ExitStack()
        hx_hi = sb("hx_hi", [P, KB, SEQ], F32R, scope=mixs)
        hx_lo = sb("hx_lo", [P, KB, SEQ], F32R, scope=mixs)
        hgs = ExitStack()
        mask = sb("mask", [P, 7, P], I32, scope=hgs)
        x_cur = sb("x_cur", [P, 10], scope=hgs)
        s_cur = sb("s_cur", [P, 4, DK], scope=hgs)
        xk = sb("xk", [P, 2, 2, SEQ], scope=hgs)
        xa = sb("xa", [P, 2, 2, SEQ], scope=hgs)
        xe = sb("xe", [P, 2, 2, SEQ], scope=hgs)
        xv = sb("xv", [P, 2, SEQ], scope=hgs)
        xq = sb("xq", [P, 2, SEQ], scope=hgs)
        xg = sb("xg", [P, 2, SEQ], scope=hgs)
        eq = [sb(f"eq{n}", [P, 2, SEQ], scope=hgs) for n in range(2)]
        ek = [sb(f"ek{n}", [P, 2, SEQ], scope=hgs) for n in range(2)]
        lq = [sb(f"lq{n}", [P, 2, SEQ], scope=hgs) for n in range(2)]
        lk = [sb(f"lk{n}", [P, 2, SEQ], scope=hgs) for n in range(2)]
        prob = sb("prob", [P, 4, P], scope=hgs)
        cross = sb("cross", [P, 4, P], scope=hgs)
        vtok = sb("vtok", [P, 4, P], scope=hgs)
        osq = sb("osq", [P, 512], scope=hgs)
        onorm = sb("onorm", [P, 2, SEQ], scope=hgs)
        hgs.close()
        hys = ExitStack()
        dfty = sb("dfty", [P, T_COLS], scope=hys)
        y_cur = sb("y_cur", [P, 24], scope=hys)
        spec = sb("spec", [P, 2, 3, 2, 256], scope=hys)
        conv = sb("conv", [P, 3, 2, SEQ], scope=hys)
        ut = sb("ut", [P, TB, 256], scope=hys)
        prod = [sb(f"prod{n}", [P, 2, 256], scope=hys) for n in range(4)]
        yf = sb("yf", [P, 2, 2, 256], scope=hys)
        zg = sb("zg", [P, 2, SEQ], scope=hys)
        hys.close()
        mixs.close()
        outs = ExitStack()
        m_hi = sb("m_hi", [P, KB, SEQ], F32R, scope=outs)
        m_lo = sb("m_lo", [P, KB, SEQ], F32R, scope=outs)
        outs.close()
        mixo.close()
        f2 = ExitStack()
        h2_hi = sb("h2_hi", [P, KB, SEQ], F32R, scope=f2)
        h2_lo = sb("h2_lo", [P, KB, SEQ], F32R, scope=f2)
        s2 = [sb(f"s2_{b}", [P, SEQ], scope=f2) for b in range(2)]
        g2 = [sb(f"g2_{b}", [P, SEQ], scope=f2) for b in range(2)]
        g2_hi = [sb(f"g2_hi{b}", [P, SEQ], F32R, scope=f2) for b in range(2)]
        g2_lo = [sb(f"g2_lo{b}", [P, SEQ], F32R, scope=f2) for b in range(2)]
        xo = sb("xo", [P, KB, SEQ], scope=f2)
        xt = sb("xt", [P, TB, D], scope=f2)
        f2.close()

        bank = [life.enter_context(nc.psum_tensor(f"bank{n}", [P, 512], F32)) for n in range(8)]
        spec_dram = nc.dram_tensor("spec_spill", [2, P, 6, HY], F32, kind="Internal").ap()

        raw_in = [sem(f"raw_in{s}") for s in range(RING)]
        hi_done = sem("hi_done")
        lo_done = sem("lo_done")
        w_used = sem("w_used")
        ada_in = [sem(f"ada_in{s}") for s in range(RING)]
        ada_x = sem("ada_x")
        ada_c = sem("ada_c")
        ada_add = sem("ada_add")
        ada_used = sem("ada_used")
        ada_pe = sem("ada_pe")
        ada_out = sem("ada_out")

        small_in = sem("small_in")
        x_in = sem("x_in")
        y_in = sem("y_in")
        tab_in = sem("tab_in")
        memsets = sem("memsets")
        rows_t = sem("rows_t")
        cols_done = sem("cols_done")
        silu_done = sem("silu_done")
        tr_done = sem("tr_done")
        tr_out = sem("tr_out")
        lb_act = sem("lb_act")
        lb_dve = sem("lb_dve")

        fm_pe = sem("fm_pe")
        fm_arg = sem("fm_arg")
        fm_sin = sem("fm_sin")
        fm_dve = sem("fm_dve")
        fs_in = sem("fs_in")
        fs_taps_pe = sem("fs_taps_pe")
        fs_taps = sem("fs_taps")
        fs_abs = sem("fs_abs")
        fs_l1 = sem("fs_l1")
        fs_inv = sem("fs_inv")
        fs_norm = sem("fs_norm")
        fs_spec = sem("fs_spec")
        fs_out = sem("fs_out")
        fs_dma = sem("fs_dma")
        fs_tz = sem("fs_tz")
        fs_hyd = sem("fs_hyd")
        stats_done = sem("stats_done")

        def norm_sems(tag):
            return {n: sem(f"{tag}_{n}") for n in ("sq", "sum", "mean", "root", "rstd", "xn", "hi", "lo")}

        n1, nctx, nx, n2, nf = [norm_sems(t) for t in ("n1", "nc", "nx", "n2", "nf")]
        mod_done = sem("mod_done")

        def ffn_sems(tag):
            return {n: sem(f"{tag}_{n}") for n in ("silu", "gmul", "ghi", "glo", "bdone", "bfree")}

        fa, fb_ = ffn_sems("ffn1"), ffn_sems("ffn2")

        def chain_sems(tag, names):
            return {n: sem(f"{tag}_{n}") for n in names}

        cs = chain_sems("ctx", ("cur", "gate", "log", "v", "k", "init", "sum", "exp", "kd", "tpe", "tok", "st", "stout"))
        xs = chain_sems("hg", ("cur", "gate", "log", "v", "k", "init", "sum", "exp", "kq", "score", "pred",
                               "tpe", "tok", "ope", "osq", "mean", "root", "rstd", "on", "mix"))
        ys = chain_sems("hy", ("cur", "spec", "tab", "cb", "conv", "tpe", "ut", "specfree", "fft", "prod", "yf", "inv", "z"))
        msk_in = sem("msk_in")
        ms = chain_sems("wout", ("hi", "lo", "res"))
        fin = chain_sems("fin", ("o", "tr", "ev", "dma"))

        def load_unit(sy, un, j, src):
            n = un.number(j)
            if not (isinstance(n, int) and n < RING):
                sy.wait_ge(lo_done, n - RING + 1)
            a = src.shape[1]
            sy.dma_start(raw[un.slot(j)][:].rearrange("p (a c) -> p a c", a=a), src).then_inc(raw_in[un.slot(j)], 16)

        def col_src(w, kg, c0):
            return w[kg * 4 * P:(kg + 1) * 4 * P, bass.ds(c0, 256)].rearrange("(k p) c -> p k c", p=P)

        def row_src(w, chunk, q):
            return w[bass.ds(chunk * CHUNK, CHUNK), q * 512:(q + 1) * 512].rearrange("(f p) c -> p f c", p=P)

        def round_unit(ac, un, j):
            ac.wait_ge(raw_in[un.slot(j)], un.loads(j) * 16)
            ac.wait_ge(w_used, un.number(j) + 1)
            nc.scalar.activation(w_hi[un.slot(j)][:], raw[un.slot(j)][:], ACT.Copy).then_inc(hi_done, 1)

        def rest_unit(ve, un, j):
            ve.wait_ge(hi_done, un.number(j) + 1)
            nc.vector.tensor_tensor(w_lo[un.slot(j)][:], raw[un.slot(j)][:], w_hi[un.slot(j)][:].bitcast(F32),
                                    ALU.subtract).then_inc(lo_done, 1)

        def used(un, j):
            return un.number(j) + 1 + RING

        AHEAD = 2

        def three_pass(o, slot, c0, hi, lo, start, stop):
            nc.tensor.matmul(o, w_hi[slot][:, c0:c0 + P], hi, start=start, stop=False, skip_group_check=True)
            nc.tensor.matmul(o, w_hi[slot][:, c0:c0 + P], lo, start=False, stop=False, skip_group_check=True)
            return nc.tensor.matmul(o, w_lo[slot][:, c0:c0 + P], hi, start=False, stop=stop, skip_group_check=True)

        def col_unit(pe, un, j, kg, outs2, hi, lo, shared):
            pe.wait_ge(lo_done, un.number(j) + 1)
            for k in range(4):
                kb = 4 * kg + k
                for b in range(2):
                    last = three_pass(outs2[b], un.slot(j), k * 256 + b * P, hi(kb), lo(kb),
                                      kb == 0 and (b == 0 or not shared), kb == KB - 1)
            last.then_inc(w_used, 1)

        def norm_act(ac, s, src, ntok):
            for kb in range(KB):
                if kb >= 2:
                    ac.wait_ge(s["sum"], kb - 1)
                for t, part in enumerate(src):
                    ins = nc.scalar.activation(sq[kb % 2][:, t * 256:(t + 1) * 256], part[:, kb, :], ACT.Square)
                ins.then_inc(s["sq"], 1)
            ac.wait_ge(s["mean"], 1)
            nc.scalar.activation(root[:, 0:ntok], bank[7][:, 0:ntok], ACT.Sqrt, bias=EPS).then_inc(s["root"], 1)

        def norm_dve(ve, s, ntok):
            for kb in range(KB):
                ve.wait_ge(s["sq"], kb + 1)
                if kb == 0:
                    nc.vector.tensor_copy(sq_sum[:, 0:ntok], sq[0][:, 0:ntok]).then_inc(s["sum"], 1)
                else:
                    ve.wait_ge(s["sum"], kb)
                    nc.vector.tensor_tensor(sq_sum[:, 0:ntok], sq_sum[:, 0:ntok], sq[kb % 2][:, 0:ntok],
                                            ALU.add).then_inc(s["sum"], 1)
            ve.wait_ge(s["root"], 1)
            nc.vector.reciprocal(rstd[:, 0:ntok], root[:, 0:ntok]).then_inc(s["rstd"], 1)

        def norm_pe(pe, s, ntok):
            pe.wait_ge(s["sum"], KB)
            nc.tensor.matmul(bank[7][:, 0:ntok], ones_d[:], sq_sum[:, 0:ntok], start=True, stop=True).then_inc(s["mean"], 1)

        def modulate_dve(ve, s, which, src, lo, tcs):
            shift = (0, 3, 6)[which]
            ve.wait_ge(s["rstd"], 1)

            def scaled(kb):
                if kb >= 2:
                    ve.wait_ge(s["lo"], kb - 1)
                for t, part in enumerate(src):
                    ins = nc.vector.scalar_tensor_tensor(
                        out=xn[kb % 2][:, t * 256:(t + 1) * 256], in0=part[:, kb, :],
                        scalar=scale_a[:, which, kb, tcs[t]:tcs[t] + 1], in1=rstd[:, t * 256:(t + 1) * 256],
                        op0=ALU.mult, op1=ALU.mult)
                ins.then_inc(s["xn"], 1)

            scaled(0)
            for kb in range(KB):
                if kb + 1 < KB:
                    scaled(kb + 1)
                ve.wait_ge(s["hi"], kb + 1)
                for t in range(len(src)):
                    ins = nc.vector.scalar_tensor_tensor(
                        out=lo(t, kb), in0=xn[kb % 2][:, t * 256:(t + 1) * 256],
                        scalar=mods[:, shift, kb, tcs[t]:tcs[t] + 1], in1=s["hi_ap"](t, kb).bitcast(F32),
                        op0=ALU.add, op1=ALU.subtract)
                ins.then_inc(s["lo"], 1)

        def modulate_act(ac, s, which, hi, tcs):
            shift = (0, 3, 6)[which]
            for kb in range(KB):
                ac.wait_ge(s["xn"], kb + 1)
                for t in range(len(tcs)):
                    ins = nc.scalar.activation(hi(t, kb), xn[kb % 2][:, t * 256:(t + 1) * 256], ACT.Identity,
                                               bias=mods[:, shift, kb, tcs[t]:tcs[t] + 1])
                ins.then_inc(s["hi"], 1)

        n1["hi_ap"] = lambda t, kb: h1_hi[:, t, kb, :]
        nctx["hi_ap"] = lambda t, kb: hc_hi[:, kb, :]
        nx["hi_ap"] = lambda t, kb: hx_hi[:, kb, :]
        n2["hi_ap"] = lambda t, kb: h2_hi[:, kb, :]

        def ffn_loops(eng, base, body, loops, before=lambda ada: None):
            start = 0
            for count, ada in loops:
                before(ada)
                with eng.Fori(0, count) as it:
                    body(Units(base + 8 + 12 * start, it, 12), it + start if start else it, ada, it)
                start += count

        F1_LOOPS = ((ADA_BOTH, 2), (ADA_LATENT, 1), (N_CHUNK - 1 - ADA_BOTH - ADA_LATENT, 0))
        F2_LOOPS = ((N_CHUNK - 1, 0),)

        def ffn_sync(sy, base, w1, w3, w2, loops):
            un = Units(base)
            for j in range(8):
                load_unit(sy, un, j, col_src(w1 if j < 4 else w3, j % 4, 0))

            def body(un, c, ada, it):
                for j in range(12):
                    if j < 8:
                        load_unit(sy, un, j, col_src(w1 if j < 4 else w3, j % 4, (c + 1) * CHUNK))
                    else:
                        load_unit(sy, un, j, row_src(w2, c, j - 8))
                    for m in ada_at(j - 3) if ada else ():
                        sy.wait_ge(ada_x, c * KB + (RING + ADA_FIRST_H * ADA_EW + m - 3))
                        if ada == 2:
                            sy.wait_ge(ada_c, c * KB + (RING + ADA_FIRST_H * ADA_EW + m - 3))
                        load_ada(sy, m, c + ADA_FIRST_H)

            def before(ada):
                if ada == 1:
                    sy.wait_ge(ada_c, RING + ADA_FIRST_H * ADA_EW + ADA_BOTH * KB)

            if len(loops) > 1:
                sy.wait_ge(ada_pe, 1 + ADA_FIRST_H)
            ffn_loops(sy, base, body, loops, before)
            un = Units(base + 8 + 12 * (N_CHUNK - 1))
            for j in range(4):
                load_unit(sy, un, j, row_src(w2, N_CHUNK - 1, j))

        ada_w = i["ada_w"][0]

        def ada_at(j):
            return range(2 * j, 2 * j + 2) if 0 <= j < 8 else ()

        def load_ada(sy, m, half):
            sy.dma_start(ada_raw[m % RING][:], ada_w[m % KB * P:(m % KB + 1) * P, bass.ds(half * HALF, HALF)]
                         ).then_inc(ada_in[m % RING], 16)

        def ada_landed(eng, m, first, it, per):
            eng.wait_ge(ada_in[m % RING], (it * (per // RING) + ((first + m) // RING + 1)) * 16)

        def ew_before(m):
            return sum(n % KB not in ADA_PE for n in range(m))

        def pe_before(m):
            return m - ew_before(m)

        def first_slot_free(sy, m, it):
            last = m - RING
            wrap = ADA_BODY if last < 0 else 0
            if (last + wrap) % KB in ADA_PE:
                value = pe_before(last + wrap + 1) - (pe_before(ADA_BODY) if wrap else 0)
                sy.wait_ge(ada_used, it * pe_before(ADA_BODY) + (RING + value))
            else:
                value = ew_before(last + wrap + 1) - (ew_before(ADA_BODY) if wrap else 0)
                sy.wait_ge(ada_x, it * ew_before(ADA_BODY) + (RING + value))
                sy.wait_ge(ada_c, it * ew_before(ADA_BODY) + (RING + value))

        def first_units(ms):
            return [m for m in ms if m % KB not in ADA_PE]

        def ada_vector(ve, m, x_done, half):
            kb = m % KB
            if kb == 0:
                ve.wait_ge(ada_pe, half + 1)
                nc.vector.tensor_scalar(ada_sum[0], ada_raw[m % RING][:], silu_c[:, kb, 0:1], None, ALU.mult
                                        ).then_inc(ada_x, 1)
            else:
                ve.wait_ge(ada_x, x_done)
                nc.vector.scalar_tensor_tensor(out=ada_sum[0], in0=ada_raw[m % RING][:], scalar=silu_c[:, kb, 0:1],
                                               in1=ada_sum[0], op0=ALU.mult, op1=ALU.add).then_inc(ada_x, 1)

        def ada_scalar(ac, m, n, added, half):
            kb = m % KB
            if kb == 0:
                ac.wait_ge(ada_pe, half + 1)
                dst = ada_sum[1]
            else:
                ac.wait_ge(ada_add, added)
                dst = ada_prod[n % 2][:]
            nc.scalar.activation(dst, ada_raw[m % RING][:], ACT.Copy, scale=silu_c[:, kb, 1:2]).then_inc(ada_c, 1)

        def ada_gpsimd(po, n, c_done, added):
            po.wait_ge(ada_c, c_done)
            po.wait_ge(ada_add, added)
            nc.gpsimd.tensor_tensor(ada_sum[1], ada_sum[1], ada_prod[n % 2][:], ALU.add).then_inc(ada_add, 1)

        def ada_total(pe, to, streams, fresh):
            for b in range(HALF // P):
                for t in range(streams):
                    ins = nc.tensor.matmul(bank[to][:, 2 * b + t:2 * b + t + 1], ada_sum[t][:, b * P:(b + 1) * P],
                                           ones_1[:, 0:1], start=fresh and b == 0 and t == 0, stop=True,
                                           skip_group_check=True)
            ins.then_inc(ada_pe, 1)

        mods_flat = mods[:].rearrange("p m k t -> p (m k) t")

        def ada_take(ve, half, to, streams):
            ve.wait_ge(ada_pe, half + 2)
            nc.vector.tensor_copy(mods_flat[:, bass.ds(half * 8, 8), 0:streams],
                                  bank[to][:, 0:16].rearrange("p (b t) -> p b t", t=2)[:, :, 0:streams]).then_inc(ada_out, 1)

        DOWN = {512: (4, 5, 6), 256: (4, 5, 6, 7)}

        def up_bank(b, ntok):
            return bank[b][:, 0:ntok] if ntok == 512 else bank[b // 2][:, b % 2 * 256:(b % 2 + 1) * 256]

        def ffn_pe(pe, s, base, hi, lo, g_hi, g_lo, ntok, loops):
            downs = DOWN[ntok]

            def out(b):
                return up_bank(b, ntok)

            def up(un, j, c):
                if c is not None and j in (0, 4):
                    pe.wait_ge(s["silu"] if j == 0 else s["gmul"], c * 2 + 2)
                b0 = 0 if j < 4 else 2
                col_unit(pe, un, j, j % 4, [out(b0), out(b0 + 1)], hi, lo, ntok == 256)

            def down(un, j, jj, c):
                if jj == 0:
                    pe.wait_ge(s["glo"], c * 2 + 2)
                pe.wait_ge(lo_done, un.number(j) + 1)
                for q in range(4):
                    d = 4 * jj + q
                    before = d - len(downs) if d >= len(downs) else 15 - (15 - d) % len(downs) - KB
                    pe.wait_ge(s["bfree"], c * KB + (before + 1 + KB))
                    for f in range(2):
                        last = three_pass(bank[downs[d % len(downs)]][:, 0:ntok], un.slot(j), f * 512 + q * P,
                                          g_hi[f][:], g_lo[f][:], f == 0, f == 1)
                    if q < 3:
                        last.then_inc(s["bdone"], 1)
                    else:
                        last.then_inc(w_used, 1)

            un = Units(base)
            for j in range(8):
                up(un, j, None)

            def body(un, c, ada, it):
                for j in range(12):
                    if j < 8:
                        up(un, j, c)
                    else:
                        down(un, j, j - 8, c)
                    if ada and j == 10:
                        pe.wait_ge(ada_x, c * KB + (RING + ADA_FIRST_H * ADA_EW + KB))
                        if ada == 2:
                            pe.wait_ge(ada_add, c * (KB - 1) + (1 + ADA_FIRST_H * (ADA_EW - 1) + KB - 1))
                        pe.wait_ge(ada_out, c + (ADA_FIRST_H + 1))
                        ada_total(pe, 7, ada, True)

            ffn_loops(pe, base, body, loops)
            un = Units(base + 8 + 12 * (N_CHUNK - 1))
            for j in range(4):
                down(un, j, j, N_CHUNK - 1)

        def ffn_act(ac, s, base, sil, g, g_hi, ntok, loops):
            def silu(un, j, c):
                ac.wait_ge(w_used, used(un, j))
                for b in range(2):
                    if not (isinstance(c, int) and c == 0):
                        ac.wait_ge(s["gmul"], c * 2 + (b + 1 - 2))
                    nc.scalar.activation(sil[b][:], up_bank(b, ntok), ACT.Silu).then_inc(s["silu"], 1)

            def ghi(c):
                for b in range(2):
                    ac.wait_ge(s["gmul"], c * 2 + (b + 1))
                    nc.scalar.activation(g_hi[b][:], g[b][:], ACT.Copy).then_inc(s["ghi"], 1)

            un = Units(base)
            for j in range(8):
                round_unit(ac, un, j + AHEAD)
                if j == 3:
                    silu(un, j, 0)
            ghi(0)

            def body(un, c, ada, it):
                for j in range(12):
                    round_unit(ac, un, j + AHEAD)
                    for m in ada_at(j) if ada == 2 else ():
                        ada_landed(ac, m, ADA_FIRST_H * KB, c, KB)
                        added = 0 if m <= 1 else m - 2
                        ada_scalar(ac, m, m - 1, c * (KB - 1) + (1 + ADA_FIRST_H * (ADA_EW - 1) + added), c + ADA_FIRST_H)
                    if j == 3:
                        silu(un, j, c + 1)
                    if j == 11:
                        ac.wait_ge(w_used, used(un, j))
                        ghi(c + 1)

            ffn_loops(ac, base, body, loops)
            un = Units(base + 8 + 12 * (N_CHUNK - 1))
            for j in range(4):
                if un.number(j + AHEAD) < U_END:
                    round_unit(ac, un, j + AHEAD)

        def ffn_dve(ve, s, base, sil, g, g_hi, g_lo, ntok, res, gt, loops):
            ve.sem_inc(s["bfree"], KB)
            downs = DOWN[ntok]

            def gmul(un, j, c):
                ve.wait_ge(w_used, used(un, j))
                for b in range(2):
                    ve.wait_ge(s["silu"], c * 2 + (b + 1))
                    nc.vector.tensor_tensor(g[b][:], sil[b][:], up_bank(2 + b, ntok), ALU.mult).then_inc(s["gmul"], 1)

            def glo(c):
                for b in range(2):
                    ve.wait_ge(s["ghi"], c * 2 + (b + 1))
                    nc.vector.tensor_tensor(g_lo[b][:], g[b][:], g_hi[b][:].bitcast(F32), ALU.subtract).then_inc(s["glo"], 1)

            def add(un, j, jj, c):
                if jj == 0:
                    ve.wait_ge(s["bfree"], c * KB + KB)
                for q in range(4):
                    d = 4 * jj + q
                    if q < 3:
                        ve.wait_ge(s["bdone"], c * 12 + (3 * jj + q + 1))
                    else:
                        ve.wait_ge(w_used, used(un, j))
                    for t, part in enumerate(res):
                        ins = nc.vector.scalar_tensor_tensor(
                            out=part[:, d, :], in0=bank[downs[d % len(downs)]][:, t * 256:(t + 1) * 256],
                            scalar=gate[:, gt, d, t:t + 1], in1=part[:, d, :], op0=ALU.mult, op1=ALU.add)
                    ins.then_inc(s["bfree"], 1)

            un = Units(base)
            for j in range(8):
                rest_unit(ve, un, j + AHEAD)
            gmul(un, 7, 0)
            glo(0)

            def body(un, c, ada, it):
                for j in range(12):
                    rest_unit(ve, un, j + AHEAD)
                    if j == 7:
                        gmul(un, j, c + 1)
                    if j >= 8:
                        add(un, j, j - 8, c)
                    for m in ada_at(j) if ada else ():
                        ada_landed(ve, m, ADA_FIRST_H * KB, c, KB)
                        ada_vector(ve, m, c * KB + (RING + ADA_FIRST_H * ADA_EW + m), c + ADA_FIRST_H)
                if ada:
                    ada_take(ve, c + ADA_FIRST_H, 7, ada)
                glo(c + 1)

            ffn_loops(ve, base, body, loops)
            un = Units(base + 8 + 12 * (N_CHUNK - 1))
            for j in range(4):
                if un.number(j + AHEAD) < U_END:
                    rest_unit(ve, un, j + AHEAD)
                add(un, j, j, N_CHUNK - 1)

        def as_rows(ap, n):
            return ap.rearrange("(n p) -> n p", p=P) if len(ap.shape) == 1 else ap

        ROWS = [
            (0, 0, 128, i["ada_b"][0, 0:128 * P]),
            (1, 0, 16, i["ada_b"][0, 128 * P:144 * P]),
            (1, 16, 16, i["norm_ffn1"][0]), (1, 32, 16, i["norm_mix"][0]), (1, 48, 16, i["norm_ffn2"][0]),
            (1, 64, 16, i["final_norm"]), (1, 80, 8, i["hg_norm"][0]),
            (1, 88, 8, i["hg_lb_logits"][0, 0]), (1, 96, 8, i["hg_lb_logits"][0, 1]),
            (1, 104, 8, i["hg_lb_logits"][1, 0]), (1, 112, 8, i["hg_lb_logits"][1, 1]),
            (2, 0, 24, i["hy_conv_w"][0, 0]), (2, 24, 24, i["hy_conv_w"][0, 1]), (2, 48, 24, i["hy_conv_w"][0, 2]),
            (2, 72, 24, i["hy_conv_b"][0]), (2, 96, 16, i["c"][0]), (2, 112, 16, i["c_ctx"]),
        ]
        N_COLS = (128, 120, 128)
        C_GAIN = {0: 16, 1: 32, 2: 48}
        w_in = i["w_in"][0]
        HG_COLS = (0, HG, 2 * HG, 3 * HG, 4 * HG)
        HY_COLS = (5 * HG, 5 * HG + HY, 5 * HG + 2 * HY)

        block = life.enter_context(nc.Block())

        @block.sync
        def _(sy):
            for tile, r, n, src in ROWS:
                sy.dma_start(rows[tile][r:r + n, :], as_rows(src, n)).then_inc(small_in, 16)
            sy.dma_start(ident[:], i["t_ident"]).then_inc(small_in, 16)
            sy.dma_start(emb[:], i["t_emb"]).then_inc(small_in, 16)
            sy.dma_start(fw1[:], i["filt_w1"][0]).then_inc(small_in, 16)
            sy.dma_start(fw23[:, 0, :], i["filt_w2"][0]).then_inc(small_in, 16)
            sy.dma_start(fw23[:, 1, :], i["filt_w3"][0]).then_inc(small_in, 16)
            for n, name in enumerate(("filt_b1", "filt_b2", "filt_b3", "filt_freq")):
                sy.dma_start(fbias[:, n:n + 1], i[name][0].rearrange("(p a) -> p a", a=1)).then_inc(small_in, 16)
            sy.dma_start(dft[:], i["t_dft"]).then_inc(tab_in, 16)
            sy.dma_start(window[:].rearrange("p a c -> p (a c)"), i["t_window"]).then_inc(tab_in, 16)
            sy.dma_start(xin[:], i["x"][0].rearrange("(a p) d -> p a d", p=P)).then_inc(x_in, 16)
            sy.dma_start(yin[:], i["ctx"][0].rearrange("(a p) d -> p a d", p=P)).then_inc(y_in, 16)
            with sy.Fori(0, 2) as filt:
                for half in range(2):
                    sy.wait_ge(fs_taps_pe, filt * 8 + (half * 4 + 4))
                    for r in range(2):
                        sy.dma_start(fout[:, r, :],
                                     i["filt_w_out"][0][:, bass.ds(filt * (2 * HY) + (r * HY + half * 512), 512)]
                                     ).then_inc(fs_in, 16)
                    sy.wait_ge(fs_norm, filt * 2 + (half + 1))
                    sy.dma_start(hyd_row[:], i["hy_d"][0][bass.ds(filt, 1), half * 512:(half + 1) * 512]
                                 ).then_inc(fs_hyd, 16)
                    for m in range(24 * half, 24 * half + 24):
                        first_slot_free(sy, m, filt)
                        load_ada(sy, m, filt * 3 + m // KB)

            ffn_sync(sy, U_FFN1, i["ffn1_w1"][0], i["ffn1_w3"][0], i["ffn1_w2"][0], F1_LOOPS)
            with sy.Fori(0, PAIRS) as it:
                un = Units(U_CTX, it, 12)
                for j in range(12):
                    load_unit(sy, un, j, col_src(w_in, j % 4, it * 256 + HG_COLS[j // 4]))
            with sy.Fori(0, PAIRS) as it:
                un = Units(U_HG, it, 20)
                for j in range(20):
                    load_unit(sy, un, j, col_src(w_in, j % 4, it * 256 + HG_COLS[j // 4]))
            with sy.Fori(0, PAIRS) as it:
                un = Units(U_HY, it, 12)
                for j in range(12):
                    load_unit(sy, un, j, col_src(w_in, j % 4, it * 256 + HY_COLS[j // 4]))
            with sy.Fori(0, KB // 4) as it:
                un = Units(U_OUT, it, 8)
                for j in range(8):
                    load_unit(sy, un, j, col_src(i["w_out"][0], j % 4, it * 512 + j // 4 * 256))
            ffn_sync(sy, U_FFN2, i["ffn2_w1"][0], i["ffn2_w3"][0], i["ffn2_w2"][0], F2_LOOPS)
            for a in range(TB):
                sy.wait_ge(fin["ev"], 4 * (a + 1))
                sy.dma_start(out[0, a * P:(a + 1) * P, :], xt[:, a, :]).then_inc(fin["dma"], 16)
            sy.wait_ge(fin["dma"], 16 * TB)

        def halves(ap, m):
            return ap.rearrange("p h (n s m) -> p (h n) s m", s=2, m=m)

        @block.gpsimd
        def _(po):
            nc.gpsimd.memset(ones_d[:], 1.0 / D).then_inc(memsets, 1)
            nc.gpsimd.memset(ones_h[:], 1.0 / DK).then_inc(memsets, 1)
            nc.gpsimd.memset(ones_1[:], 1.0).then_inc(memsets, 1)

            po.sem_inc(ada_add, 1)
            with po.Fori(0, 2) as filt:
                for m in first_units(range(ADA_BODY)):
                    if m % KB:
                        n = ew_before(m) - (m // KB + 1)
                        ada_gpsimd(po, n, filt * (3 * ADA_EW) + (RING + ew_before(m) + 1),
                                   filt * (3 * (ADA_EW - 1)) + (1 + n))
            with po.Fori(0, ADA_BOTH) as it:
                for m in range(1, KB):
                    ada_gpsimd(po, m - 1, it * KB + (RING + ADA_FIRST_H * ADA_EW + m + 1),
                               it * (KB - 1) + (1 + ADA_FIRST_H * (ADA_EW - 1) + m - 1))

            with po.Fori(0, PAIRS) as it:
                po.wait_ge(cs["log"], it * 2 + 2)
                po.wait_ge(cs["init"], it + 1)
                total = cg[:].rearrange("p d h t -> p d (h t)")
                for lv in range(LEVELS):
                    m = 1 << lv
                    if lv:
                        po.wait_ge(cs["sum"], it * 24 + 3 * lv)
                    pair = total.rearrange("p d (n s) -> p d n s", s=2)
                    behind, before = halves(csum[:, 0], m)[:, :, 0, :], halves(csum[:, 1], m)[:, :, 1, :]
                    shape = list(behind.shape)
                    nc.gpsimd.tensor_tensor(behind, behind, pair[:, 0, :, 1:2].to_broadcast(shape), ALU.add
                                            ).then_inc(cs["sum"], 1)
                    nc.gpsimd.tensor_tensor(before, before, pair[:, 1, :, 0:1].to_broadcast(shape), ALU.add
                                            ).then_inc(cs["sum"], 1)
                    nxt = ctot[lv % 2][:].rearrange("p d h t -> p d (h t)")[:, :, 0:SEQ // m]
                    nc.gpsimd.tensor_tensor(nxt, pair[:, :, :, 0], pair[:, :, :, 1], ALU.add).then_inc(cs["sum"], 1)
                    total = nxt
                po.wait_ge(cs["exp"], it + 1)
                po.wait_ge(cs["k"], it * 2 + 2)
                nc.gpsimd.tensor_tensor(ckd[:], ck[:], cexp[:], ALU.mult).then_inc(cs["kd"], 1)

            po.wait_ge(nx["lo"], KB)
            po.dma_start(mask[:].rearrange("p a c -> p (a c)"), i["t_mask"]).then_inc(msk_in, 16)
            with po.Fori(0, PAIRS) as it:
                po.wait_ge(xs["init"], it + 1)
                po.wait_ge(xs["log"], it * 2 + 2)
                for lv in range(LEVELS):
                    m = 1 << lv
                    po.wait_ge(xs["exp"], it * 9 + (lv + 1))
                    if lv:
                        po.wait_ge(xs["sum"], it * 32 + 4 * lv)
                    upto, fromon = halves(xa[:, 0], m), halves(xa[:, 1], m)
                    behind, before = halves(xe[:, 0], m), halves(xe[:, 1], m)
                    shape = [P, SEQ // m, m]
                    for dst, side, tot in ((behind, 0, upto[:, :, 1, m - 1:m]), (upto, 1, upto[:, :, 0, m - 1:m]),
                                           (before, 1, fromon[:, :, 0, 0:1]), (fromon, 0, fromon[:, :, 1, 0:1])):
                        if dst is upto:
                            po.wait_ge(xs["sum"], it * 32 + (4 * lv + 1))
                        if dst is fromon:
                            po.wait_ge(xs["sum"], it * 32 + (4 * lv + 3))
                        nc.gpsimd.tensor_tensor(dst[:, :, side, :], dst[:, :, side, :], tot.to_broadcast(shape),
                                                ALU.add).then_inc(xs["sum"], 1)

            po.wait_ge(xs["mix"], 1 + PAIRS)
            po.dma_start(dfty[:], i["t_dft"]).then_inc(ys["tab"], 16)
            with po.Fori(0, PAIRS) as it:
                po.wait_ge(ys["specfree"], it + 1)
                for f in range(2):
                    po.dma_start(spec[:, f, :, :, :].rearrange("p a b c -> p (a b) c"),
                                 spec_dram[f][:, :, bass.ds(it * 256, 256)]).then_inc(ys["spec"], 16)

        SMALL = 16 * (len(ROWS) + 9)

        @block.tensor
        def _(pe):
            pe.sem_inc(w_used, RING)
            pe.sem_inc(ada_used, RING)
            pe.sem_inc(ada_pe, 1)
            pe.sem_inc(fs_taps_pe, 4)
            pe.sem_inc(fs_spec, 5)
            pe.wait_ge(small_in, SMALL)
            for n in range(3):
                nc.tensor.transpose(bank[n][:, 0:N_COLS[n]], rows[n][0:N_COLS[n], :],
                                    ident[0:N_COLS[n], 0:N_COLS[n]]).then_inc(rows_t, 1)
            pe.wait_ge(cols_done, 3)
            for n in range(3):
                if n:
                    pe.wait_ge(fm_sin, n)
                nc.tensor.matmul(bank[0][0:FILT_ORDER, 0:SEQ], fw1[:] if n == 0 else fw23[:, n - 1, :],
                                 emb[:] if n == 0 else hid[n - 1][:], start=True, stop=True).then_inc(fm_pe, 1)
            pe.wait_ge(fm_dve, 18)
            for g in range(16):
                src = xin if g < 8 else yin
                pe.wait_ge(x_in if g < 8 else y_in, 16)
                if g >= 4:
                    pe.wait_ge(tr_out, g - 3)
                for k in range(2):
                    for a in range(TB):
                        kb = 2 * (g % 8) + k
                        ins = nc.tensor.transpose(bank[g % 4][:, k * 256 + a * P:k * 256 + (a + 1) * P],
                                                  src[:, a, kb * P:(kb + 1) * P], ident[:])
                ins.then_inc(tr_done, 1)
            pe.wait_ge(memsets, 3)
            norm_pe(pe, n1, 512)
            pe.wait_ge(silu_done, 1)
            pe.wait_ge(fm_sin, 3)
            pe.wait_ge(tab_in, 32)
            pe.wait_ge(n1["root"], 1)
            with pe.Fori(0, 2) as filt:
                for half in range(2):
                    def units(*ms):
                        for m in ms:
                            if m % KB == ADA_PE[0]:
                                pe.wait_ge(ada_out, filt * 3 + (m // KB + 1))
                            ada_landed(pe, m, 0, filt, ADA_BODY)
                            for b in range(HALF // P):
                                ins = nc.tensor.matmul(bank[6][:, 2 * b:2 * b + 2], ada_raw[m % RING][:, b * P:(b + 1) * P],
                                                       silu_c[:, m % KB, :], start=(m % KB == ADA_PE[0] and b == 0),
                                                       stop=False, skip_group_check=True)
                            ins.then_inc(ada_used, 1)

                    def total(h):
                        pe.wait_ge(ada_x, filt * (3 * ADA_EW) + (RING + (h + 1) * ADA_EW))
                        pe.wait_ge(ada_add, filt * (3 * (ADA_EW - 1)) + (1 + (h + 1) * (ADA_EW - 1)))
                        ada_total(pe, 6, 2, False)

                    def spectra(o, tab, part):
                        pe.wait_ge(fs_out, filt * 10 + (half * 5 + o + 1))
                        for a in range(TB):
                            step = 256 if tab != T_COSN else P
                            ins = nc.tensor.matmul(bank[5 if (half * 5 + o) % 2 else 7][:],
                                                   dft[:, tab + a * step:tab + a * step + P], part[:, a, :],
                                                   start=(a == 0), stop=(a == 1))
                        ins.then_inc(fs_spec, 1)

                    if half:
                        units(25)
                    pe.wait_ge(fs_in, filt * 64 + (half * 32 + 32))
                    pe.wait_ge(fs_taps, filt * 8 + (half * 4 + 4))
                    for a in range(TB):
                        for r in range(2):
                            nc.tensor.matmul(bank[2 * a + r][:], hid[2][:, a * P:(a + 1) * P], fout[:, r, :],
                                             start=True, stop=True).then_inc(fs_taps_pe, 1)
                    units(*((28, 31) if half else (3,)))
                    if half:
                        total(1)
                    pe.wait_ge(fs_abs, filt * 2 + (half + 1))
                    for n in range(4):
                        ins = nc.tensor.matmul(bank[4][:], ones_1[:], tabs[:, n // 2, n % 2, :], start=(n == 0), stop=(n == 3))
                    ins.then_inc(fs_l1, 1)
                    units(*((35, 38) if half else (6, 9)))
                    pe.wait_ge(fs_norm, filt * 2 + (half + 2))
                    spectra(0, T_COS, tsum)
                    spectra(1, T_COS + P, tsum)
                    spectra(2, T_SIN, tdif)
                    units(41 if half else 12)
                    spectra(3, T_SIN + P, tdif)
                    spectra(4, T_COSN, tsum)
                    units(*((44, 47) if half else (15,)))
                    total(2 if half else 0)
                    if not half:
                        units(19, 22)

            pe.wait_ge(fs_taps, 20)
            pe.wait_ge(fs_out, 22)
            pe.wait_ge(n1["lo"], KB)
            ffn_pe(pe, fa, U_FFN1, lambda k: h1_hi[:, :, k, :], lambda k: h1_lo[:, :, k, :], g1_hi, g1_lo, 512, F1_LOOPS)

            norm_pe(pe, nctx, 256)
            pe.wait_ge(nctx["lo"], KB)
            with pe.Fori(0, PAIRS) as it:
                un = Units(U_CTX, it, 12)
                pe.wait_ge(cs["stout"], it + 1)
                for j in range(12):
                    col_unit(pe, un, j, j % 4, [bank[j // 4][:, 0:256], bank[j // 4][:, 256:512]],
                             lambda k: hc_hi[:, k, :], lambda k: hc_lo[:, k, :], True)
                for n in range(3):
                    pe.wait_ge(cs["kd"], it + 1)
                    pe.wait_ge(cs["v"], it + 1)
                    for h in range(2):
                        for a in range(TB):
                            src = cv[:, h, a * P:(a + 1) * P] if n == 2 else ckd[:, n, h, a * P:(a + 1) * P]
                            ins = nc.tensor.transpose(bank[3 + n][:, (2 * h + a) * P:(2 * h + a + 1) * P], src, ident[:])
                    ins.then_inc(cs["tpe"], 1)
                pe.wait_ge(cs["tok"], it * 3 + 3)
                for d in range(2):
                    for h in range(2):
                        for a in range(TB):
                            ins = nc.tensor.matmul(bank[6][:, (2 * d + h) * P:(2 * d + h + 1) * P],
                                                   ctok[:, d, 2 * h + a, :], ctok[:, 2, 2 * h + a, :],
                                                   start=(a == 0), stop=(a == 1))
                ins.then_inc(cs["st"], 1)

            norm_pe(pe, nx, 256)
            pe.wait_ge(nx["lo"], KB)
            with pe.Fori(0, PAIRS) as it:
                un = Units(U_HG, it, 20)
                pe.wait_ge(xs["mix"], it + 1)
                for j in range(20):
                    col_unit(pe, un, j, j % 4, [bank[j // 4][:, 0:256], bank[j // 4][:, 256:512]],
                             lambda k: hx_hi[:, k, :], lambda k: hx_lo[:, k, :], True)
                pe.wait_ge(xs["v"], it * 3 + 1)
                for h in range(2):
                    for a in range(TB):
                        ins = nc.tensor.transpose(bank[7][:, (2 * h + a) * P:(2 * h + a + 1) * P],
                                                  xv[:, h, a * P:(a + 1) * P], ident[:])
                ins.then_inc(xs["tpe"], 1)
                for s in range(LEVELS + 1):
                    pe.wait_ge(xs["kq"], it * 10 + (s + 1))
                    pe.wait_ge(xs["pred"], it * 9 + (s - 1) + 2)
                    for h in range(2):
                        for a in range(TB):
                            b = a if s < LEVELS else 1 - a
                            ins = nc.tensor.matmul(bank[5 + s % 2][:, (2 * h + a) * P:(2 * h + a + 1) * P],
                                                   lk[s % 2][:, h, a * P:(a + 1) * P], lq[s % 2][:, h, b * P:(b + 1) * P],
                                                   start=True, stop=True)
                    ins.then_inc(xs["score"], 1)
                pe.wait_ge(xs["pred"], it * 9 + 11)
                pe.wait_ge(xs["tok"], it + 1)
                pe.wait_ge(xs["kq"], it * 10 + 10)
                pe.wait_ge(xs["cur"], it + 1)
                pe.wait_ge(xs["v"], it * 3 + 2)
                for h in range(2):
                    for a in range(TB):
                        o = bank[3][:, h * 256 + a * P:h * 256 + (a + 1) * P]
                        b = 2 * h + a
                        other = 2 * h + 1 - a
                        nc.tensor.matmul(o, vtok[:, b, :], prob[:, b, :], start=True, stop=False)
                        nc.tensor.matmul(o, vtok[:, other, :], cross[:, other, :], start=False, stop=False)
                        nc.tensor.matmul(o, s_cur[:, h, :], lq[1][:, h, a * P:(a + 1) * P], start=False, stop=False)
                        ins = nc.tensor.matmul(o, s_cur[:, 2 + h, :], lk[1][:, h, a * P:(a + 1) * P], start=False, stop=True)
                ins.then_inc(xs["ope"], 1)
                pe.wait_ge(xs["osq"], it + 1)
                pe.wait_ge(xs["v"], it * 3 + 3)
                nc.tensor.matmul(bank[4][:], ones_h[:], osq[:], start=True, stop=True).then_inc(xs["mean"], 1)

            pe.wait_ge(ys["tab"], 16)
            with pe.Fori(0, PAIRS) as it:
                un = Units(U_HY, it, 12)
                pe.wait_ge(ys["z"], it * 2 + 2)
                for j in range(12):
                    col_unit(pe, un, j, j % 4, [bank[j // 4][:, 0:256], bank[j // 4][:, 256:512]],
                             lambda k: hx_hi[:, k, :], lambda k: hx_lo[:, k, :], True)
                for f in range(2):
                    if f == 0:
                        pe.wait_ge(ys["conv"], it * 12 + 4)
                    else:
                        pe.wait_ge(ys["z"], it * 2 + 3)
                    for a in range(TB):
                        for b in range(2):
                            src = conv[:, 0, b, a * P:(a + 1) * P] if f == 0 else zg[:, b, a * P:(a + 1) * P]
                            ins = nc.tensor.transpose(bank[3][:, a * 256 + b * P:a * 256 + (b + 1) * P], src, ident[:])
                    ins.then_inc(ys["tpe"], 1)
                    pe.wait_ge(ys["ut"], it * 2 + (f + 1))
                    for ri, tab in enumerate((T_COS, T_SINN)):
                        for b in range(2):
                            for a in range(TB):
                                ins = nc.tensor.matmul(bank[4 + ri][:, b * 256:(b + 1) * 256],
                                                       dfty[:, tab + a * 256 + b * P:tab + a * 256 + (b + 1) * P],
                                                       ut[:, a, :], start=(a == 0), stop=(a == 1))
                    ins.then_inc(ys["fft"], 1)
                    pe.wait_ge(ys["yf"], it * 4 + (2 * f + 2))
                    for b in range(2):
                        for n, (ri, fb) in enumerate(((0, 0), (0, 1), (1, 0), (1, 1))):
                            tab = (T_ITR, T_ITI)[ri] + fb * 256
                            ins = nc.tensor.matmul(bank[6][:, b * 256:(b + 1) * 256], yf[:, ri, fb, b * P:(b + 1) * P],
                                                   dfty[:, tab:tab + 256], start=(n == 0), stop=(n == 3))
                    ins.then_inc(ys["inv"], 1)

            pe.wait_ge(ms["lo"], 4)
            with pe.Fori(0, KB // 4) as it:
                un = Units(U_OUT, it, 8)
                for j in range(8):
                    if j % 4 == 0:
                        pe.wait_ge(ms["res"], it * 2 + (j // 4 + 1))
                    col_unit(pe, un, j, j % 4, [bank[j // 4][:, 0:256], bank[j // 4][:, 256:512]],
                             lambda k: m_hi[:, k, :], lambda k: m_lo[:, k, :], True)

            norm_pe(pe, n2, 256)
            pe.wait_ge(n2["lo"], KB)
            ffn_pe(pe, fb_, U_FFN2, lambda k: h2_hi[:, k, :], lambda k: h2_lo[:, k, :], g2_hi, g2_lo, 256, F2_LOOPS)
            norm_pe(pe, nf, 256)
            for g in range(8):
                a, q = g // 4, g % 4
                pe.wait_ge(fin["o"], KB)
                if g >= 4:
                    pe.wait_ge(fin["ev"], g - 3)
                for k in range(4):
                    ins = nc.tensor.transpose(bank[g % 4][:, k * P:(k + 1) * P], xo[:, 4 * q + k, a * P:(a + 1) * P], ident[:])
                ins.then_inc(fin["tr"], 1)

        @block.scalar
        def _(ac):
            ac.sem_inc(cs["stout"], 1)
            ac.sem_inc(fs_out, 2)
            ac.sem_inc(ada_c, RING)
            ac.wait_ge(cols_done, 3)
            nc.scalar.activation(silu_c[:, :, 0], cols[2][:, 96:112], ACT.Silu)
            nc.scalar.activation(silu_c[:, :, 1], cols[2][:, 112:128], ACT.Silu).then_inc(silu_done, 1)
            ac.wait_ge(lb_dve, 3)
            nc.scalar.activation(lbe[:], lbe[:], ACT.Exp).then_inc(lb_act, 1)
            for n in range(3):
                ac.wait_ge(fm_dve, 6 * (n + 1))
                nc.scalar.activation(hid[n][:], ang[n % 2][:], ACT.Sin).then_inc(fm_sin, 1)
            for g in range(16):
                ac.wait_ge(tr_done, g + 1)
                dst = x_res if g < 8 else y_res
                nc.scalar.activation(dst[:, 2 * (g % 8):2 * (g % 8) + 2, :].rearrange("p a c -> p (a c)"),
                                     bank[g % 4][:], ACT.Copy).then_inc(tr_out, 1)
            ac.wait_ge(tr_out, 16)
            norm_act(ac, n1, [x_res, y_res], 512)
            with ac.Fori(0, 2) as filt:
                for half in range(2):
                    def products(first, end):
                        for m in first_units(range(first, end)):
                            ada_landed(ac, m, 0, filt, ADA_BODY)
                            n = ew_before(m) - (m // KB + 1)
                            ada_scalar(ac, m, n, filt * (3 * (ADA_EW - 1)) + (1 + max(n - 1, 0)), filt * 3 + m // KB)

                    products(24 * half, 24 * half + 4)
                    ac.wait_ge(fs_tz, filt * 2 + (half + 1))
                    nc.scalar.activation(tabs[:], taps[:], ACT.Abs).then_inc(fs_abs, 1)
                    products(24 * half + 4, 24 * half + 14)
                    if half:
                        ac.wait_ge(fs_dma, filt * 64 + 32)
                    for o in range(5):
                        ac.wait_ge(fs_spec, filt * 10 + (half * 5 + o + 6))
                        nc.scalar.activation(spec_out[:, o, :], bank[5 if (half * 5 + o) % 2 else 7][:], ACT.Copy
                                             ).then_inc(fs_out, 1)
                    ac.wait_ge(fs_out, filt * 10 + (half * 5 + 7))
                    dst = spec_dram[bass.ds(filt, 1)].rearrange("a p s c -> (a p) s c")[:, :, half * 512:(half + 1) * 512]
                    ac.dma_start(dst[:, 0:5, :], spec_out[:]).then_inc(fs_dma, 16)
                    ac.dma_start(dst[:, 5:6, :], spec_out[:, 1:2, :]).then_inc(fs_dma, 16)
                    products(24 * half + 14, 24 * half + 24)
                ac.wait_ge(fs_dma, filt * 64 + 64)
            for j in range(AHEAD):
                round_unit(ac, Units(0), j)
            modulate_act(ac, n1, 0, n1["hi_ap"], (0, 1))
            ffn_act(ac, fa, U_FFN1, s1, g1, g1_hi, 512, F1_LOOPS)

            ac.wait_ge(fa["bfree"], KB + KB * N_CHUNK)
            norm_act(ac, nctx, [y_res], 256)
            modulate_act(ac, nctx, 1, nctx["hi_ap"], (1,))

            def gates(s, it, d, b, k_ap, g_ap, cur, value):
                ac.wait_ge(w_used, value)
                nc.scalar.activation(k_ap, bank[b][:], ACT.Sigmoid, scale=-1.0)
                nc.scalar.activation(g_ap, bank[b][:], ACT.Sigmoid).then_inc(s["gate"], 1)
                ac.wait_ge(s["gate"], it * 2 + (d + 1))
                ac.wait_ge(s["cur"], it + 1)
                for h in range(2):
                    ins = nc.scalar.activation(g_ap[:, h * 256:(h + 1) * 256], g_ap[:, h * 256:(h + 1) * 256], ACT.Ln,
                                               scale=cur[:, 4 + 2 * d + h:5 + 2 * d + h], bias=cur[:, 2 * d + h:2 * d + h + 1])
                ins.then_inc(s["log"], 1)
                for h in range(2):
                    ins = nc.scalar.activation(k_ap[:, h * 256:(h + 1) * 256], k_ap[:, h * 256:(h + 1) * 256], ACT.Copy,
                                               scale=cur[:, 4 + 2 * d + h:5 + 2 * d + h])
                ins.then_inc(s["k"], 1)

            def flat(ap):
                return ap.rearrange("p h t -> p (h t)")

            with ac.Fori(0, PAIRS) as it:
                un = Units(U_CTX, it, 12)
                for j in range(12):
                    round_unit(ac, un, j + AHEAD)
                    if j in (3, 7):
                        d = j // 4
                        gates(cs, it, d, d, flat(ck[:, d]), flat(cg[:, d]), c_cur, used(un, j))
                ac.wait_ge(w_used, used(un, 11))
                nc.scalar.activation(flat(cv[:]), bank[2][:], ACT.Copy).then_inc(cs["v"], 1)
                ac.wait_ge(cs["sum"], it * 24 + 24)
                nc.scalar.activation(cexp[:], csum[:], ACT.Exp).then_inc(cs["exp"], 1)
                for n in range(3):
                    ac.wait_ge(cs["tpe"], it * 3 + (n + 1))
                    nc.scalar.activation(flat(ctok[:, n]), bank[3 + n][:], ACT.Copy).then_inc(cs["tok"], 1)
                ac.wait_ge(cs["st"], it + 1)
                nc.scalar.activation(states[:, bass.ds(it, 1)].rearrange("p a n c -> p (a n c)"), bank[6][:], ACT.Copy
                                     ).then_inc(cs["stout"], 1)

            norm_act(ac, nx, [x_res], 256)
            modulate_act(ac, nx, 1, nx["hi_ap"], (0,))
            with ac.Fori(0, PAIRS) as it:
                un = Units(U_HG, it, 20)
                for j in range(20):
                    round_unit(ac, un, j + AHEAD)
                    if j in (3, 7):
                        d = j // 4
                        gates(xs, it, d, d, flat(xk[:, d]), flat(xa[:, d]), x_cur, used(un, j))
                    if j == 11:
                        ac.wait_ge(w_used, used(un, j))
                        nc.scalar.activation(flat(xv[:]), bank[2][:], ACT.Copy).then_inc(xs["v"], 1)
                    if j == 15:
                        ac.wait_ge(w_used, used(un, j))
                        nc.scalar.activation(flat(xq[:]), bank[3][:], ACT.Copy, scale=DK ** -0.5).then_inc(xs["v"], 1)
                    if j == 19:
                        ac.wait_ge(w_used, used(un, j))
                        nc.scalar.activation(flat(xg[:]), bank[4][:], ACT.Silu).then_inc(xs["v"], 1)
                ac.wait_ge(xs["tpe"], it + 1)
                nc.scalar.activation(flat(vtok[:]), bank[7][:], ACT.Copy).then_inc(xs["tok"], 1)
                ac.wait_ge(xs["log"], it * 2 + 2)
                ac.wait_ge(xs["init"], it + 1)
                for lv in range(LEVELS + 1):
                    s = lv + 1
                    if lv:
                        ac.wait_ge(xs["sum"], it * 32 + 4 * lv)
                    if lv >= 2:
                        ac.wait_ge(xs["kq"], it * 10 + (s - 1))
                    if lv < LEVELS:
                        m = 1 << lv
                        nc.scalar.activation(halves(eq[s % 2][:], m)[:, :, 1, :], halves(xa[:, 0], m)[:, :, 1, :], ACT.Exp)
                        nc.scalar.activation(halves(eq[s % 2][:], m)[:, :, 0, :], halves(xa[:, 1], m)[:, :, 0, :], ACT.Exp)
                        nc.scalar.activation(halves(ek[s % 2][:], m)[:, :, 0, :], halves(xe[:, 0], m)[:, :, 0, :], ACT.Exp)
                        nc.scalar.activation(halves(ek[s % 2][:], m)[:, :, 1, :], halves(xe[:, 1], m)[:, :, 1, :], ACT.Exp
                                             ).then_inc(xs["exp"], 1)
                    else:
                        nc.scalar.activation(eq[1][:], xa[:, 0], ACT.Exp)
                        nc.scalar.activation(ek[1][:], xa[:, 1], ACT.Exp).then_inc(xs["exp"], 1)
                ac.wait_ge(xs["ope"], it + 1)
                nc.scalar.activation(osq[:], bank[3][:], ACT.Square).then_inc(xs["osq"], 1)
                ac.wait_ge(xs["mean"], it + 1)
                nc.scalar.activation(root[:], bank[4][:], ACT.Sqrt, bias=EPS).then_inc(xs["root"], 1)

            with ac.Fori(0, PAIRS) as it:
                un = Units(U_HY, it, 12)
                for j in range(12):
                    round_unit(ac, un, j + AHEAD)
                    if j % 4 == 3:
                        ac.wait_ge(w_used, used(un, j))
                        ac.wait_ge(ys["cur"], it + 1)
                        p = j // 4
                        for b in range(2):
                            c0 = p * 8 + b * 4
                            ins = nc.scalar.activation(conv[:, p, b, :], bank[p][:, b * 256:(b + 1) * 256], ACT.Identity,
                                                       scale=y_cur[:, c0 + 1:c0 + 2], bias=y_cur[:, c0 + 3:c0 + 4])
                        ins.then_inc(ys["cb"], 1)
                for f in range(2):
                    ac.wait_ge(ys["tpe"], it * 2 + (f + 1))
                    nc.scalar.activation(flat(ut[:]), bank[3][:], ACT.Copy).then_inc(ys["ut"], 1)

            ac.wait_ge(ys["z"], 2 + 2 * PAIRS)
            for n in range(4):
                nc.scalar.activation(m_hi[:, 4 * n:4 * n + 4, :], mix[:, 4 * n:4 * n + 4, :], ACT.Copy).then_inc(ms["hi"], 1)
            with ac.Fori(0, KB // 4) as it:
                un = Units(U_OUT, it, 8)
                for j in range(8):
                    round_unit(ac, un, j + AHEAD)
            ac.wait_ge(ms["res"], 2 + KB // 2)
            norm_act(ac, n2, [x_res], 256)
            modulate_act(ac, n2, 2, n2["hi_ap"], (0,))
            ffn_act(ac, fb_, U_FFN2, s2, g2, g2_hi, 256, F2_LOOPS)
            ac.wait_ge(fb_["bfree"], KB + KB * N_CHUNK)
            norm_act(ac, nf, [x_res], 256)
            for g in range(8):
                a, q = g // 4, g % 4
                ac.wait_ge(fin["tr"], g + 1)
                nc.scalar.activation(xt[:, a, q * 512:(q + 1) * 512], bank[g % 4][:], ACT.Copy).then_inc(fin["ev"], 1)

        @block.vector
        def _(ve):
            ve.sem_inc(ada_out, 1)
            ve.sem_inc(ada_x, RING)
            ve.sem_inc(fs_taps, 4)
            ve.sem_inc(fs_norm, 1)
            ve.sem_inc(xs["mix"], 1)
            ve.sem_inc(xs["pred"], 2)
            ve.sem_inc(ys["z"], 2)
            ve.sem_inc(ys["specfree"], 1)
            ve.sem_inc(ms["res"], 2)
            for n in range(3):
                ve.wait_ge(rows_t, n + 1)
                nc.vector.tensor_copy(cols[n][:, 0:N_COLS[n]], bank[n][:, 0:N_COLS[n]]).then_inc(cols_done, 1)
            ve.wait_ge(cols_done, 3)
            logits = cols[1][:, 88:120].rearrange("p (d n h) -> p d n h", d=2, n=2)
            nc.vector.tensor_tensor(lbt[:], logits[:, :, 0], logits[:, :, 1], ALU.max).then_inc(lb_dve, 1)
            ve.wait_ge(lb_dve, 1)
            for n in range(2):
                nc.vector.tensor_tensor(lbe[:, n], logits[:, :, n], lbt[:], ALU.subtract).then_inc(lb_dve, 1)
            ve.wait_ge(lb_act, 1)
            nc.vector.tensor_tensor(lbt[:], lbe[:, 0], lbe[:, 1], ALU.add).then_inc(lb_dve, 1)
            ve.wait_ge(lb_dve, 4)
            nc.vector.reciprocal(lbt[:], lbt[:]).then_inc(lb_dve, 1)
            ve.wait_ge(lb_dve, 5)
            nc.vector.tensor_tensor(lb[:], lbe[:, 0], lbt[:], ALU.mult).then_inc(lb_dve, 1)
            ve.wait_ge(lb_dve, 6)
            for d in range(2):
                by_pair = lb[:, d, :].rearrange("p (a h) -> p a h", h=2)
                nc.vector.tensor_copy(hg_cols[:, :, 2 * d:2 * d + 2], by_pair)
                nc.vector.tensor_scalar(hg_cols[:, :, 4 + 2 * d:6 + 2 * d], by_pair, -1.0, 1.0, ALU.mult, ALU.add)
            nc.vector.tensor_copy(hg_cols[:, :, 8:10], cols[1][:, 80:88].rearrange("p (a h) -> p a h", h=2))
            for part in range(3):
                for w in range(4):
                    c0 = w * 24 + part * 8
                    dst = hy_cols[:, :, part * 8:(part + 1) * 8].rearrange("p a (b w) -> p a b w", w=4)[:, :, :, w]
                    ins = nc.vector.tensor_copy(dst, cols[2][:, c0:c0 + 8].rearrange("p (a b) -> p a b", b=2))
            ins.then_inc(lb_dve, 1)
            MAGIC = 1.5 * 2.0 ** 23
            C1 = 6.28125
            C2 = float(np.float32(TWO_PI - C1))
            C3 = float(np.float32(TWO_PI - C1 - C2))
            PI = float(np.nextafter(np.float32(np.pi), np.float32(0)))
            ve.wait_ge(small_in, SMALL)
            for n in range(3):
                ve.wait_ge(fm_pe, n + 1)
                r, a, k = ang[n % 2], ang[2], ang[3]
                nc.vector.tensor_scalar(a[:], bank[0][0:FILT_ORDER, 0:SEQ], fbias[:, n:n + 1], fbias[:, 3:4],
                                        ALU.add, ALU.mult).then_inc(fm_dve, 1)
                ve.wait_ge(fm_dve, 6 * n + 1)
                nc.vector.tensor_scalar(k[:], a[:], 1.0 / TWO_PI, MAGIC, ALU.mult, ALU.add).then_inc(fm_dve, 1)
                ve.wait_ge(fm_dve, 6 * n + 2)
                nc.vector.tensor_scalar(k[:], k[:], MAGIC, None, ALU.subtract).then_inc(fm_dve, 1)
                ve.wait_ge(fm_dve, 6 * n + 3)
                for m, (c, src) in enumerate(((C1, a), (C2, r))):
                    nc.vector.scalar_tensor_tensor(out=r[:], in0=k[:], scalar=-c, in1=src[:], op0=ALU.mult, op1=ALU.add
                                                   ).then_inc(fm_dve, 1)
                    ve.wait_ge(fm_dve, 6 * n + 4 + m)
                nc.vector.scalar_tensor_tensor(out=a[:], in0=k[:], scalar=-C3, in1=r[:], op0=ALU.mult, op1=ALU.add
                                               ).then_inc(fm_arg, 1)
                ve.wait_ge(fm_arg, n + 1)
                nc.vector.tensor_scalar(r[:], a[:], PI, -PI, ALU.min, ALU.max).then_inc(fm_dve, 1)
            norm_dve(ve, n1, 512)
            ve.wait_ge(tab_in, 32)
            with ve.Fori(0, 2) as filt:
                for half in range(2):
                    def sums(first, end):
                        for m in first_units(range(24 * half + first, 24 * half + end)):
                            ada_landed(ve, m, 0, filt, ADA_BODY)
                            ada_vector(ve, m, filt * (3 * ADA_EW) + (RING + ew_before(m)), filt * 3 + m // KB)

                    sums(0, 4)
                    for n in range(4):
                        ve.wait_ge(fs_taps_pe, filt * 8 + (half * 4 + n + 5))
                        nc.vector.tensor_tensor(taps[:, n // 2, n % 2, :], bank[n][:],
                                                window[:, n // 2, half * 512:(half + 1) * 512], ALU.mult).then_inc(fs_taps, 1)
                    ve.wait_ge(fs_taps, filt * 8 + (half * 4 + 8))
                    nc.vector.memset(taps[0:1, 0, 1, :], 0.0).then_inc(fs_tz, 1)
                    sums(4, 8)
                    if half:
                        ada_take(ve, filt * 3 + 1, 6, 2)
                    ve.wait_ge(fs_l1, filt * 2 + (half + 1))
                    nc.vector.reciprocal(l1inv[:], bank[4][:]).then_inc(fs_inv, 1)
                    ve.wait_ge(fs_tz, filt * 2 + (half + 1))
                    ve.wait_ge(fs_spec, filt * 10 + (half * 5 + 5))
                    nc.vector.tensor_tensor(tsum[:], taps[:, :, 0, :], taps[:, :, 1, :], ALU.add)
                    nc.vector.tensor_tensor(tdif[:], taps[:, :, 1, :], taps[:, :, 0, :], ALU.subtract).then_inc(fs_inv, 1)
                    ve.wait_ge(fs_inv, filt * 8 + (half * 4 + 2))
                    for a in range(TB):
                        nc.vector.tensor_tensor(tsum[:, a, :], tsum[:, a, :], l1inv[:], ALU.mult)
                        ins = nc.vector.tensor_tensor(tdif[:, a, :], tdif[:, a, :], l1inv[:], ALU.mult)
                        ins.then_inc(fs_inv, 1)
                    ve.wait_ge(fs_inv, filt * 8 + (half * 4 + 4))
                    ve.wait_ge(fs_hyd, filt * 32 + (half * 16 + 16))
                    nc.vector.tensor_tensor(tsum[0:1, 0, :], tsum[0:1, 0, :], hyd_row[:], ALU.add).then_inc(fs_norm, 1)
                    sums(8, 16)
                    if not half:
                        ada_take(ve, filt * 3, 6, 2)
                    sums(16, 24)
                    if half:
                        ada_take(ve, filt * 3 + 2, 6, 2)

            def finish_mods(m0, m1, both):
                for t in range(2):
                    for m in range(m0, m1 if t == 0 else both):
                        bias = cols[0][:, m * KB:(m + 1) * KB] if m < 8 else cols[1][:, 0:KB]
                        ins = nc.vector.tensor_tensor(mods[:, m, :, t], mods[:, m, :, t], bias, ALU.add)
                ins.then_inc(mod_done, 1)

            def norm_scale(which, m, streams):
                g = C_GAIN[which]
                for t in range(streams):
                    nc.vector.scalar_tensor_tensor(out=scale_a[:, which, :, t], in0=mods[:, m, :, t], scalar=1.0,
                                                   in1=cols[1][:, g:g + KB], op0=ALU.add, op1=ALU.mult)

            ve.wait_ge(ada_out, 1 + ADA_FIRST_H)
            finish_mods(0, ADA_FIRST, ADA_FIRST)
            ve.wait_ge(mod_done, 1)
            norm_scale(0, 1, 2)
            nc.vector.tensor_scalar(gate[:, 0], mods[:, 2], 0.5, None, ALU.mult).then_inc(mod_done, 1)
            for j in range(AHEAD):
                rest_unit(ve, Units(0), j)
            ve.wait_ge(mod_done, 2)
            modulate_dve(ve, n1, 0, [x_res, y_res], lambda t, kb: h1_lo[:, t, kb, :], (0, 1))
            ffn_dve(ve, fa, U_FFN1, s1, g1, g1_hi, g1_lo, 512, [x_res, y_res], 0, F1_LOOPS)

            ve.wait_ge(ada_out, 1 + 2 * N_MOD)
            finish_mods(ADA_FIRST, N_MOD, 5)
            ve.wait_ge(mod_done, 3)
            norm_scale(1, 4, 2)
            norm_scale(2, 7, 1)
            nc.vector.tensor_copy(gate_x[:], mods[:, 5, :, 0])
            nc.vector.tensor_scalar(gate[:, 2, :, 0], mods[:, 8, :, 0], 0.5, None, ALU.mult).then_inc(mod_done, 1)
            norm_dve(ve, nctx, 256)
            ve.wait_ge(mod_done, 4)
            modulate_dve(ve, nctx, 1, [y_res], lambda t, kb: hc_lo[:, kb, :], (1,))
            with ve.Fori(0, PAIRS) as it:
                un = Units(U_CTX, it, 12)
                ve.wait_ge(cs["stout"], it + 1)
                nc.vector.tensor_copy(c_cur[:], hg_cols[:, bass.ds(it, 1), :].rearrange("p a c -> p (a c)")).then_inc(cs["cur"], 1)
                nc.vector.memset(csum[:], 0.0).then_inc(cs["init"], 1)
                for j in range(12):
                    rest_unit(ve, un, j + AHEAD)

            norm_dve(ve, nx, 256)
            ve.wait_ge(cs["stout"], 1 + PAIRS)
            modulate_dve(ve, nx, 1, [x_res], lambda t, kb: hx_lo[:, kb, :], (0,))
            ve.wait_ge(msk_in, 16)
            with ve.Fori(0, PAIRS) as it:
                un = Units(U_HG, it, 20)
                nc.vector.tensor_copy(s_cur[:].rearrange("p n c -> p (n c)"),
                                      states[:, bass.ds(it, 1)].rearrange("p a n c -> p (a n c)"))
                nc.vector.tensor_copy(x_cur[:], hg_cols[:, bass.ds(it, 1), :].rearrange("p a c -> p (a c)")).then_inc(xs["cur"], 1)
                nc.vector.memset(xe[:], 0.0).then_inc(xs["init"], 1)
                for j in range(20):
                    rest_unit(ve, un, j + AHEAD)

                def keys(s):
                    b = s % 2
                    if s >= 2:
                        ve.wait_ge(xs["score"], it * 9 + (s - 1))
                    if s == 0:
                        ve.wait_ge(xs["k"], it * 2 + 2)
                        ve.wait_ge(xs["v"], it * 3 + 2)
                        nc.vector.tensor_tensor(lk[b][:], xk[:, 0], xk[:, 1], ALU.add)
                        nc.vector.tensor_copy(lq[b][:], xq[:]).then_inc(xs["kq"], 1)
                        return
                    ve.wait_ge(xs["exp"], it * 9 + s)
                    nc.vector.tensor_tensor(lq[b][:], xq[:], eq[b][:], ALU.mult)
                    if s <= LEVELS:
                        m = 1 << (s - 1)
                        for side in range(2):
                            ins = nc.vector.tensor_tensor(halves(lk[b][:], m)[:, :, side, :], halves(xk[:, side], m)[:, :, side, :],
                                                          halves(ek[b][:], m)[:, :, side, :], ALU.mult)
                    else:
                        ins = nc.vector.tensor_tensor(lk[b][:], xq[:], ek[b][:], ALU.mult)
                    ins.then_inc(xs["kq"], 1)

                keys(0)
                for s in range(LEVELS + 1):
                    keys(s + 1)
                    ve.wait_ge(xs["score"], it * 9 + (s + 1))
                    scores = bank[5 + s % 2][:].rearrange("p (n c) -> p n c", n=4)
                    if s == 0:
                        nc.vector.tensor_tensor(prob[:], scores, ident[:].rearrange("p (a c) -> p a c", a=1).to_broadcast([P, 4, P]),
                                                ALU.mult).then_inc(xs["pred"], 1)
                    elif s < LEVELS:
                        ve.wait_ge(xs["pred"], it * 9 + (s + 2))
                        nc.vector.tensor_copy(spec_mark[:], ident[:, 0:1])
                        nc.vector.copy_predicated(prob[:], mask[:, s - 1:s, :].to_broadcast([P, 4, P]), scores
                                                  ).then_inc(xs["pred"], 1)
                    else:
                        nc.vector.tensor_copy(cross[:], scores).then_inc(xs["pred"], 1)
                ve.wait_ge(xs["root"], it + 1)
                nc.vector.reciprocal(rstd[:], root[:]).then_inc(xs["rstd"], 1)
                ve.wait_ge(xs["rstd"], it + 1)
                for h in range(2):
                    ins = nc.vector.scalar_tensor_tensor(out=onorm[:, h, :], in0=bank[3][:, h * 256:(h + 1) * 256],
                                                         scalar=x_cur[:, 8 + h:9 + h], in1=rstd[:, h * 256:(h + 1) * 256],
                                                         op0=ALU.mult, op1=ALU.mult)
                ins.then_inc(xs["on"], 1)
                ve.wait_ge(xs["on"], it + 1)
                ve.wait_ge(xs["v"], it * 3 + 3)
                nc.vector.tensor_tensor(mix[:, bass.ds(it * 2, 2), :], onorm[:], xg[:], ALU.mult).then_inc(xs["mix"], 1)

            with ve.Fori(0, PAIRS) as it:
                un = Units(U_HY, it, 12)
                nc.vector.tensor_copy(y_cur[:], hy_cols[:, bass.ds(it, 1), :].rearrange("p a c -> p (a c)")).then_inc(ys["cur"], 1)
                for j in range(12):
                    rest_unit(ve, un, j + AHEAD)
                    if j % 4 == 3:
                        p = j // 4
                        ve.wait_ge(ys["cb"], it * 3 + (p + 1))
                        for b in range(2):
                            c0 = p * 8 + b * 4
                            o = conv[:, p, b, :].rearrange("p (r c) -> p r c", c=GRID_W)
                            u = bank[p][:, b * 256:(b + 1) * 256].rearrange("p (r c) -> p r c", c=GRID_W)
                            nc.vector.scalar_tensor_tensor(out=o[:, :, 1:], in0=u[:, :, :-1], scalar=y_cur[:, c0:c0 + 1],
                                                           in1=o[:, :, 1:], op0=ALU.mult, op1=ALU.add).then_inc(ys["conv"], 1)
                            ve.wait_ge(ys["conv"], it * 12 + (4 * p + 2 * b + 1))
                            nc.vector.scalar_tensor_tensor(out=o[:, :, :-1], in0=u[:, :, 1:], scalar=y_cur[:, c0 + 2:c0 + 3],
                                                           in1=o[:, :, :-1], op0=ALU.mult, op1=ALU.add).then_inc(ys["conv"], 1)
                ve.wait_ge(ys["spec"], it * 32 + 32)
                for f in range(2):
                    ve.wait_ge(ys["fft"], it * 2 + (f + 1))
                    re, im = (bank[4 + n][:].rearrange("p (b c) -> p b c", b=2) for n in range(2))
                    for n, (part, s) in enumerate(((re, 0), (im, 1), (re, 1), (im, 2))):
                        ins = nc.vector.tensor_tensor(prod[n][:], part, spec[:, f, s], ALU.mult)
                        if n % 2:
                            ins.then_inc(ys["prod"], 1)
                    for n in range(2):
                        ve.wait_ge(ys["prod"], it * 4 + (2 * f + n + 1))
                        nc.vector.tensor_tensor(yf[:, n], prod[2 * n][:], prod[2 * n + 1][:],
                                                ALU.add if n else ALU.subtract).then_inc(ys["yf"], 1)
                    if f == 1:
                        ve.wait_ge(ys["prod"], it * 4 + 4)
                        nc.vector.tensor_copy(spec_mark[:], ident[:, 0:1]).then_inc(ys["specfree"], 1)
                    ve.wait_ge(ys["inv"], it * 2 + (f + 1))
                    ve.wait_ge(ys["conv"], it * 12 + 12)
                    y = bank[6][:].rearrange("p (b c) -> p b c", b=2)
                    if f == 0:
                        nc.vector.tensor_tensor(zg[:], y, conv[:, 1], ALU.mult).then_inc(ys["z"], 1)
                    else:
                        nc.vector.tensor_tensor(mix[:, bass.ds(it * 2 + HEADS, 2), :], y, conv[:, 2], ALU.mult).then_inc(ys["z"], 1)

            for n in range(4):
                ve.wait_ge(ms["hi"], n + 1)
                nc.vector.tensor_tensor(m_lo[:, 4 * n:4 * n + 4, :], mix[:, 4 * n:4 * n + 4, :],
                                        m_hi[:, 4 * n:4 * n + 4, :].bitcast(F32), ALU.subtract).then_inc(ms["lo"], 1)
            with ve.Fori(0, KB // 4) as it:
                un = Units(U_OUT, it, 8)
                for j in range(8):
                    rest_unit(ve, un, j + AHEAD)
                    if j % 4 == 3:
                        ve.wait_ge(w_used, used(un, j))
                        for b in range(2):
                            d = it * 4 + (j // 4 * 2 + b)
                            res = x_res[:, bass.ds(d, 1), :].rearrange("p a c -> p (a c)")
                            ins = nc.vector.scalar_tensor_tensor(
                                out=res, in0=bank[j // 4][:, b * 256:(b + 1) * 256],
                                scalar=gate_x[:, bass.ds(d, 1)], in1=res, op0=ALU.mult, op1=ALU.add)
                        ins.then_inc(ms["res"], 1)

            norm_dve(ve, n2, 256)
            modulate_dve(ve, n2, 2, [x_res], lambda t, kb: h2_lo[:, kb, :], (0,))
            ffn_dve(ve, fb_, U_FFN2, s2, g2, g2_hi, g2_lo, 256, [x_res], 2, F2_LOOPS)
            norm_dve(ve, nf, 256)
            ve.wait_ge(nf["rstd"], 1)
            for kb in range(KB):
                nc.vector.scalar_tensor_tensor(out=xo[:, kb, :], in0=x_res[:, kb, :], scalar=cols[1][:, 64 + kb:65 + kb],
                                               in1=rstd[:, 0:256], op0=ALU.mult, op1=ALU.mult).then_inc(fin["o"], 1)


_INS = ['x', 'c', 'ctx', 'c_ctx', 'ada_w', 'ada_b', 'norm_ffn1', 'ffn1_w1', 'ffn1_w3', 'ffn1_w2', 'norm_mix', 'w_in',
        'hg_lb_logits', 'hg_norm', 'hy_conv_w', 'hy_conv_b', 'filt_w1', 'filt_b1', 'filt_w2', 'filt_b2', 'filt_w3',
        'filt_b3', 'filt_freq', 'filt_w_out', 'hy_d', 'w_out', 'norm_ffn2', 'ffn2_w1', 'ffn2_w3', 'ffn2_w2',
        'final_norm']


def kernel(**inputs):
    import concourse.bacc as _bacc
    from concourse.bass_utils import run_bass_kernel_spmd as _run

    nc = _bacc.Bacc("TRN2", target_bir_lowering=False, num_devices=1)
    arrays, args = {}, {}
    for name, a in [(n, inputs[n]) for n in _INS] + list(shape_tables().items()):
        a = np.ascontiguousarray(a)
        arrays[f"in_{name}_dram"] = a
        args[name] = nc.dram_tensor(f"in_{name}_dram", a.shape, mybir.dt.from_np(a.dtype), kind="ExternalInput").ap()
    out = nc.dram_tensor("out_0_dram", (1, SEQ, D), F32, kind="ExternalOutput").ap()
    build(nc, args, out)
    r = _run(nc, [arrays], core_ids=[0])
    return r.results[0]["out_0_dram"]
```

```python
from contextlib import ExitStack

import numpy as np

import concourse.bass as bass
from concourse import mybir

F32 = mybir.dt.float32
F32R = mybir.dt.float32r
I32 = mybir.dt.int32
ACT = mybir.ActivationFunctionType
ALU = mybir.AluOpType

P = 128
D = 2048
KB = D // P
SEQ = 256
CTX = 256
TB = SEQ // P
FF = 5632
CHUNK = 256
N_CHUNK = FF // CHUNK
N_MOD = 9
EPS = 1e-6
HEADS = 8
PAIRS = HEADS // 2
DK = 128
HG = HEADS * DK
HY = D - HG
GRID_W = 64
FILT_EMB = 33
FILT_ORDER = 64
LEVELS = 8
UNIT = 1024
RING = 4
KG = KB // 4
TWO_PI = 2.0 * np.pi

U_FFN1 = 0
U_CTX = U_FFN1 + 12 * N_CHUNK
U_HG = U_CTX + 12 * PAIRS
U_HY = U_HG + 20 * PAIRS
U_OUT = U_HY + 12 * PAIRS
U_FFN2 = U_OUT + 4 * (KB // 2)
U_END = U_FFN2 + 12 * N_CHUNK

ADA_FIRST = 3
HALF = 1024
ADA_FIRST_H = 2 * ADA_FIRST
ADA_BOTH = 4
ADA_LATENT = 8
FILT_STEPS = 4
ADA_BODY = 3 * KB
ADA_PE = (4, 8, 11, 15)
ADA_EW = KB - len(ADA_PE)
WIDE = 8

T_COS, T_SIN, T_COSN, T_SINN, T_ITR, T_ITI = 0, 512, 1024, 1280, 1792, 2304
T_COLS = 2816


def shape_tables():
    n2 = 2 * SEQ
    t = np.arange(SEQ, dtype=np.float64)
    ang = 2 * np.pi * ((t[:, None] * t[None, :]) % n2) / n2
    alt = 1.0 - 2.0 * (t % 2)

    def blocks(m):
        return m.reshape(TB, P, m.shape[1]).transpose(1, 0, 2).reshape(P, -1)

    cosn = np.cos(ang)[:, :P].copy()
    cosn[:, 0] = alt
    sinn = -np.sin(ang)
    sinn[:, 0] = alt
    weight = np.where(t == 0, 1.0, 2.0)[:, None] / n2
    itr = weight * np.cos(ang)
    iti = -weight * np.sin(ang)
    iti[0] = alt / n2
    dft = np.concatenate([blocks(m) for m in (np.cos(ang), np.sin(ang), cosn, sinn, itr, iti)], 1).astype(np.float32)

    pos = np.arange(SEQ, dtype=np.float32)
    tt = pos / np.float32(SEQ - 1)
    bands = (FILT_EMB - 1) // 2
    fb = np.linspace(1e-4, bands - 1, bands, dtype=np.float32)
    a = np.float32(2 * np.pi / SEQ) * pos[:, None] * fb[None, :]
    z = np.concatenate([tt[:, None], np.cos(a), -np.sin(a)], 1).T.astype(np.float32)
    deltas = np.abs(np.linspace(np.log(1e-2) / 1.5, np.log(1e-2) / 0.3, HY, dtype=np.float32))
    window = blocks(np.exp(-tt[:, None] * deltas)).astype(np.float32)

    i = np.arange(P)
    masks = [((i[:, None] // (2 * m) == i[None, :] // (2 * m)) & (i[:, None] // m != i[None, :] // m))
             for m in (1, 2, 4, 8, 16, 32, 64)]
    masks = np.concatenate(masks, 1).astype(np.int32)
    return {
        "t_dft": np.ascontiguousarray(dft),
        "t_emb": np.ascontiguousarray(z),
        "t_window": np.ascontiguousarray(window),
        "t_mask": np.ascontiguousarray(masks),
        "t_ident": np.eye(P, dtype=np.float32),
    }


class Units:

    def __init__(self, base, it=0, per=0):
        self.base, self.it, self.per = base, it, per

    def slot(self, j):
        return j % RING

    def number(self, j):
        return self.it * self.per + (self.base + j) if self.per else self.base + j

    def loads(self, j):
        n = (self.base + j) // RING + 1
        return self.it * (self.per // RING) + n if self.per else n


def build(nc, i, out):
    with ExitStack() as life:
        def sem(name):
            return life.enter_context(nc.semaphore(name))

        def sb(name, shape, dt=F32, scope=life):
            return scope.enter_context(nc.sbuf_tensor(name, shape, dt))

        x_res = sb("x_res", [P, KB, SEQ])
        raw = [sb(f"raw{s}", [P, UNIT]) for s in range(RING)]
        wide = ExitStack()
        ada_wide = [sb(f"ada_wide{s}", [P, UNIT], scope=wide) for s in range(WIDE)]
        wide.close()
        w_hi = [sb(f"w_hi{s}", [P, UNIT], F32R) for s in range(RING)]
        w_lo = [sb(f"w_lo{s}", [P, UNIT], F32R) for s in range(RING)]
        ident = sb("ident", [P, P])
        ones_d = sb("ones_d", [P, P])
        ones_h = sb("ones_h", [P, P])
        ones_1 = sb("ones_1", [P, P])
        rows = [sb(f"rows{n}", [P, P]) for n in range(3)]
        cols = [sb(f"cols{n}", [P, P]) for n in range(3)]
        mods = sb("mods", [P, N_MOD, KB, 2])
        silu_c = sb("silu_c", [P, KB, 2])
        scale_a = sb("scale_a", [P, 3, KB, 2])
        gate = sb("gate", [P, 3, KB, 2])
        gate_x = sb("gate_x", [P, KB])
        spec_mark = sb("spec_mark", [P, 1])
        lb = sb("lb", [P, 2, HEADS])
        lbe = sb("lbe", [P, 2, 2, HEADS])
        lbt = sb("lbt", [P, 2, HEADS])
        hg_cols = sb("hg_cols", [P, PAIRS, 10])
        hy_cols = sb("hy_cols", [P, PAIRS, 24])
        states = sb("states", [P, PAIRS, 4, DK])
        sq2 = sb("sq2", [P, 2 * 512])
        sq = [sq2[:, n * 512:(n + 1) * 512] for n in range(2)]
        sq_sum = sb("sq_sum", [P, 512])
        root = sb("root", [P, 512])
        rstd = sb("rstd", [P, 512])
        xn2 = sb("xn2", [P, 2 * 512])
        xn = [xn2[:, n * 512:(n + 1) * 512] for n in range(2)]

        ffn1 = ExitStack()
        y_res = sb("y_res", [P, KB, CTX], scope=ffn1)
        ada_raw = [sb(f"ada_raw{s}", [P, UNIT], scope=ffn1) for s in range(RING)]
        first = ExitStack()
        ada_prod3 = sb("ada_prod3", [P, UNIT], scope=first)
        ada_sum = [[states[:, 2 * t:2 * t + 2].rearrange("p a n c -> p (a n c)") for t in range(2)],
                   [ada_raw[0][:], ada_raw[1][:]], [ada_raw[2][:], ada_raw[3][:]]]
        ada_prod = [sq2[:], xn2[:], ada_prod3[:]]
        dft = sb("dft", [P, T_COLS], scope=first)
        emb = sb("emb", [FILT_EMB, SEQ], scope=first)
        window = sb("window", [P, TB, HY], scope=first)
        fw1 = sb("fw1", [FILT_EMB, FILT_ORDER], scope=first)
        fw23 = sb("fw23", [FILT_ORDER, 2, FILT_ORDER], scope=first)
        fbias = sb("fbias", [FILT_ORDER, 4], scope=first)
        fout = sb("fout", [FILT_ORDER, 2, 512], scope=first)
        hyd_row = sb("hyd_row", [1, 512], scope=first)
        hid = [sb(f"hid{n}", [FILT_ORDER, SEQ], scope=first) for n in range(3)]
        ang = [sb(f"ang{n}", [FILT_ORDER, SEQ], scope=first) for n in range(4)]
        tok_in = ExitStack()
        xin = sb("xin", [P, TB, D], scope=tok_in)
        yin = sb("yin", [P, TB, D], scope=tok_in)
        tok_in.close()
        taps = sb("taps", [P, TB, 2, 512], scope=first)
        tabs = sb("tabs", [P, TB, 2, 512], scope=first)
        l1inv = sb("l1inv", [P, 512], scope=first)
        tsum = sb("tsum", [P, TB, 512], scope=first)
        tdif = sb("tdif", [P, TB, 512], scope=first)
        spec_out = sb("spec_out", [P, 5, 512], scope=first)
        first.close()
        ffn = ExitStack()
        h1_hi = sb("h1_hi", [P, 2, KB, SEQ], F32R, scope=ffn)
        h1_lo = sb("h1_lo", [P, 2, KB, SEQ], F32R, scope=ffn)
        s1 = [sb(f"s1_{b}", [P, 512], scope=ffn) for b in range(2)]
        g1 = [sb(f"g1_{b}", [P, 512], scope=ffn) for b in range(2)]
        g1_hi = [sb(f"g1_hi{b}", [P, 512], F32R, scope=ffn) for b in range(2)]
        g1_lo = [sb(f"g1_lo{b}", [P, 512], F32R, scope=ffn) for b in range(2)]
        ffn.close()
        con = ExitStack()
        hc_hi = sb("hc_hi", [P, KB, CTX], F32R, scope=con)
        hc_lo = sb("hc_lo", [P, KB, CTX], F32R, scope=con)
        c_cur = sb("c_cur", [P, 10], scope=con)
        ck = sb("ck", [P, 2, 2, CTX], scope=con)
        cg = sb("cg", [P, 2, 2, CTX], scope=con)
        cv = sb("cv", [P, 2, CTX], scope=con)
        ctot = [sb(f"ctot{n}", [P, 2, 2, CTX // 2], scope=con) for n in range(2)]
        csum = sb("csum", [P, 2, 2, CTX], scope=con)
        cexp = sb("cexp", [P, 2, 2, CTX], scope=con)
        ckd = sb("ckd", [P, 2, 2, CTX], scope=con)
        ctok = sb("ctok", [P, 3, 4, P], scope=con)
        con.close()
        ffn1.close()

        mixo = ExitStack()
        hx_lo = sb("hx_lo", [P, KB, SEQ], F32R, scope=mixo)
        hx_hi = sb("hx_hi", [P, KB, SEQ], F32R, scope=mixo)
        mix = sb("mix", [P, KB, SEQ], scope=mixo)
        hgs = ExitStack()
        mask = sb("mask", [P, 7, P], I32, scope=hgs)
        x_cur = sb("x_cur", [P, 10], scope=hgs)
        s_cur = sb("s_cur", [P, 4, DK], scope=hgs)
        xk = sb("xk", [P, 2, 2, SEQ], scope=hgs)
        xa = sb("xa", [P, 2, 2, SEQ], scope=hgs)
        xe = sb("xe", [P, 2, 2, SEQ], scope=hgs)
        xv = sb("xv", [P, 2, SEQ], scope=hgs)
        xq = sb("xq", [P, 2, SEQ], scope=hgs)
        xg = sb("xg", [P, 2, SEQ], scope=hgs)
        eq = [sb(f"eq{n}", [P, 2, SEQ], scope=hgs) for n in range(2)]
        ek = [sb(f"ek{n}", [P, 2, SEQ], scope=hgs) for n in range(2)]
        lq = [sb(f"lq{n}", [P, 2, SEQ], scope=hgs) for n in range(2)]
        lk = [sb(f"lk{n}", [P, 2, SEQ], scope=hgs) for n in range(2)]
        prob = sb("prob", [P, 4, P], scope=hgs)
        cross = sb("cross", [P, 4, P], scope=hgs)
        vtok = sb("vtok", [P, 4, P], scope=hgs)
        osq = sb("osq", [P, 512], scope=hgs)
        onorm = sb("onorm", [P, 2, SEQ], scope=hgs)
        hgs.close()
        hys = ExitStack()
        dfty = sb("dfty", [P, T_COLS], scope=hys)
        y_cur = sb("y_cur", [P, 24], scope=hys)
        spec = sb("spec", [P, 2, 3, 2, 256], scope=hys)
        conv = sb("conv", [P, 3, 2, SEQ], scope=hys)
        ut = sb("ut", [P, TB, 256], scope=hys)
        prod = [sb(f"prod{n}", [P, 2, 256], scope=hys) for n in range(4)]
        yf = sb("yf", [P, 2, 2, 256], scope=hys)
        zg = sb("zg", [P, 2, SEQ], scope=hys)
        hys.close()
        outs = ExitStack()
        m_hi = sb("m_hi", [P, KB, SEQ], F32R, scope=outs)
        m_lo = sb("m_lo", [P, KB, SEQ], F32R, scope=outs)
        outs.close()
        mixo.close()
        f2 = ExitStack()
        h2_hi = sb("h2_hi", [P, KB, SEQ], F32R, scope=f2)
        h2_lo = sb("h2_lo", [P, KB, SEQ], F32R, scope=f2)
        s2 = [sb(f"s2_{b}", [P, SEQ], scope=f2) for b in range(2)]
        g2 = [sb(f"g2_{b}", [P, SEQ], scope=f2) for b in range(2)]
        g2_hi = [sb(f"g2_hi{b}", [P, SEQ], F32R, scope=f2) for b in range(2)]
        g2_lo = [sb(f"g2_lo{b}", [P, SEQ], F32R, scope=f2) for b in range(2)]
        xo = sb("xo", [P, KB, SEQ], scope=f2)
        xt = sb("xt", [P, TB, D], scope=f2)
        f2.close()

        bank = [life.enter_context(nc.psum_tensor(f"bank{n}", [P, 512], F32)) for n in range(8)]
        spec_dram = nc.dram_tensor("spec_spill", [2, P, 6, HY], F32, kind="Internal").ap()

        raw_in = [sem(f"raw_in{s}") for s in range(RING)]
        hi_done = sem("hi_done")
        lo_done = sem("lo_done")
        w_used = sem("w_used")
        ada_in = [sem(f"ada_in{s}") for s in range(RING)]
        wide_in = ada_in + [sem(f"wide_in{s}") for s in range(RING, WIDE)]
        ada_x = sem("ada_x")
        ada_c = sem("ada_c")
        ada_add = sem("ada_add")
        ada_used = sem("ada_used")
        ada_pe = sem("ada_pe")
        ada_out = sem("ada_out")

        small_in = sem("small_in")
        x_in = sem("x_in")
        y_in = sem("y_in")
        tab_in = sem("tab_in")
        memsets = sem("memsets")
        rows_t = sem("rows_t")
        cols_done = sem("cols_done")
        silu_done = sem("silu_done")
        tr_done = sem("tr_done")
        tr_out = sem("tr_out")
        lb_act = sem("lb_act")
        lb_dve = sem("lb_dve")

        fm_pe = sem("fm_pe")
        fm_arg = sem("fm_arg")
        fm_sin = sem("fm_sin")
        fm_dve = sem("fm_dve")
        fs_in = sem("fs_in")
        fs_taps_pe = sem("fs_taps_pe")
        fs_taps = sem("fs_taps")
        fs_abs = sem("fs_abs")
        fs_l1 = sem("fs_l1")
        fs_inv = sem("fs_inv")
        fs_norm = sem("fs_norm")
        fs_spec = sem("fs_spec")
        fs_out = sem("fs_out")
        fs_dma = sem("fs_dma")
        fs_tz = sem("fs_tz")
        fs_hyd = sem("fs_hyd")

        def norm_sems(tag, names):
            return {n: sem(f"{tag}_{n}") for n in names}

        STATS, SPLIT = ("sq", "sum", "mean", "root", "rstd"), ("xn", "hi", "lo")
        n1, nctx, n2 = [norm_sems(t, STATS + SPLIT) for t in ("n1", "nc", "n2")]
        nx, nf = norm_sems("nx", SPLIT), norm_sems("nf", STATS)
        mod_done = sem("mod_done")

        def ffn_sems(tag):
            return {n: sem(f"{tag}_{n}") for n in ("silu", "gmul", "ghi", "glo", "bdone", "bfree")}

        fa, fb_ = ffn_sems("ffn1"), ffn_sems("ffn2")

        def chain_sems(tag, names):
            return {n: sem(f"{tag}_{n}") for n in names}

        cs = chain_sems("ctx", ("cur", "gate", "log", "v", "k", "init", "sum", "sumb", "exp", "kd", "tpe", "tok", "st", "stout"))
        xs = chain_sems("hg", ("cur", "gate", "log", "v", "k", "init", "sum", "exp", "kq", "score", "pred",
                               "tpe", "tok", "ope", "osq", "mean", "root", "rstd", "on", "mix"))
        ys = chain_sems("hy", ("cur", "spec", "tab", "cb", "conv", "tpe", "ut", "specfree", "fft", "prod", "yf", "inv", "z"))
        msk_in = sem("msk_in")
        ms = chain_sems("wout", ("hi", "lo", "res"))
        fin = chain_sems("fin", ("o", "tr", "ev", "dma"))

        def load_unit(sy, un, j, src):
            n = un.number(j)
            if not (isinstance(n, int) and n < RING):
                sy.wait_ge(lo_done, n - RING + 1)
            a = src.shape[1]
            sy.dma_start(raw[un.slot(j)][:].rearrange("p (a c) -> p a c", a=a), src).then_inc(raw_in[un.slot(j)], 16)

        def col_src(w, kg, c0):
            return w[kg * 4 * P:(kg + 1) * 4 * P, bass.ds(c0, 256)].rearrange("(k p) c -> p k c", p=P)

        def row_src(w, chunk, q):
            return w[bass.ds(chunk * CHUNK, CHUNK), q * 512:(q + 1) * 512].rearrange("(f p) c -> p f c", p=P)

        def round_unit(ac, un, j):
            ac.wait_ge(raw_in[un.slot(j)], un.loads(j) * 16)
            ac.wait_ge(w_used, un.number(j) + 1)
            nc.scalar.activation(w_hi[un.slot(j)][:], raw[un.slot(j)][:], ACT.Copy).then_inc(hi_done, 1)

        def rest_unit(ve, un, j):
            ve.wait_ge(hi_done, un.number(j) + 1)
            nc.vector.tensor_tensor(w_lo[un.slot(j)][:], raw[un.slot(j)][:], w_hi[un.slot(j)][:].bitcast(F32),
                                    ALU.subtract).then_inc(lo_done, 1)

        def used(un, j):
            return un.number(j) + 1 + RING

        AHEAD = 3

        def three_pass(o, slot, c0, hi, lo, start, stop):
            nc.tensor.matmul(o, w_hi[slot][:, c0:c0 + P], hi, start=start, stop=False, skip_group_check=True)
            nc.tensor.matmul(o, w_hi[slot][:, c0:c0 + P], lo, start=False, stop=False, skip_group_check=True)
            return nc.tensor.matmul(o, w_lo[slot][:, c0:c0 + P], hi, start=False, stop=stop, skip_group_check=True)

        def col_unit(pe, un, j, kg, outs2, hi, lo, shared):
            pe.wait_ge(lo_done, un.number(j) + 1)
            for k in range(4):
                kb = 4 * kg + k
                for b in range(2):
                    last = three_pass(outs2[b], un.slot(j), k * 256 + b * P, hi(kb), lo(kb),
                                      kb == 0 and (b == 0 or not shared), kb == KB - 1)
            last.then_inc(w_used, 1)

        def square_block(ac, s, src, kb):
            if kb >= 2:
                ac.wait_ge(s["sum"], kb - 1)
            for t, part in enumerate(src):
                ins = nc.scalar.activation(sq[kb % 2][:, t * 256:(t + 1) * 256], part[:, kb, :], ACT.Square)
            ins.then_inc(s["sq"], 1)

        def sum_block(ve, s, kb, ntok):
            ve.wait_ge(s["sq"], kb + 1)
            if kb == 0:
                nc.vector.tensor_copy(sq_sum[:, 0:ntok], sq[0][:, 0:ntok]).then_inc(s["sum"], 1)
            else:
                ve.wait_ge(s["sum"], kb)
                nc.vector.tensor_tensor(sq_sum[:, 0:ntok], sq_sum[:, 0:ntok], sq[kb % 2][:, 0:ntok],
                                        ALU.add).then_inc(s["sum"], 1)

        def root_act(ac, s, ntok):
            ac.wait_ge(s["mean"], 1)
            nc.scalar.activation(root[:, 0:ntok], bank[7][:, 0:ntok], ACT.Sqrt, bias=EPS).then_inc(s["root"], 1)

        def rstd_dve(ve, s, order):
            ve.wait_ge(s["root"], 1)
            for t in order:
                nc.vector.reciprocal(rstd[:, t * 256:(t + 1) * 256], root[:, t * 256:(t + 1) * 256]).then_inc(s["rstd"], 1)

        def norm_pe(pe, s, ntok):
            pe.wait_ge(s["sum"], KB)
            nc.tensor.matmul(bank[7][:, 0:ntok], ones_d[:], sq_sum[:, 0:ntok], start=True, stop=True).then_inc(s["mean"], 1)

        def modulate_dve(ve, s, which, src, lo, tcs, r0=0, halves_done=1):
            shift = (0, 3, 6)[which]
            ve.wait_ge(s["rstd"], halves_done)

            def scaled(kb):
                if kb >= 2:
                    ve.wait_ge(s["lo"], kb - 1)
                for t, part in enumerate(src):
                    ins = nc.vector.scalar_tensor_tensor(
                        out=xn[kb % 2][:, t * 256:(t + 1) * 256], in0=part[:, kb, :],
                        scalar=scale_a[:, which, kb, tcs[t]:tcs[t] + 1], in1=rstd[:, r0 + t * 256:r0 + (t + 1) * 256],
                        op0=ALU.mult, op1=ALU.mult)
                ins.then_inc(s["xn"], 1)

            scaled(0)
            for kb in range(KB):
                if kb + 1 < KB:
                    scaled(kb + 1)
                ve.wait_ge(s["hi"], kb + 1)
                for t in range(len(src)):
                    ins = nc.vector.scalar_tensor_tensor(
                        out=lo(t, kb), in0=xn[kb % 2][:, t * 256:(t + 1) * 256],
                        scalar=mods[:, shift, kb, tcs[t]:tcs[t] + 1], in1=s["hi_ap"](t, kb).bitcast(F32),
                        op0=ALU.add, op1=ALU.subtract)
                ins.then_inc(s["lo"], 1)

        def modulate_act(ac, s, which, hi, tcs):
            shift = (0, 3, 6)[which]
            for kb in range(KB):
                ac.wait_ge(s["xn"], kb + 1)
                for t in range(len(tcs)):
                    ins = nc.scalar.activation(hi(t, kb), xn[kb % 2][:, t * 256:(t + 1) * 256], ACT.Identity,
                                               bias=mods[:, shift, kb, tcs[t]:tcs[t] + 1])
                ins.then_inc(s["hi"], 1)

        def column(vectors, kb, t):
            return vectors[:, bass.ds(kb, 1), t:t + 1].rearrange("p a c -> p (a c)")

        n1["hi_ap"] = lambda t, kb: h1_hi[:, t, kb, :]
        nctx["hi_ap"] = lambda t, kb: hc_hi[:, kb, :]
        n2["hi_ap"] = lambda t, kb: h2_hi[:, kb, :]

        def ffn_loops(eng, base, body, loops, before=lambda ada: None):
            start = 0
            for count, ada in loops:
                before(ada)
                with eng.Fori(0, count) as it:
                    body(Units(base + 8 + 12 * start, it, 12), it + start if start else it, ada, it)
                start += count

        F1_LOOPS = ((ADA_BOTH, 2), (ADA_LATENT, 1), (N_CHUNK - 1 - ADA_BOTH - ADA_LATENT, 0))
        F2_LOOPS = ((N_CHUNK - 1, 0),)

        def ffn_sync(sy, base, w1, w3, w2, loops):
            un = Units(base)
            for j in range(8):
                load_unit(sy, un, j, col_src(w1 if j < 4 else w3, j % 4, 0))

            def body(un, c, ada, it):
                for j in range(12):
                    if j < 8:
                        load_unit(sy, un, j, col_src(w1 if j < 4 else w3, j % 4, (c + 1) * CHUNK))
                    else:
                        load_unit(sy, un, j, row_src(w2, c, j - 8))
                    for m in ada_at(j - 3) if ada else ():
                        sy.wait_ge(ada_x, c * KB + (WIDE + ADA_FIRST_H * ADA_EW + m - 3))
                        if ada == 2:
                            sy.wait_ge(ada_c, c * KB + (WIDE + ADA_FIRST_H * ADA_EW + m - 3))
                        load_ada(sy, m, c + ADA_FIRST_H)

            def before(ada):
                if ada == 1:
                    sy.wait_ge(ada_c, WIDE + ADA_FIRST_H * ADA_EW + ADA_BOTH * KB)

            if len(loops) > 1:
                sy.wait_ge(ada_pe, 1 + ADA_FIRST_H)
            ffn_loops(sy, base, body, loops, before)
            un = Units(base + 8 + 12 * (N_CHUNK - 1))
            for j in range(4):
                load_unit(sy, un, j, row_src(w2, N_CHUNK - 1, j))

        ada_w = i["ada_w"][0]

        def ada_at(j):
            return range(2 * j, 2 * j + 2) if 0 <= j < 8 else ()

        def load_ada(sy, m, half):
            sy.dma_start(ada_raw[m % RING][:], ada_w[m % KB * P:(m % KB + 1) * P, bass.ds(half * HALF, HALF)]
                         ).then_inc(ada_in[m % RING], 16)

        def ada_landed(eng, m, it):
            before = 2 * ADA_BODY // WIDE
            eng.wait_ge(ada_in[m % RING], (it * (KB // RING) + (before + m // RING + 1)) * 16)

        def wide_landed(eng, m, it):
            eng.wait_ge(wide_in[m % WIDE], (it * (ADA_BODY // WIDE) + (m // WIDE + 1)) * 16)

        def ew_before(m):
            return sum(n % KB not in ADA_PE for n in range(m))

        def pe_before(m):
            return m - ew_before(m)

        def load_wide(sy, m, it):
            last = m - WIDE
            wrap = ADA_BODY if last < 0 else 0
            if (last + wrap) % KB in ADA_PE:
                value = pe_before(last + wrap + 1) - (pe_before(ADA_BODY) if wrap else 0)
                sy.wait_ge(ada_used, it * pe_before(ADA_BODY) + (WIDE + value))
            else:
                value = ew_before(last + wrap + 1) - (ew_before(ADA_BODY) if wrap else 0)
                sy.wait_ge(ada_x, it * ew_before(ADA_BODY) + (WIDE + value))
                sy.wait_ge(ada_c, it * ew_before(ADA_BODY) + (WIDE + value))
            sy.dma_start(ada_wide[m % WIDE][:], ada_w[m % KB * P:(m % KB + 1) * P,
                                                     bass.ds((it * 3 + m // KB) * HALF, HALF)]).then_inc(wide_in[m % WIDE], 16)

        def ada_vector(ve, src, sums, kb, x_done):
            if kb == 0:
                nc.vector.tensor_scalar(sums[0], src, silu_c[:, kb, 0:1], None, ALU.mult).then_inc(ada_x, 1)
            else:
                ve.wait_ge(ada_x, x_done)
                nc.vector.scalar_tensor_tensor(out=sums[0], in0=src, scalar=silu_c[:, kb, 0:1],
                                               in1=sums[0], op0=ALU.mult, op1=ALU.add).then_inc(ada_x, 1)

        def ada_scalar(ac, src, sums, kb, prod, added):
            if kb:
                ac.wait_ge(ada_add, added)
            nc.scalar.activation(prod if kb else sums[1], src, ACT.Copy, scale=silu_c[:, kb, 1:2]).then_inc(ada_c, 1)

        def ada_gpsimd(po, sums, prod, c_done, added):
            po.wait_ge(ada_c, c_done)
            po.wait_ge(ada_add, added)
            nc.gpsimd.tensor_tensor(sums[1], sums[1], prod, ALU.add).then_inc(ada_add, 1)

        def ada_total(pe, sums, to, streams, fresh):
            for b in range(HALF // P):
                for t in range(streams):
                    ins = nc.tensor.matmul(bank[to][:, 2 * b + t:2 * b + t + 1], sums[t][:, b * P:(b + 1) * P],
                                           ones_1[:, 0:1], start=fresh and b == 0 and t == 0, stop=True,
                                           skip_group_check=True)
            ins.then_inc(ada_pe, 1)

        mods_flat = mods[:].rearrange("p m k t -> p (m k) t")

        def ada_take(ve, half, to, streams):
            ve.wait_ge(ada_pe, half + 2)
            nc.vector.tensor_copy(mods_flat[:, bass.ds(half * 8, 8), 0:streams],
                                  bank[to][:, 0:16].rearrange("p (b t) -> p b t", t=2)[:, :, 0:streams]).then_inc(ada_out, 1)

        DOWN = {512: (4, 5, 6), 256: (4, 5, 6, 7)}

        def up_bank(b, ntok):
            return bank[b][:, 0:ntok] if ntok == 512 else bank[b // 2][:, b % 2 * 256:(b % 2 + 1) * 256]

        def ffn_pe(pe, s, base, hi, lo, g_hi, g_lo, ntok, loops, split):
            downs = DOWN[ntok]

            def out(b):
                return up_bank(b, ntok)

            def up(un, j, c):
                if c is not None and j in (0, 4):
                    pe.wait_ge(s["silu"] if j == 0 else s["gmul"], c * 2 + 2)
                b0 = 0 if j < 4 else 2
                col_unit(pe, un, j, j % 4, [out(b0), out(b0 + 1)], hi, lo, ntok == 256)

            def down(un, j, jj, c):
                if jj == 0:
                    pe.wait_ge(s["glo"], c * 2 + 2)
                pe.wait_ge(lo_done, un.number(j) + 1)
                for q in range(4):
                    d = 4 * jj + q
                    before = d - len(downs) if d >= len(downs) else 15 - (15 - d) % len(downs) - KB
                    pe.wait_ge(s["bfree"], c * KB + (before + 1 + KB))
                    for f in range(2):
                        last = three_pass(bank[downs[d % len(downs)]][:, 0:ntok], un.slot(j), f * 512 + q * P,
                                          g_hi[f][:], g_lo[f][:], f == 0, f == 1)
                    if q < 3:
                        last.then_inc(s["bdone"], 1)
                    else:
                        last.then_inc(w_used, 1)

            un = Units(base)
            for j in range(8):
                if j < 4:
                    pe.wait_ge(split, 4 * (j + 1))
                up(un, j, None)

            def body(un, c, ada, it):
                for j in range(12):
                    if j < 8:
                        up(un, j, c)
                    else:
                        down(un, j, j - 8, c)
                    if ada and j == 10:
                        pe.wait_ge(ada_x, c * KB + (WIDE + ADA_FIRST_H * ADA_EW + KB))
                        if ada == 2:
                            pe.wait_ge(ada_add, c * (KB - 1) + (3 + ADA_FIRST_H * (ADA_EW - 1) + KB - 1))
                        pe.wait_ge(ada_out, c + (ADA_FIRST_H + 1))
                        ada_total(pe, ada_sum[0], 7, ada, True)

            ffn_loops(pe, base, body, loops)
            un = Units(base + 8 + 12 * (N_CHUNK - 1))
            for j in range(4):
                down(un, j, j, N_CHUNK - 1)

        def ffn_act(ac, s, base, sil, g, g_hi, ntok, loops, norm, res):
            def silu(un, j, c):
                ac.wait_ge(w_used, used(un, j))
                for b in range(2):
                    if not (isinstance(c, int) and c == 0):
                        ac.wait_ge(s["gmul"], c * 2 + (b + 1 - 2))
                    nc.scalar.activation(sil[b][:], up_bank(b, ntok), ACT.Silu).then_inc(s["silu"], 1)

            def ghi(c):
                for b in range(2):
                    ac.wait_ge(s["gmul"], c * 2 + (b + 1))
                    nc.scalar.activation(g_hi[b][:], g[b][:], ACT.Copy).then_inc(s["ghi"], 1)

            un = Units(base)
            for j in range(8):
                round_unit(ac, un, j + AHEAD)
                if j == 3:
                    silu(un, j, 0)
            ghi(0)

            def body(un, c, ada, it):
                for j in range(12):
                    round_unit(ac, un, j + AHEAD)
                    for m in ada_at(j) if ada == 2 else ():
                        ada_landed(ac, m, c)
                        if m == 0:
                            ac.wait_ge(ada_pe, c + (ADA_FIRST_H + 1))
                        added = 0 if m <= 1 else m - 2
                        ada_scalar(ac, ada_raw[m % RING][:], ada_sum[0], m, ada_prod[(m - 1) % 2], c * (KB - 1) + (3 + ADA_FIRST_H * (ADA_EW - 1) + added))
                    if j == 3:
                        silu(un, j, c + 1)
                    if j == 11:
                        ac.wait_ge(w_used, used(un, j))
                        ghi(c + 1)

            ffn_loops(ac, base, body, loops)
            un = Units(base + 8 + 12 * (N_CHUNK - 1))
            for j in range(4):
                if un.number(j + AHEAD) < U_END:
                    round_unit(ac, un, j + AHEAD)
                for kb in range(4 * j, 4 * j + 4):
                    ac.wait_ge(s["bfree"], KB * N_CHUNK + kb + 1)
                    square_block(ac, norm, res, kb)

        def ffn_dve(ve, s, base, sil, g, g_hi, g_lo, ntok, res, gt, loops, norm):
            ve.sem_inc(s["bfree"], KB)
            downs = DOWN[ntok]

            def gmul(un, j, c):
                ve.wait_ge(w_used, used(un, j))
                for b in range(2):
                    ve.wait_ge(s["silu"], c * 2 + (b + 1))
                    nc.vector.tensor_tensor(g[b][:], sil[b][:], up_bank(2 + b, ntok), ALU.mult).then_inc(s["gmul"], 1)

            def glo(c):
                for b in range(2):
                    ve.wait_ge(s["ghi"], c * 2 + (b + 1))
                    nc.vector.tensor_tensor(g_lo[b][:], g[b][:], g_hi[b][:].bitcast(F32), ALU.subtract).then_inc(s["glo"], 1)

            def add(un, j, jj, c, norm=None):
                if jj == 0:
                    ve.wait_ge(s["bfree"], c * KB + KB)
                for q in range(4):
                    d = 4 * jj + q
                    if q < 3:
                        ve.wait_ge(s["bdone"], c * 12 + (3 * jj + q + 1))
                    else:
                        ve.wait_ge(w_used, used(un, j))
                    for t, part in enumerate(res):
                        ins = nc.vector.scalar_tensor_tensor(
                            out=part[:, d, :], in0=bank[downs[d % len(downs)]][:, t * 256:(t + 1) * 256],
                            scalar=gate[:, gt, d, t:t + 1], in1=part[:, d, :], op0=ALU.mult, op1=ALU.add)
                    ins.then_inc(s["bfree"], 1)
                    if norm and d:
                        sum_block(ve, norm, d - 1, ntok)

            un = Units(base)
            for j in range(8):
                rest_unit(ve, un, j + AHEAD)
            gmul(un, 7, 0)
            glo(0)

            def body(un, c, ada, it):
                for j in range(12):
                    rest_unit(ve, un, j + AHEAD)
                    if j == 7:
                        gmul(un, j, c + 1)
                    if j >= 8:
                        add(un, j, j - 8, c)
                    for m in ada_at(j) if ada else ():
                        ada_landed(ve, m, c)
                        if m == 0:
                            ve.wait_ge(ada_pe, c + (ADA_FIRST_H + 1))
                        ada_vector(ve, ada_raw[m % RING][:], ada_sum[0], m, c * KB + (WIDE + ADA_FIRST_H * ADA_EW + m))
                if ada:
                    ada_take(ve, c + ADA_FIRST_H, 7, ada)
                glo(c + 1)

            ffn_loops(ve, base, body, loops)
            un = Units(base + 8 + 12 * (N_CHUNK - 1))
            for j in range(4):
                if un.number(j + AHEAD) < U_END:
                    rest_unit(ve, un, j + AHEAD)
                add(un, j, j, N_CHUNK - 1, norm)
            sum_block(ve, norm, KB - 1, ntok)

        def as_rows(ap, n):
            return ap.rearrange("(n p) -> n p", p=P) if len(ap.shape) == 1 else ap

        ROWS = [
            (0, 0, 128, i["ada_b"][0, 0:128 * P]),
            (1, 0, 16, i["ada_b"][0, 128 * P:144 * P]),
            (1, 16, 16, i["norm_ffn1"][0]), (1, 32, 16, i["norm_mix"][0]), (1, 48, 16, i["norm_ffn2"][0]),
            (1, 64, 16, i["final_norm"]), (1, 80, 8, i["hg_norm"][0]),
            (1, 88, 8, i["hg_lb_logits"][0, 0]), (1, 96, 8, i["hg_lb_logits"][0, 1]),
            (1, 104, 8, i["hg_lb_logits"][1, 0]), (1, 112, 8, i["hg_lb_logits"][1, 1]),
            (2, 0, 24, i["hy_conv_w"][0, 0]), (2, 24, 24, i["hy_conv_w"][0, 1]), (2, 48, 24, i["hy_conv_w"][0, 2]),
            (2, 72, 24, i["hy_conv_b"][0]), (2, 96, 16, i["c"][0]), (2, 112, 16, i["c_ctx"]),
        ]
        N_COLS = (128, 120, 128)
        C_GAIN = {0: 16, 1: 32, 2: 48}
        w_in = i["w_in"][0]
        CTX_COLS = (0, HG, 2 * HG)
        HG_COLS = (0, HG, 3 * HG, 2 * HG, 4 * HG)
        HY_COLS = (5 * HG, 5 * HG + HY, 5 * HG + 2 * HY)

        block = life.enter_context(nc.Block())

        @block.sync
        def _(sy):
            for tile, r, n, src in ROWS:
                sy.dma_start(rows[tile][r:r + n, :], as_rows(src, n)).then_inc(small_in, 16)
            sy.dma_start(ident[:], i["t_ident"]).then_inc(small_in, 16)
            sy.dma_start(emb[:], i["t_emb"]).then_inc(small_in, 16)
            sy.dma_start(fw1[:], i["filt_w1"][0]).then_inc(small_in, 16)
            sy.dma_start(fw23[:, 0, :], i["filt_w2"][0]).then_inc(small_in, 16)
            sy.dma_start(fw23[:, 1, :], i["filt_w3"][0]).then_inc(small_in, 16)
            for n, name in enumerate(("filt_b1", "filt_b2", "filt_b3", "filt_freq")):
                sy.dma_start(fbias[:, n:n + 1], i[name][0].rearrange("(p a) -> p a", a=1)).then_inc(small_in, 16)
            sy.dma_start(dft[:], i["t_dft"]).then_inc(tab_in, 16)
            sy.dma_start(window[:].rearrange("p a c -> p (a c)"), i["t_window"]).then_inc(tab_in, 16)
            sy.dma_start(xin[:], i["x"][0].rearrange("(a p) d -> p a d", p=P)).then_inc(x_in, 16)
            sy.dma_start(yin[:], i["ctx"][0].rearrange("(a p) d -> p a d", p=P)).then_inc(y_in, 16)
            with sy.Fori(0, 2) as filt:
                for half in range(2):
                    for o in range(24):
                        if o == 0:
                            sy.wait_ge(fs_taps_pe, filt * 8 + (half * 4 + 4))
                            for r in range(2):
                                sy.dma_start(fout[:, r, :],
                                             i["filt_w_out"][0][:, bass.ds(filt * (2 * HY) + (r * HY + half * 512), 512)]
                                             ).then_inc(fs_in, 16)
                        if o == 12:
                            sy.wait_ge(fs_norm, filt * 2 + (half + 1))
                            sy.dma_start(hyd_row[:], i["hy_d"][0][bass.ds(filt, 1), half * 512:(half + 1) * 512]
                                         ).then_inc(fs_hyd, 16)
                        load_wide(sy, 24 * half + o, filt)

            ffn_sync(sy, U_FFN1, i["ffn1_w1"][0], i["ffn1_w3"][0], i["ffn1_w2"][0], F1_LOOPS)
            with sy.Fori(0, PAIRS) as it:
                un = Units(U_CTX, it, 12)
                for j in range(12):
                    load_unit(sy, un, j, col_src(w_in, j % 4, it * 256 + CTX_COLS[j // 4]))
            with sy.Fori(0, PAIRS) as it:
                un = Units(U_HG, it, 20)
                for j in range(20):
                    load_unit(sy, un, j, col_src(w_in, j % 4, it * 256 + HG_COLS[j // 4]))
            with sy.Fori(0, PAIRS) as it:
                un = Units(U_HY, it, 12)
                for j in range(12):
                    load_unit(sy, un, j, col_src(w_in, j % 4, it * 256 + HY_COLS[j // 4]))
            with sy.Fori(0, KB // 4) as it:
                un = Units(U_OUT, it, 8)
                for j in range(8):
                    load_unit(sy, un, j, col_src(i["w_out"][0], j % 4, it * 512 + j // 4 * 256))
            ffn_sync(sy, U_FFN2, i["ffn2_w1"][0], i["ffn2_w3"][0], i["ffn2_w2"][0], F2_LOOPS)
            for q in range(4):
                sy.wait_ge(fin["ev"], 2 * (q + 1))
                sy.dma_start(out[0][:, q * 512:(q + 1) * 512].rearrange("(a p) d -> p a d", p=P),
                             xt[:, :, q * 512:(q + 1) * 512]).then_inc(fin["dma"], 16)
            sy.wait_ge(fin["dma"], 16 * 4)

        def halves(ap, m):
            return ap.rearrange("p h (n s m) -> p (h n) s m", s=2, m=m)

        def ctx_level(eng, ops, d, lv, done, it):
            if lv:
                eng.wait_ge(done, it * 16 + 2 * lv)
            total = (cg if lv == 0 else ctot[(lv - 1) % 2])[:, d].rearrange("p h t -> p (h t)")
            pair = total[:, 0:2 * SEQ >> lv].rearrange("p (n s) -> p n s", s=2)
            part = halves(csum[:, d], 1 << lv)[:, :, d, :]
            ops.tensor_tensor(part, part, pair[:, :, 1 - d:2 - d].to_broadcast(list(part.shape)), ALU.add).then_inc(done, 1)
            nxt = ctot[lv % 2][:, d].rearrange("p h t -> p (h t)")[:, 0:SEQ >> lv]
            ops.tensor_tensor(nxt, pair[:, :, 0], pair[:, :, 1], ALU.add).then_inc(done, 1)

        @block.gpsimd
        def _(po):
            nc.gpsimd.memset(ones_d[:], 1.0 / D).then_inc(memsets, 1)
            nc.gpsimd.memset(ones_h[:], 1.0 / DK).then_inc(memsets, 1)
            nc.gpsimd.memset(ones_1[:], 1.0).then_inc(memsets, 1)

            po.sem_inc(ada_add, 3)
            with po.Fori(0, 2) as filt:
                for m in range(ADA_BODY):
                    if m % KB and m % KB not in ADA_PE:
                        n = ew_before(m) - (m // KB + 1)
                        ada_gpsimd(po, ada_sum[m // KB], ada_prod[n % 3], filt * (3 * ADA_EW) + (WIDE + ew_before(m) + 1),
                                   filt * (3 * (ADA_EW - 1)) + (3 + n))
            with po.Fori(0, ADA_BOTH) as it:
                for m in range(1, KB):
                    ada_gpsimd(po, ada_sum[0], ada_prod[(m - 1) % 2], it * KB + (WIDE + ADA_FIRST_H * ADA_EW + m + 1),
                               it * (KB - 1) + (3 + ADA_FIRST_H * (ADA_EW - 1) + m - 1))

            with po.Fori(0, PAIRS) as it:
                po.wait_ge(cs["init"], it + 1)
                po.wait_ge(cs["log"], it * 2 + 1)
                for lv in range(LEVELS):
                    ctx_level(po, nc.gpsimd, 0, lv, cs["sum"], it)
                for d in range(2):
                    po.wait_ge(cs["exp"], it * 2 + (d + 1))
                    po.wait_ge(cs["k"], it * 2 + (d + 1))
                    nc.gpsimd.tensor_tensor(ckd[:, d], ck[:, d], cexp[:, d], ALU.mult).then_inc(cs["kd"], 1)

            po.dma_start(mask[:].rearrange("p a c -> p (a c)"), i["t_mask"]).then_inc(msk_in, 16)
            with po.Fori(0, PAIRS) as it:
                po.wait_ge(xs["init"], it + 1)
                po.wait_ge(xs["log"], it * 2 + 2)
                for lv in range(LEVELS):
                    m = 1 << lv
                    shape = [P, SEQ // m, m]
                    for d in range(2):
                        upto, behind = halves(xa[:, d], m), halves(xe[:, d], m)
                        tot = upto[:, :, d, m - 1:m] if d == 0 else upto[:, :, 1, 0:1]
                        other = upto[:, :, 1, m - 1:m] if d == 0 else upto[:, :, 0, 0:1]
                        po.wait_ge(xs["exp"], it * 18 + (2 * lv + d + 1))
                        if lv:
                            po.wait_ge(xs["sum"], it * 32 + (4 * lv + 2 * d - 2))
                        nc.gpsimd.tensor_tensor(behind[:, :, d, :], behind[:, :, d, :], other.to_broadcast(shape),
                                                ALU.add).then_inc(xs["sum"], 1)
                        po.wait_ge(xs["sum"], it * 32 + (4 * lv + 2 * d + 1))
                        nc.gpsimd.tensor_tensor(upto[:, :, 1 - d, :], upto[:, :, 1 - d, :], tot.to_broadcast(shape),
                                                ALU.add).then_inc(xs["sum"], 1)

            po.wait_ge(xs["mix"], 1 + PAIRS)
            po.dma_start(dfty[:], i["t_dft"]).then_inc(ys["tab"], 16)
            with po.Fori(0, PAIRS) as it:
                po.wait_ge(ys["specfree"], it + 1)
                for f in range(2):
                    po.dma_start(spec[:, f, :, :, :].rearrange("p a b c -> p (a b) c"),
                                 spec_dram[f][:, :, bass.ds(it * 256, 256)]).then_inc(ys["spec"], 16)

        SMALL = 16 * (len(ROWS) + 9)
        SUMS_AT = (6, 7, 6)
        SPEC_BANKS = (0, 1, 2, 3, 5)
        SPECTRA_AT = (16, 17, 18, 20, 21)

        @block.tensor
        def _(pe):
            pe.sem_inc(w_used, RING)
            pe.sem_inc(ada_used, WIDE)
            pe.sem_inc(ada_pe, 1)
            pe.sem_inc(fs_taps_pe, 4)
            pe.sem_inc(fs_spec, 5)
            pe.wait_ge(small_in, SMALL)
            for n in range(3):
                nc.tensor.transpose(bank[n][:, 0:N_COLS[n]], rows[n][0:N_COLS[n], :],
                                    ident[0:N_COLS[n], 0:N_COLS[n]]).then_inc(rows_t, 1)
            pe.wait_ge(cols_done, 3)
            def layer(n):
                if n:
                    pe.wait_ge(fm_sin, n)
                nc.tensor.matmul(bank[4][0:FILT_ORDER, 0:SEQ], fw1[:] if n == 0 else fw23[:, n - 1, :],
                                 emb[:] if n == 0 else hid[n - 1][:], start=True, stop=True).then_inc(fm_pe, 1)

            layer(0)
            for g in range(16):
                if g == 6:
                    layer(1)
                if g == 12:
                    layer(2)
                src = xin if g < 8 else yin
                pe.wait_ge(x_in if g < 8 else y_in, 16)
                if g >= 4:
                    pe.wait_ge(tr_out, g - 3)
                for k in range(2):
                    for a in range(TB):
                        kb = 2 * (g % 8) + k
                        ins = nc.tensor.transpose(bank[g % 4][:, k * 256 + a * P:k * 256 + (a + 1) * P],
                                                  src[:, a, kb * P:(kb + 1) * P], ident[:])
                ins.then_inc(tr_done, 1)
            pe.wait_ge(memsets, 3)
            norm_pe(pe, n1, 512)
            pe.wait_ge(silu_done, 1)
            pe.wait_ge(fm_sin, 3)
            pe.wait_ge(tab_in, 32)
            pe.wait_ge(n1["root"], 1)
            with pe.Fori(0, 2) as filt:
                for half in range(2):
                    def unit(m):
                        if m % KB == ADA_PE[0]:
                            pe.wait_ge(ada_out, filt * 3 + (2 if m // KB == 2 else 1))
                        wide_landed(pe, m, filt)
                        for b in range(HALF // P):
                            ins = nc.tensor.matmul(bank[SUMS_AT[m // KB]][:, 2 * b:2 * b + 2], ada_wide[m % WIDE][:, b * P:(b + 1) * P],
                                                   silu_c[:, m % KB, :], start=(m % KB == ADA_PE[0] and b == 0),
                                                   stop=False, skip_group_check=True)
                        ins.then_inc(ada_used, 1)

                    def total(h):
                        pe.wait_ge(ada_x, filt * (3 * ADA_EW) + (WIDE + (h + 1) * ADA_EW))
                        pe.wait_ge(ada_add, filt * (3 * (ADA_EW - 1)) + (3 + (h + 1) * (ADA_EW - 1)))
                        ada_total(pe, ada_sum[h], SUMS_AT[h], 2, False)

                    def raw_taps():
                        pe.wait_ge(fs_in, filt * 64 + (half * 32 + 32))
                        pe.wait_ge(fs_out, filt * 10 + (half * 5 + 2))
                        for a in range(TB):
                            for r in range(2):
                                nc.tensor.matmul(bank[2 * a + r][:], hid[2][:, a * P:(a + 1) * P], fout[:, r, :],
                                                 start=True, stop=True).then_inc(fs_taps_pe, 1)

                    def l1_norm():
                        pe.wait_ge(fs_abs, filt * 2 + (half + 1))
                        for n in range(4):
                            ins = nc.tensor.matmul(bank[4][:], ones_1[:], tabs[:, n // 2, n % 2, :], start=(n == 0), stop=(n == 3))
                        ins.then_inc(fs_l1, 1)

                    def spectra(o):
                        tab, part = ((T_COS, tsum), (T_COS + P, tsum), (T_SIN, tdif), (T_SIN + P, tdif), (T_COSN, tsum))[o]
                        pe.wait_ge(fs_norm, filt * 2 + (half + 2))
                        for a in range(TB):
                            step = 256 if tab != T_COSN else P
                            ins = nc.tensor.matmul(bank[SPEC_BANKS[o]][:],
                                                   dft[:, tab + a * step:tab + a * step + P], part[:, a, :],
                                                   start=(a == 0), stop=(a == 1))
                        ins.then_inc(fs_spec, 1)

                    for o in range(24):
                        m = 24 * half + o
                        if o == 3:
                            raw_taps()
                        if o == 10:
                            l1_norm()
                        if half and o == 3:
                            total(0)
                        if half and o == 15:
                            total(1)
                        if o in SPECTRA_AT:
                            spectra(SPECTRA_AT.index(o))
                        if m % KB in ADA_PE:
                            unit(m)
                    if half:
                        total(2)

            pe.wait_ge(fs_taps, 20)
            pe.wait_ge(fs_out, 22)
            ffn_pe(pe, fa, U_FFN1, lambda k: h1_hi[:, :, k, :], lambda k: h1_lo[:, :, k, :], g1_hi, g1_lo, 512, F1_LOOPS,
                   n1["lo"])

            norm_pe(pe, nctx, 512)
            with pe.Fori(0, PAIRS) as it:
                un = Units(U_CTX, it, 12)

                def to_tokens(n):
                    if n < 2:
                        pe.wait_ge(cs["kd"], it * 2 + (n + 1))
                    else:
                        pe.wait_ge(cs["v"], it + 2)
                    for h in range(2):
                        for a in range(TB):
                            src = cv[:, h, a * P:(a + 1) * P] if n == 2 else ckd[:, n, h, a * P:(a + 1) * P]
                            ins = nc.tensor.transpose(bank[3 + n][:, (2 * h + a) * P:(2 * h + a + 1) * P], src, ident[:])
                    ins.then_inc(cs["tpe"], 1)

                for j in range(12):
                    if j < 4:
                        pe.wait_ge(nctx["lo"], 4 * (j + 1))
                    if j == 8:
                        pe.wait_ge(cs["stout"], it + 1)
                    col_unit(pe, un, j, j % 4, [bank[j // 4][:, 0:256], bank[j // 4][:, 256:512]],
                             lambda k: hc_hi[:, k, :], lambda k: hc_lo[:, k, :], True)
                    if j == 10:
                        to_tokens(0)
                to_tokens(1)
                to_tokens(2)
                pe.wait_ge(cs["tok"], it * 3 + 3)
                for d in range(2):
                    for h in range(2):
                        for a in range(TB):
                            ins = nc.tensor.matmul(bank[6][:, (2 * d + h) * P:(2 * d + h + 1) * P],
                                                   ctok[:, d, 2 * h + a, :], ctok[:, 2, 2 * h + a, :],
                                                   start=(a == 0), stop=(a == 1))
                ins.then_inc(cs["st"], 1)

            pe.wait_ge(nx["lo"], KB + 2)
            with pe.Fori(0, PAIRS) as it:
                un = Units(U_HG, it, 20)

                def score(s):
                    pe.wait_ge(xs["kq"], it * 10 + (s + 1))
                    pe.wait_ge(xs["pred"], it * 9 + (s - 1) + 2)
                    for h in range(2):
                        for a in range(TB):
                            b = a if s < LEVELS else 1 - a
                            ins = nc.tensor.matmul(bank[5 + s % 2][:, (2 * h + a) * P:(2 * h + a + 1) * P],
                                                   lk[s % 2][:, h, a * P:(a + 1) * P], lq[s % 2][:, h, b * P:(b + 1) * P],
                                                   start=True, stop=True)
                    ins.then_inc(xs["score"], 1)

                for j in range(20):
                    if j == 8:
                        pe.wait_ge(xs["mix"], it + 1)
                    col_unit(pe, un, j, j % 4, [bank[j // 4][:, 0:256], bank[j // 4][:, 256:512]],
                             lambda k: hx_hi[:, k, :], lambda k: hx_lo[:, k, :], True)
                    if j >= 12:
                        score(j - 12)
                    if j == 17:
                        pe.wait_ge(xs["v"], it * 3 + 2)
                        for h in range(2):
                            for a in range(TB):
                                ins = nc.tensor.transpose(bank[7][:, (2 * h + a) * P:(2 * h + a + 1) * P],
                                                          xv[:, h, a * P:(a + 1) * P], ident[:])
                        ins.then_inc(xs["tpe"], 1)
                score(LEVELS)
                pe.wait_ge(xs["cur"], it + 1)
                pe.wait_ge(xs["tok"], it + 1)
                pe.wait_ge(xs["pred"], it * 9 + 10)
                for n in range(4):
                    if n == 1:
                        pe.wait_ge(xs["kq"], it * 10 + 10)
                    if n == 3:
                        pe.wait_ge(xs["pred"], it * 9 + 11)
                    for h in range(2):
                        for a in range(TB):
                            at = 2 * h + a
                            other = 2 * h + 1 - a
                            left, right = ((vtok[:, at, :], prob[:, at, :]),
                                           (s_cur[:, h, :], lq[1][:, h, a * P:(a + 1) * P]),
                                           (s_cur[:, 2 + h, :], lk[1][:, h, a * P:(a + 1) * P]),
                                           (vtok[:, other, :], cross[:, other, :]))[n]
                            ins = nc.tensor.matmul(bank[2][:, at * P:(at + 1) * P], left, right, start=(n == 0 and at == 0),
                                                   stop=(n == 3), skip_group_check=True)
                ins.then_inc(xs["ope"], 1)
                pe.wait_ge(xs["osq"], it + 1)
                nc.tensor.matmul(bank[7][:], ones_h[:], osq[:], start=True, stop=True).then_inc(xs["mean"], 1)

            HY_STEPS = {4: (0, 0), 5: (1, 0), 7: (2, 0), 9: (0, 1), 10: (1, 1)}
            with pe.Fori(0, PAIRS) as it:
                un = Units(U_HY, it, 12)

                def to_tokens(f):
                    if f == 0:
                        pe.wait_ge(ys["conv"], it * 12 + 4)
                    else:
                        pe.wait_ge(ys["z"], it * 2 + 3)
                    for a in range(TB):
                        for b in range(2):
                            src = conv[:, 0, b, a * P:(a + 1) * P] if f == 0 else zg[:, b, a * P:(a + 1) * P]
                            ins = nc.tensor.transpose(bank[3][:, a * 256 + b * P:a * 256 + (b + 1) * P], src, ident[:])
                    ins.then_inc(ys["tpe"], 1)

                def forward(f):
                    pe.wait_ge(ys["tab"], 16)
                    pe.wait_ge(ys["ut"], it * 2 + (f + 1))
                    for ri, tab in enumerate((T_COS, T_SINN)):
                        for b in range(2):
                            for a in range(TB):
                                ins = nc.tensor.matmul(bank[4 + ri][:, b * 256:(b + 1) * 256],
                                                       dfty[:, tab + a * 256 + b * P:tab + a * 256 + (b + 1) * P],
                                                       ut[:, a, :], start=(a == 0), stop=(a == 1))
                    ins.then_inc(ys["fft"], 1)

                def back(f):
                    pe.wait_ge(ys["yf"], it * 4 + (2 * f + 2))
                    for b in range(2):
                        for n, (ri, fb) in enumerate(((0, 0), (0, 1), (1, 0), (1, 1))):
                            tab = (T_ITR, T_ITI)[ri] + fb * 256
                            ins = nc.tensor.matmul(bank[6][:, b * 256:(b + 1) * 256], yf[:, ri, fb, b * P:(b + 1) * P],
                                                   dfty[:, tab:tab + 256], start=(n == 0), stop=(n == 3))
                    ins.then_inc(ys["inv"], 1)

                for j in range(12):
                    if j in (0, 7):
                        pe.wait_ge(ys["z"], it * 2 + (2 if j else 1))
                    col_unit(pe, un, j, j % 4, [bank[j // 4][:, 0:256], bank[j // 4][:, 256:512]],
                             lambda k: hx_hi[:, k, :], lambda k: hx_lo[:, k, :], True)
                    if j in HY_STEPS:
                        step, f = HY_STEPS[j]
                        (to_tokens, forward, back)[step](f)
                back(1)

            with pe.Fori(0, KB // 4) as it:
                un = Units(U_OUT, it, 8)
                for j in range(8):
                    if j < 4:
                        pe.wait_ge(ms["lo"], j + 1)
                    if j % 4 == 0:
                        pe.wait_ge(ms["res"], it * 2 + (j // 4 + 1))
                    col_unit(pe, un, j, j % 4, [bank[j // 4][:, 0:256], bank[j // 4][:, 256:512]],
                             lambda k: m_hi[:, k, :], lambda k: m_lo[:, k, :], True)

            pe.wait_ge(n2["sum"], 1 + KB // 2)
            for t in range(2):
                ins = nc.tensor.matmul(bank[7][:, 0:256], ones_d[:], sq_sum[:, t * 256:(t + 1) * 256], start=(t == 0), stop=(t == 1))
            ins.then_inc(n2["mean"], 1)
            ffn_pe(pe, fb_, U_FFN2, lambda k: h2_hi[:, k, :], lambda k: h2_lo[:, k, :], g2_hi, g2_lo, 256, F2_LOOPS,
                   n2["lo"])
            norm_pe(pe, nf, 256)
            for g in range(8):
                q, a = g // 2, g % 2
                pe.wait_ge(fin["o"], 4 * q + 4)
                if g >= 4:
                    pe.wait_ge(fin["ev"], g - 3)
                for k in range(4):
                    ins = nc.tensor.transpose(bank[g % 4][:, k * P:(k + 1) * P], xo[:, 4 * q + k, a * P:(a + 1) * P], ident[:])
                ins.then_inc(fin["tr"], 1)

        @block.scalar
        def _(ac):
            ac.sem_inc(cs["stout"], 1)
            ac.sem_inc(cs["v"], 1)
            ac.sem_inc(fs_out, 2)
            ac.sem_inc(ada_c, WIDE)
            ac.wait_ge(cols_done, 3)
            nc.scalar.activation(silu_c[:, :, 0], cols[2][:, 96:112], ACT.Silu)
            nc.scalar.activation(silu_c[:, :, 1], cols[2][:, 112:128], ACT.Silu).then_inc(silu_done, 1)
            ac.wait_ge(lb_dve, 3)
            nc.scalar.activation(lbe[:], lbe[:], ACT.Exp).then_inc(lb_act, 1)
            for g in range(16):
                if g % 6 == 0:
                    n = g // 6
                    ac.wait_ge(fm_dve, 6 * (n + 1))
                    nc.scalar.activation(hid[n][:], ang[n % 2][:], ACT.Sin).then_inc(fm_sin, 1)
                ac.wait_ge(tr_done, g + 1)
                dst = x_res if g < 8 else y_res
                nc.scalar.activation(dst[:, 2 * (g % 8):2 * (g % 8) + 2, :].rearrange("p a c -> p (a c)"),
                                     bank[g % 4][:], ACT.Copy).then_inc(tr_out, 1)
            ac.wait_ge(tr_out, 16)
            for kb in range(KB):
                square_block(ac, n1, [x_res, y_res], kb)
            root_act(ac, n1, 512)
            with ac.Fori(0, 2) as filt:
                for half in range(2):
                    for o in range(24):
                        m = 24 * half + o
                        if o == 7:
                            ac.wait_ge(fs_tz, filt * 2 + (half + 1))
                            nc.scalar.activation(tabs[:], taps[:], ACT.Abs).then_inc(fs_abs, 1)
                        if o >= 19:
                            q = o - 19
                            if half and q == 0:
                                ac.wait_ge(fs_dma, filt * 64 + 32)
                            ac.wait_ge(fs_spec, filt * 10 + (half * 5 + q + 6))
                            nc.scalar.activation(spec_out[:, q, :], bank[SPEC_BANKS[q]][:], ACT.Copy
                                                 ).then_inc(fs_out, 1)
                            if q == 4:
                                ac.wait_ge(fs_out, filt * 10 + (half * 5 + 7))
                                dst = spec_dram[bass.ds(filt, 1)].rearrange("a p s c -> (a p) s c")[:, :, half * 512:(half + 1) * 512]
                                ac.dma_start(dst[:, 0:5, :], spec_out[:]).then_inc(fs_dma, 16)
                                ac.dma_start(dst[:, 5:6, :], spec_out[:, 1:2, :]).then_inc(fs_dma, 16)
                        if m % KB not in ADA_PE:
                            wide_landed(ac, m, filt)
                            n = ew_before(m) - (m // KB + 1)
                            ada_scalar(ac, ada_wide[m % WIDE][:], ada_sum[m // KB], m % KB, ada_prod[n % 3],
                                       filt * (3 * (ADA_EW - 1)) + (n + 1))
                ac.wait_ge(fs_dma, filt * 64 + 64)
            ac.wait_ge(ada_pe, 1 + ADA_FIRST_H)
            for j in range(AHEAD):
                round_unit(ac, Units(0), j)
            modulate_act(ac, n1, 0, n1["hi_ap"], (0, 1))
            ffn_act(ac, fa, U_FFN1, s1, g1, g1_hi, 512, F1_LOOPS, nctx, [x_res, y_res])

            root_act(ac, nctx, 512)
            modulate_act(ac, nctx, 1, nctx["hi_ap"], (1,))

            def gates(s, d, b, k_ap, g_ap, value):
                ac.wait_ge(w_used, value)
                nc.scalar.activation(k_ap, bank[b][:], ACT.Sigmoid, scale=-1.0)
                nc.scalar.activation(g_ap, bank[b][:], ACT.Sigmoid).then_inc(s["gate"], 1)

            def keys_logs(s, it, d, k_ap, g_ap, cur):
                ac.wait_ge(s["gate"], it * 2 + (d + 1))
                ac.wait_ge(s["cur"], it + 1)
                for h in range(2):
                    ins = nc.scalar.activation(g_ap[:, h * 256:(h + 1) * 256], g_ap[:, h * 256:(h + 1) * 256], ACT.Ln,
                                               scale=cur[:, 4 + 2 * d + h:5 + 2 * d + h], bias=cur[:, 2 * d + h:2 * d + h + 1])
                ins.then_inc(s["log"], 1)
                for h in range(2):
                    ins = nc.scalar.activation(k_ap[:, h * 256:(h + 1) * 256], k_ap[:, h * 256:(h + 1) * 256], ACT.Copy,
                                               scale=cur[:, 4 + 2 * d + h:5 + 2 * d + h])
                ins.then_inc(s["k"], 1)

            def flat(ap):
                return ap.rearrange("p h t -> p (h t)")

            with ac.Fori(0, PAIRS) as it:
                un = Units(U_CTX, it, 12)

                def decay(d):
                    ac.wait_ge(cs["sumb" if d else "sum"], it * 16 + 16)
                    nc.scalar.activation(cexp[:, d], csum[:, d], ACT.Exp).then_inc(cs["exp"], 1)

                def tokens(n):
                    ac.wait_ge(cs["tpe"], it * 3 + (n + 1))
                    nc.scalar.activation(flat(ctok[:, n]), bank[3 + n][:], ACT.Copy).then_inc(cs["tok"], 1)

                for j in range(12):
                    round_unit(ac, un, j + AHEAD)
                    if j in (4, 6, 8, 10):
                        k = (j - 4) // 2
                        ac.wait_ge(nx["xn"], it * 4 + (k + 1))
                        nc.scalar.activation(hx_hi[:, bass.ds(it * 4 + k, 1), :].rearrange("p a c -> p (a c)"),
                                             xn[k % 2][:, 0:256], ACT.Identity, bias=column(mods[:, 3], it * 4 + k, 0)
                                             ).then_inc(nx["hi"], 1)
                    if j in (3, 7):
                        d = j // 4
                        gates(cs, d, d, flat(ck[:, d]), flat(cg[:, d]), used(un, j))
                    if j in (4, 8):
                        d = j // 4 - 1
                        keys_logs(cs, it, d, flat(ck[:, d]), flat(cg[:, d]), c_cur)
                    if j == 9:
                        decay(0)
                    if j == 10:
                        decay(1)
                    if j == 11:
                        tokens(0)
                ac.wait_ge(w_used, used(un, 11))
                nc.scalar.activation(flat(cv[:]), bank[2][:], ACT.Copy).then_inc(cs["v"], 1)
                tokens(1)
                tokens(2)
                ac.wait_ge(cs["st"], it + 1)
                nc.scalar.activation(states[:, bass.ds(it, 1)].rearrange("p a n c -> p (a n c)"), bank[6][:], ACT.Copy
                                     ).then_inc(cs["stout"], 1)

            EXP_AT = (8, 10, 12, 13, 14, 15, 16, 17, 18)
            with ac.Fori(0, PAIRS) as it:
                un = Units(U_HG, it, 20)

                def decays(lv):
                    s = lv + 1
                    if lv == 0:
                        ac.wait_ge(xs["log"], it * 2 + 2)
                        ac.wait_ge(xs["init"], it + 1)
                    if lv >= 2:
                        ac.wait_ge(xs["kq"], it * 10 + (s - 1))
                    for d in range(2):
                        if lv:
                            ac.wait_ge(xs["sum"], it * 32 + (4 * lv + 2 * d - 2))
                        if lv < LEVELS:
                            m = 1 << lv
                            nc.scalar.activation(halves(eq[s % 2][:], m)[:, :, 1 - d, :], halves(xa[:, d], m)[:, :, 1 - d, :], ACT.Exp)
                            nc.scalar.activation(halves(ek[s % 2][:], m)[:, :, d, :], halves(xe[:, d], m)[:, :, d, :], ACT.Exp
                                                 ).then_inc(xs["exp"], 1)
                        else:
                            nc.scalar.activation((ek if d else eq)[1][:], xa[:, d], ACT.Exp).then_inc(xs["exp"], 1)

                for j in range(20):
                    round_unit(ac, un, j + AHEAD)
                    if j in (3, 7):
                        d = j // 4
                        gates(xs, d, d, flat(xk[:, d]), flat(xa[:, d]), used(un, j))
                    if j in (4, 8):
                        d = j // 4 - 1
                        keys_logs(xs, it, d, flat(xk[:, d]), flat(xa[:, d]), x_cur)
                    if j == 11:
                        ac.wait_ge(w_used, used(un, j))
                        nc.scalar.activation(flat(xq[:]), bank[2][:], ACT.Copy, scale=DK ** -0.5).then_inc(xs["v"], 1)
                    if j == 15:
                        ac.wait_ge(w_used, used(un, j))
                        nc.scalar.activation(flat(xv[:]), bank[3][:], ACT.Copy).then_inc(xs["v"], 1)
                    if j in EXP_AT:
                        decays(EXP_AT.index(j))
                    if j == 18:
                        ac.wait_ge(xs["tpe"], it + 1)
                        nc.scalar.activation(flat(vtok[:]), bank[7][:], ACT.Copy).then_inc(xs["tok"], 1)
                ac.wait_ge(w_used, used(un, 19))
                nc.scalar.activation(flat(xg[:]), bank[4][:], ACT.Silu).then_inc(xs["v"], 1)
                ac.wait_ge(xs["ope"], it + 1)
                nc.scalar.activation(osq[:], bank[2][:], ACT.Square).then_inc(xs["osq"], 1)
                ac.wait_ge(xs["mean"], it + 1)
                nc.scalar.activation(root[:], bank[7][:], ACT.Sqrt, bias=EPS).then_inc(xs["root"], 1)

            with ac.Fori(0, PAIRS) as it:
                un = Units(U_HY, it, 12)
                for j in range(12):
                    round_unit(ac, un, j + AHEAD)
                    if j % 4 == 3:
                        ac.wait_ge(w_used, used(un, j))
                        ac.wait_ge(ys["cur"], it + 1)
                        p = j // 4
                        for b in range(2):
                            c0 = p * 8 + b * 4
                            ins = nc.scalar.activation(conv[:, p, b, :], bank[p][:, b * 256:(b + 1) * 256], ACT.Identity,
                                                       scale=y_cur[:, c0 + 1:c0 + 2], bias=y_cur[:, c0 + 3:c0 + 4])
                        ins.then_inc(ys["cb"], 1)
                    if j in (5, 10):
                        ac.wait_ge(ys["tpe"], it * 2 + j // 5)
                        nc.scalar.activation(flat(ut[:]), bank[3][:], ACT.Copy).then_inc(ys["ut"], 1)

            ac.wait_ge(ys["z"], 2 + 2 * PAIRS)
            for n in range(4):
                nc.scalar.activation(m_hi[:, 4 * n:4 * n + 4, :], mix[:, 4 * n:4 * n + 4, :], ACT.Copy).then_inc(ms["hi"], 1)
            with ac.Fori(0, KB // 4) as it:
                un = Units(U_OUT, it, 8)
                for j in range(8):
                    round_unit(ac, un, j + AHEAD)
                    if j % 4 == 3:
                        b = j // 4
                        ac.wait_ge(ms["res"], it * 2 + (b + 3))
                        ac.wait_ge(n2["sum"], it * 2 + (b + 1))
                        nc.scalar.activation(sq[b], x_res[:, bass.ds(it * 4 + 2 * b, 2), :].rearrange("p a c -> p (a c)"),
                                             ACT.Square).then_inc(n2["sq"], 1)
            root_act(ac, n2, 256)
            modulate_act(ac, n2, 2, n2["hi_ap"], (0,))
            ffn_act(ac, fb_, U_FFN2, s2, g2, g2_hi, 256, F2_LOOPS, nf, [x_res])
            root_act(ac, nf, 256)
            for g in range(8):
                q, a = g // 2, g % 2
                ac.wait_ge(fin["tr"], g + 1)
                nc.scalar.activation(xt[:, a, q * 512:(q + 1) * 512], bank[g % 4][:], ACT.Copy).then_inc(fin["ev"], 1)

        @block.vector
        def _(ve):
            ve.sem_inc(ada_out, 1)
            ve.sem_inc(ada_x, WIDE)
            ve.sem_inc(fs_taps, 4)
            ve.sem_inc(fs_norm, 1)
            ve.sem_inc(xs["mix"], 1)
            ve.sem_inc(xs["pred"], 2)
            ve.sem_inc(ys["z"], 2)
            ve.sem_inc(ys["specfree"], 1)
            ve.sem_inc(ms["res"], 2)
            ve.sem_inc(nx["lo"], 2)
            for n in range(3):
                ve.wait_ge(rows_t, n + 1)
                nc.vector.tensor_copy(cols[n][:, 0:N_COLS[n]], bank[n][:, 0:N_COLS[n]]).then_inc(cols_done, 1)
            ve.wait_ge(cols_done, 3)
            logits = cols[1][:, 88:120].rearrange("p (d n h) -> p d n h", d=2, n=2)
            nc.vector.tensor_tensor(lbt[:], logits[:, :, 0], logits[:, :, 1], ALU.max).then_inc(lb_dve, 1)
            ve.wait_ge(lb_dve, 1)
            for n in range(2):
                nc.vector.tensor_tensor(lbe[:, n], logits[:, :, n], lbt[:], ALU.subtract).then_inc(lb_dve, 1)
            ve.wait_ge(lb_act, 1)
            nc.vector.tensor_tensor(lbt[:], lbe[:, 0], lbe[:, 1], ALU.add).then_inc(lb_dve, 1)
            ve.wait_ge(lb_dve, 4)
            nc.vector.reciprocal(lbt[:], lbt[:]).then_inc(lb_dve, 1)
            ve.wait_ge(lb_dve, 5)
            nc.vector.tensor_tensor(lb[:], lbe[:, 0], lbt[:], ALU.mult).then_inc(lb_dve, 1)
            ve.wait_ge(lb_dve, 6)
            for d in range(2):
                by_pair = lb[:, d, :].rearrange("p (a h) -> p a h", h=2)
                nc.vector.tensor_copy(hg_cols[:, :, 2 * d:2 * d + 2], by_pair)
                nc.vector.tensor_scalar(hg_cols[:, :, 4 + 2 * d:6 + 2 * d], by_pair, -1.0, 1.0, ALU.mult, ALU.add)
            nc.vector.tensor_copy(hg_cols[:, :, 8:10], cols[1][:, 80:88].rearrange("p (a h) -> p a h", h=2))
            for part in range(3):
                for w in range(4):
                    c0 = w * 24 + part * 8
                    dst = hy_cols[:, :, part * 8:(part + 1) * 8].rearrange("p a (b w) -> p a b w", w=4)[:, :, :, w]
                    ins = nc.vector.tensor_copy(dst, cols[2][:, c0:c0 + 8].rearrange("p (a b) -> p a b", b=2))
            ins.then_inc(lb_dve, 1)
            MAGIC = 1.5 * 2.0 ** 23
            C1 = 6.28125
            C2 = float(np.float32(TWO_PI - C1))
            C3 = float(np.float32(TWO_PI - C1 - C2))
            PI = float(np.nextafter(np.float32(np.pi), np.float32(0)))
            ve.wait_ge(small_in, SMALL)
            for n in range(3):
                ve.wait_ge(fm_pe, n + 1)
                r, a, k = ang[n % 2], ang[2], ang[3]
                nc.vector.tensor_scalar(a[:], bank[4][0:FILT_ORDER, 0:SEQ], fbias[:, n:n + 1], fbias[:, 3:4],
                                        ALU.add, ALU.mult).then_inc(fm_dve, 1)
                ve.wait_ge(fm_dve, 6 * n + 1)
                nc.vector.tensor_scalar(k[:], a[:], 1.0 / TWO_PI, MAGIC, ALU.mult, ALU.add).then_inc(fm_dve, 1)
                ve.wait_ge(fm_dve, 6 * n + 2)
                nc.vector.tensor_scalar(k[:], k[:], MAGIC, None, ALU.subtract).then_inc(fm_dve, 1)
                ve.wait_ge(fm_dve, 6 * n + 3)
                for m, (c, src) in enumerate(((C1, a), (C2, r))):
                    nc.vector.scalar_tensor_tensor(out=r[:], in0=k[:], scalar=-c, in1=src[:], op0=ALU.mult, op1=ALU.add
                                                   ).then_inc(fm_dve, 1)
                    ve.wait_ge(fm_dve, 6 * n + 4 + m)
                nc.vector.scalar_tensor_tensor(out=a[:], in0=k[:], scalar=-C3, in1=r[:], op0=ALU.mult, op1=ALU.add
                                               ).then_inc(fm_arg, 1)
                ve.wait_ge(fm_arg, n + 1)
                nc.vector.tensor_scalar(r[:], a[:], PI, -PI, ALU.min, ALU.max).then_inc(fm_dve, 1)
            for kb in range(KB):
                sum_block(ve, n1, kb, 512)
            rstd_dve(ve, n1, (0, 1))
            ve.wait_ge(tab_in, 32)
            with ve.Fori(0, 2) as filt:
                for half in range(2):
                    def window_taps():
                        for n in range(4):
                            ve.wait_ge(fs_taps_pe, filt * 8 + (half * 4 + n + 5))
                            nc.vector.tensor_tensor(taps[:, n // 2, n % 2, :], bank[n][:],
                                                    window[:, n // 2, half * 512:(half + 1) * 512], ALU.mult).then_inc(fs_taps, 1)
                        ve.wait_ge(fs_taps, filt * 8 + (half * 4 + 8))
                        nc.vector.memset(taps[0:1, 0, 1, :], 0.0).then_inc(fs_tz, 1)

                    def even_odd():
                        ve.wait_ge(fs_tz, filt * 2 + (half + 1))
                        ve.wait_ge(fs_spec, filt * 10 + (half * 5 + 5))
                        nc.vector.tensor_tensor(tsum[:], taps[:, :, 0, :], taps[:, :, 1, :], ALU.add)
                        nc.vector.tensor_tensor(tdif[:], taps[:, :, 1, :], taps[:, :, 0, :], ALU.subtract).then_inc(fs_inv, 1)

                    def inverse():
                        ve.wait_ge(fs_l1, filt * 2 + (half + 1))
                        nc.vector.reciprocal(l1inv[:], bank[4][:]).then_inc(fs_inv, 1)

                    def scale(a):
                        if a == 0:
                            ve.wait_ge(fs_inv, filt * 8 + (half * 4 + 2))
                        nc.vector.tensor_tensor(tsum[:, a, :], tsum[:, a, :], l1inv[:], ALU.mult)
                        nc.vector.tensor_tensor(tdif[:, a, :], tdif[:, a, :], l1inv[:], ALU.mult).then_inc(fs_inv, 1)

                    def direct():
                        ve.wait_ge(fs_inv, filt * 8 + (half * 4 + 4))
                        ve.wait_ge(fs_hyd, filt * 32 + (half * 16 + 16))
                        nc.vector.tensor_tensor(tsum[0:1, 0, :], tsum[0:1, 0, :], hyd_row[:], ALU.add).then_inc(fs_norm, 1)

                    for o in range(24):
                        m = 24 * half + o
                        if m % KB not in ADA_PE:
                            wide_landed(ve, m, filt)
                            ada_vector(ve, ada_wide[m % WIDE][:], ada_sum[m // KB], m % KB,
                                       filt * (3 * ADA_EW) + (WIDE + ew_before(m)))
                        if o == 4:
                            window_taps()
                        if o == 6:
                            even_odd()
                        if o == 11:
                            inverse()
                        if o in (12, 13):
                            scale(o - 12)
                        if o == 14:
                            direct()
                        if half and o == 5:
                            ada_take(ve, filt * 3, SUMS_AT[0], 2)
                        if half and o == 18:
                            ada_take(ve, filt * 3 + 1, SUMS_AT[1], 2)
                    if half:
                        ada_take(ve, filt * 3 + 2, SUMS_AT[2], 2)

            def finish_mods(m0, m1, both):
                for t in range(2):
                    for m in range(m0, m1 if t == 0 else both):
                        bias = cols[0][:, m * KB:(m + 1) * KB] if m < 8 else cols[1][:, 0:KB]
                        ins = nc.vector.tensor_tensor(mods[:, m, :, t], mods[:, m, :, t], bias, ALU.add)
                ins.then_inc(mod_done, 1)

            def norm_scale(which, m, streams):
                g = C_GAIN[which]
                for t in range(streams):
                    nc.vector.scalar_tensor_tensor(out=scale_a[:, which, :, t], in0=mods[:, m, :, t], scalar=1.0,
                                                   in1=cols[1][:, g:g + KB], op0=ALU.add, op1=ALU.mult)

            ve.wait_ge(ada_out, 1 + ADA_FIRST_H)
            finish_mods(0, ADA_FIRST, ADA_FIRST)
            ve.wait_ge(mod_done, 1)
            norm_scale(0, 1, 2)
            nc.vector.tensor_scalar(gate[:, 0], mods[:, 2], 0.5, None, ALU.mult).then_inc(mod_done, 1)
            for j in range(AHEAD):
                rest_unit(ve, Units(0), j)
            ve.wait_ge(mod_done, 2)
            modulate_dve(ve, n1, 0, [x_res, y_res], lambda t, kb: h1_lo[:, t, kb, :], (0, 1), 0, 2)
            ffn_dve(ve, fa, U_FFN1, s1, g1, g1_hi, g1_lo, 512, [x_res, y_res], 0, F1_LOOPS, nctx)

            ve.wait_ge(ada_out, 1 + 2 * N_MOD)
            finish_mods(ADA_FIRST, N_MOD, 5)
            ve.wait_ge(mod_done, 3)
            norm_scale(1, 4, 2)
            norm_scale(2, 7, 1)
            nc.vector.tensor_copy(gate_x[:], mods[:, 5, :, 0])
            nc.vector.tensor_scalar(gate[:, 2, :, 0], mods[:, 8, :, 0], 0.5, None, ALU.mult).then_inc(mod_done, 1)
            rstd_dve(ve, nctx, (1, 0))
            ve.wait_ge(mod_done, 4)
            modulate_dve(ve, nctx, 1, [y_res], lambda t, kb: hc_lo[:, kb, :], (1,), 256)
            with ve.Fori(0, PAIRS) as it:
                un = Units(U_CTX, it, 12)
                ve.wait_ge(cs["v"], it + 1)
                nc.vector.tensor_copy(c_cur[:], hg_cols[:, bass.ds(it, 1), :].rearrange("p a c -> p (a c)")).then_inc(cs["cur"], 1)
                for j in range(12):
                    rest_unit(ve, un, j + AHEAD)
                    if j in (3, 5, 7, 9):
                        k = (j - 3) // 2
                        ve.wait_ge(nctx["rstd"], 2)
                        ve.wait_ge(nctx["lo"], KB)
                        ve.wait_ge(nx["lo"], it * 4 + (k + 1))
                        nc.vector.scalar_tensor_tensor(
                            out=xn[k % 2][:, 0:256], in0=x_res[:, bass.ds(it * 4 + k, 1), :].rearrange("p a c -> p (a c)"),
                            scalar=column(scale_a[:, 1], it * 4 + k, 0), in1=rstd[:, 0:256], op0=ALU.mult, op1=ALU.mult
                            ).then_inc(nx["xn"], 1)
                    if j in (4, 6, 8, 10):
                        k = (j - 4) // 2
                        ve.wait_ge(nx["hi"], it * 4 + (k + 1))
                        nc.vector.scalar_tensor_tensor(
                            out=hx_lo[:, bass.ds(it * 4 + k, 1), :].rearrange("p a c -> p (a c)"), in0=xn[k % 2][:, 0:256],
                            scalar=column(mods[:, 3], it * 4 + k, 0),
                            in1=hx_hi[:, bass.ds(it * 4 + k, 1), :].rearrange("p a c -> p (a c)").bitcast(F32),
                            op0=ALU.add, op1=ALU.subtract).then_inc(nx["lo"], 1)
                    if j in (8, 9):
                        if j == 8:
                            ve.wait_ge(cs["log"], it * 2 + 2)
                        for lv in range(4 * (j - 8), 4 * (j - 7)):
                            ctx_level(ve, nc.vector, 1, lv, cs["sumb"], it)
                    if j == 2:
                        ve.wait_ge(cs["stout"], it + 1)
                        nc.vector.memset(csum[:], 0.0).then_inc(cs["init"], 1)
                        ve.wait_ge(cs["init"], it + 1)

            ve.wait_ge(cs["stout"], 1 + PAIRS)
            with ve.Fori(0, PAIRS) as it:
                un = Units(U_HG, it, 20)
                nc.vector.tensor_copy(s_cur[:].rearrange("p n c -> p (n c)"),
                                      states[:, bass.ds(it, 1)].rearrange("p a n c -> p (a n c)"))
                nc.vector.tensor_copy(x_cur[:], hg_cols[:, bass.ds(it, 1), :].rearrange("p a c -> p (a c)")).then_inc(xs["cur"], 1)
                nc.vector.memset(xe[:], 0.0).then_inc(xs["init"], 1)

                def keys(s):
                    b = s % 2
                    if s >= 2:
                        ve.wait_ge(xs["score"], it * 9 + (s - 1))
                    if s == 0:
                        ve.wait_ge(xs["k"], it * 2 + 2)
                        ve.wait_ge(xs["v"], it * 3 + 1)
                        nc.vector.tensor_tensor(lk[b][:], xk[:, 0], xk[:, 1], ALU.add)
                        nc.vector.tensor_copy(lq[b][:], xq[:]).then_inc(xs["kq"], 1)
                        return
                    ve.wait_ge(xs["exp"], it * 18 + 2 * s)
                    nc.vector.tensor_tensor(lq[b][:], xq[:], eq[b][:], ALU.mult)
                    if s <= LEVELS:
                        m = 1 << (s - 1)
                        for side in range(2):
                            ins = nc.vector.tensor_tensor(halves(lk[b][:], m)[:, :, side, :], halves(xk[:, side], m)[:, :, side, :],
                                                          halves(ek[b][:], m)[:, :, side, :], ALU.mult)
                    else:
                        ins = nc.vector.tensor_tensor(lk[b][:], xq[:], ek[b][:], ALU.mult)
                    ins.then_inc(xs["kq"], 1)

                def take(s):
                    ve.wait_ge(xs["score"], it * 9 + (s + 1))
                    scores = bank[5 + s % 2][:].rearrange("p (n c) -> p n c", n=4)
                    if s == 0:
                        nc.vector.tensor_tensor(prob[:], scores, ident[:].rearrange("p (a c) -> p a c", a=1).to_broadcast([P, 4, P]),
                                                ALU.mult).then_inc(xs["pred"], 1)
                    elif s < LEVELS:
                        ve.wait_ge(xs["pred"], it * 9 + (s + 2))
                        ve.wait_ge(msk_in, 16)
                        nc.vector.tensor_copy(spec_mark[:], ident[:, 0:1])
                        nc.vector.copy_predicated(prob[:], mask[:, s - 1:s, :].to_broadcast([P, 4, P]), scores
                                                  ).then_inc(xs["pred"], 1)
                    else:
                        nc.vector.tensor_copy(cross[:], scores).then_inc(xs["pred"], 1)

                for j in range(20):
                    if j >= 11:
                        keys(j - 11)
                    rest_unit(ve, un, j + AHEAD)
                    if j >= 13:
                        take(j - 13)
                keys(LEVELS + 1)
                take(LEVELS - 1)
                take(LEVELS)
                ve.wait_ge(xs["root"], it + 1)
                nc.vector.reciprocal(rstd[:], root[:]).then_inc(xs["rstd"], 1)
                ve.wait_ge(xs["rstd"], it + 1)
                for h in range(2):
                    ins = nc.vector.scalar_tensor_tensor(out=onorm[:, h, :], in0=bank[2][:, h * 256:(h + 1) * 256],
                                                         scalar=x_cur[:, 8 + h:9 + h], in1=rstd[:, h * 256:(h + 1) * 256],
                                                         op0=ALU.mult, op1=ALU.mult)
                ins.then_inc(xs["on"], 1)
                ve.wait_ge(xs["on"], it + 1)
                ve.wait_ge(xs["v"], it * 3 + 3)
                nc.vector.tensor_tensor(mix[:, bass.ds(it * 2, 2), :], onorm[:], xg[:], ALU.mult).then_inc(xs["mix"], 1)

            with ve.Fori(0, PAIRS) as it:
                un = Units(U_HY, it, 12)
                nc.vector.tensor_copy(y_cur[:], hy_cols[:, bass.ds(it, 1), :].rearrange("p a c -> p (a c)")).then_inc(ys["cur"], 1)

                def products(f):
                    if f == 0:
                        ve.wait_ge(ys["spec"], it * 32 + 32)
                    ve.wait_ge(ys["fft"], it * 2 + (f + 1))
                    re, im = (bank[4 + n][:].rearrange("p (b c) -> p b c", b=2) for n in range(2))
                    for n, (part, s) in enumerate(((re, 0), (im, 1), (re, 1), (im, 2))):
                        ins = nc.vector.tensor_tensor(prod[n][:], part, spec[:, f, s], ALU.mult)
                        if n % 2:
                            ins.then_inc(ys["prod"], 1)
                    for n in range(2):
                        ve.wait_ge(ys["prod"], it * 4 + (2 * f + n + 1))
                        nc.vector.tensor_tensor(yf[:, n], prod[2 * n][:], prod[2 * n + 1][:],
                                                ALU.add if n else ALU.subtract).then_inc(ys["yf"], 1)

                def gated(f):
                    ve.wait_ge(ys["inv"], it * 2 + (f + 1))
                    ve.wait_ge(ys["conv"], it * 12 + (12 if f else 8))
                    y = bank[6][:].rearrange("p (b c) -> p b c", b=2)
                    dst = mix[:, bass.ds(it * 2 + HEADS, 2), :] if f else zg[:]
                    nc.vector.tensor_tensor(dst, y, conv[:, 1 + f], ALU.mult).then_inc(ys["z"], 1)

                for j in range(12):
                    rest_unit(ve, un, j + AHEAD)
                    if j in (6, 11):
                        products(j // 11)
                    if j == 8:
                        gated(0)
                    if j % 4 == 3:
                        p = j // 4
                        ve.wait_ge(ys["cb"], it * 3 + (p + 1))
                        for b in range(2):
                            c0 = p * 8 + b * 4
                            o = conv[:, p, b, :].rearrange("p (r c) -> p r c", c=GRID_W)
                            u = bank[p][:, b * 256:(b + 1) * 256].rearrange("p (r c) -> p r c", c=GRID_W)
                            nc.vector.scalar_tensor_tensor(out=o[:, :, 1:], in0=u[:, :, :-1], scalar=y_cur[:, c0:c0 + 1],
                                                           in1=o[:, :, 1:], op0=ALU.mult, op1=ALU.add).then_inc(ys["conv"], 1)
                            ve.wait_ge(ys["conv"], it * 12 + (4 * p + 2 * b + 1))
                            nc.vector.scalar_tensor_tensor(out=o[:, :, :-1], in0=u[:, :, 1:], scalar=y_cur[:, c0 + 2:c0 + 3],
                                                           in1=o[:, :, :-1], op0=ALU.mult, op1=ALU.add).then_inc(ys["conv"], 1)
                ve.wait_ge(ys["prod"], it * 4 + 4)
                nc.vector.tensor_copy(spec_mark[:], ident[:, 0:1]).then_inc(ys["specfree"], 1)
                gated(1)

            for n in range(4):
                ve.wait_ge(ms["hi"], n + 1)
                nc.vector.tensor_tensor(m_lo[:, 4 * n:4 * n + 4, :], mix[:, 4 * n:4 * n + 4, :],
                                        m_hi[:, 4 * n:4 * n + 4, :].bitcast(F32), ALU.subtract).then_inc(ms["lo"], 1)
            nc.vector.memset(sq_sum[:], 0.0).then_inc(n2["sum"], 1)
            with ve.Fori(0, KB // 4) as it:
                un = Units(U_OUT, it, 8)

                def squares(b):
                    ve.wait_ge(n2["sq"], it * 2 + (b + 1))
                    ve.wait_ge(n2["sum"], it * 2 + (b + 1))
                    nc.vector.tensor_tensor(sq_sum[:], sq_sum[:], sq[b], ALU.add).then_inc(n2["sum"], 1)

                for j in range(8):
                    rest_unit(ve, un, j + AHEAD)
                    if j == 4:
                        squares(0)
                    if j % 4 == 3:
                        ve.wait_ge(w_used, used(un, j))
                        for b in range(2):
                            d = it * 4 + (j // 4 * 2 + b)
                            res = x_res[:, bass.ds(d, 1), :].rearrange("p a c -> p (a c)")
                            ins = nc.vector.scalar_tensor_tensor(
                                out=res, in0=bank[j // 4][:, b * 256:(b + 1) * 256],
                                scalar=gate_x[:, bass.ds(d, 1)], in1=res, op0=ALU.mult, op1=ALU.add)
                        ins.then_inc(ms["res"], 1)
                squares(1)

            rstd_dve(ve, n2, (0,))
            modulate_dve(ve, n2, 2, [x_res], lambda t, kb: h2_lo[:, kb, :], (0,))
            ffn_dve(ve, fb_, U_FFN2, s2, g2, g2_hi, g2_lo, 256, [x_res], 2, F2_LOOPS, nf)
            rstd_dve(ve, nf, (0,))
            ve.wait_ge(nf["rstd"], 1)
            for kb in range(KB):
                nc.vector.scalar_tensor_tensor(out=xo[:, kb, :], in0=x_res[:, kb, :], scalar=cols[1][:, 64 + kb:65 + kb],
                                               in1=rstd[:, 0:256], op0=ALU.mult, op1=ALU.mult).then_inc(fin["o"], 1)


_INS = ['x', 'c', 'ctx', 'c_ctx', 'ada_w', 'ada_b', 'norm_ffn1', 'ffn1_w1', 'ffn1_w3', 'ffn1_w2', 'norm_mix', 'w_in',
        'hg_lb_logits', 'hg_norm', 'hy_conv_w', 'hy_conv_b', 'filt_w1', 'filt_b1', 'filt_w2', 'filt_b2', 'filt_w3',
        'filt_b3', 'filt_freq', 'filt_w_out', 'hy_d', 'w_out', 'norm_ffn2', 'ffn2_w1', 'ffn2_w3', 'ffn2_w2',
        'final_norm']


def kernel(**inputs):
    import concourse.bacc as _bacc
    from concourse.bass_utils import run_bass_kernel_spmd as _run

    nc = _bacc.Bacc("TRN2", target_bir_lowering=False, num_devices=1)
    arrays, args = {}, {}
    for name, a in [(n, inputs[n]) for n in _INS] + list(shape_tables().items()):
        a = np.ascontiguousarray(a)
        arrays[f"in_{name}_dram"] = a
        args[name] = nc.dram_tensor(f"in_{name}_dram", a.shape, mybir.dt.from_np(a.dtype), kind="ExternalInput").ap()
    out = nc.dram_tensor("out_0_dram", (1, SEQ, D), F32, kind="ExternalOutput").ap()
    build(nc, args, out)
    r = _run(nc, [arrays], core_ids=[0])
    return r.results[0]["out_0_dram"]
```
